# Optimizing a Trainium2 kernel written in Bass

```python
import jax, jax.numpy as jnp
from jax import lax
import numpy as np

D_MODEL = 1024
BATCH = 1
SEQ = 1024
DEPTH = 1

N_HEADS_A = 16
N_KV_A = 2
HEAD_DIM_A = 64
GROUP_A = N_HEADS_A // N_KV_A
CMP_BLOCK = 32
CMP_STRIDE = 16
CMP_HIDDEN = 128
SEL_BLOCK = 64
SEL_TOPK = 16
WINDOW = 512
Q_BLOCK = 128
N_HEADS_R = 4
KEY_DIM_R = 128
VAL_DIM_R = 256
RET_CHUNK = 128
D_FF = ((8 * D_MODEL + 767) // 768) * 256
ROPE_THETA = 10000.0
EPS = 1e-6
NEG = -1e30
BIG = 1e9

W_Q_A = N_HEADS_A * HEAD_DIM_A
W_KV_A = 3 * 2 * N_KV_A * HEAD_DIM_A
W_G_A = 3 * N_HEADS_A
W_Q_R = N_HEADS_R * KEY_DIM_R
W_K_R = N_HEADS_R * KEY_DIM_R
W_V_R = N_HEADS_R * VAL_DIM_R
W_G_R = N_HEADS_R * VAL_DIM_R
W_MERGE = 2 * D_MODEL
IN_WIDTHS = (W_Q_A, W_KV_A, W_G_A, W_Q_R, W_K_R, W_V_R, W_G_R, W_MERGE)
IN_SPLITS = tuple(int(v) for v in np.cumsum(IN_WIDTHS)[:-1])
N_IN = sum(IN_WIDTHS)

kernel_name = "nsa_retention_gated_hybrid_block"

def _rmsnorm(x, g):
    xf = x.astype(jnp.float32)
    y = xf * lax.rsqrt(jnp.mean(xf * xf, axis=-1, keepdims=True) + EPS) * g.astype(jnp.float32)
    return y.astype(x.dtype)

def _rope(x, pos):
    d = x.shape[-1]
    half = d // 2
    inv = ROPE_THETA ** (-jnp.arange(half, dtype=jnp.float32) * 2.0 / d)
    ang = pos[:, None] * inv[None, :]
    cos = jnp.cos(ang)[None, :, None, :]
    sin = jnp.sin(ang)[None, :, None, :]
    xf = x.astype(jnp.float32)
    x1, x2 = xf[..., :half], xf[..., half:]
    return jnp.concatenate([x1 * cos - x2 * sin, x2 * cos + x1 * sin], axis=-1).astype(x.dtype)

def _masked_softmax(s, mask):
    s = jnp.where(mask, s, NEG)
    m = jnp.max(s, axis=-1, keepdims=True)
    p = jnp.exp(s - m) * mask
    return p / jnp.maximum(jnp.sum(p, axis=-1, keepdims=True), 1e-30)

def _compress(x, blk, pos_emb, w1, w2):
    B, _, hkv, _ = x.shape
    xb = x[:, blk] + pos_emb[None, None, :, None, :].astype(x.dtype)
    xb = xb.transpose(0, 1, 3, 2, 4).reshape(B, blk.shape[0], hkv, -1)
    return jax.nn.gelu(xb @ w1) @ w2

def _nsa(q, kc, vc, ks, vs, kw, vw, gates, cmp_pos_k, cmp_w1_k, cmp_w2_k, cmp_pos_v, cmp_w1_v, cmp_w2_v):
    B, S, H, Dh = q.shape
    n_cmp = (S - CMP_BLOCK) // CMP_STRIDE + 1
    n_sel = S // SEL_BLOCK
    n_top = min(SEL_TOPK, n_sel)
    scale = Dh ** -0.5
    blk = jnp.arange(n_cmp)[:, None] * CMP_STRIDE + jnp.arange(CMP_BLOCK)[None, :]
    k_cmp = _compress(kc, blk, cmp_pos_k, cmp_w1_k, cmp_w2_k)
    v_cmp = _compress(vc, blk, cmp_pos_v, cmp_w1_v, cmp_w2_v)
    cmp_end = jnp.arange(n_cmp) * CMP_STRIDE + CMP_BLOCK - 1
    cs = jnp.arange(n_cmp)[:, None] * CMP_STRIDE
    ss = jnp.arange(n_sel)[None, :] * SEL_BLOCK
    overlap = jnp.clip(jnp.minimum(cs + CMP_BLOCK, ss + SEL_BLOCK) - jnp.maximum(cs, ss), 0, None)
    cmp_to_sel = overlap.astype(jnp.float32) / CMP_BLOCK
    k_sel_blk = ks.reshape(B, n_sel, SEL_BLOCK, N_KV_A, Dh).transpose(0, 3, 1, 2, 4)
    v_sel_blk = vs.reshape(B, n_sel, SEL_BLOCK, N_KV_A, Dh).transpose(0, 3, 1, 2, 4)
    pad = ((0, 0), (WINDOW, 0), (0, 0), (0, 0))
    k_win = jnp.pad(kw, pad)
    v_win = jnp.pad(vw, pad)
    b_idx = jnp.arange(B)[:, None, None, None]
    h_idx = jnp.arange(N_KV_A)[None, None, :, None]
    sel_off = jnp.arange(SEL_BLOCK)
    win_off = jnp.arange(WINDOW + Q_BLOCK) - WINDOW
    jb = jnp.arange(n_sel)[None, :]

    def block(i):
        s0 = i * Q_BLOCK
        t = s0 + jnp.arange(Q_BLOCK)
        qb = lax.dynamic_slice_in_dim(q, s0, Q_BLOCK, axis=1).reshape(B, Q_BLOCK, N_KV_A, GROUP_A, Dh)
        gb = lax.dynamic_slice_in_dim(gates, s0, Q_BLOCK, axis=1).reshape(B, Q_BLOCK, N_KV_A, GROUP_A, 3)
        s = jnp.einsum('bqkgd,bnkd->bqkgn', qb, k_cmp).astype(jnp.float32) * scale
        cmask = (cmp_end[None, :] <= t[:, None])[None, :, None, None, :]
        p_cmp = _masked_softmax(s, cmask)
        o_cmp = jnp.einsum('bqkgn,bnkd->bqkgd', p_cmp.astype(v_cmp.dtype), v_cmp)
        imp = jnp.einsum('bqkgn,nj->bqkj', p_cmp, cmp_to_sel)
        cur = (t // SEL_BLOCK)[:, None]
        causal = (jb <= cur)[None, :, None, :]
        forced = ((jb == 0) | (jb == cur) | (jb == cur - 1))[None, :, None, :]
        score = jnp.where(forced, BIG, jnp.where(causal, imp, NEG))
        top_val, top_idx = lax.top_k(score, n_top)
        top_ok = top_val > 0.5 * NEG
        kg = k_sel_blk[b_idx, h_idx, top_idx].reshape(B, Q_BLOCK, N_KV_A, n_top * SEL_BLOCK, Dh)
        vg = v_sel_blk[b_idx, h_idx, top_idx].reshape(B, Q_BLOCK, N_KV_A, n_top * SEL_BLOCK, Dh)
        kpos = top_idx[..., None] * SEL_BLOCK + sel_off
        smask = (top_ok[..., None] & (kpos <= t[None, :, None, None, None]))
        smask = smask.reshape(B, Q_BLOCK, N_KV_A, 1, n_top * SEL_BLOCK)
        s = jnp.einsum('bqkgd,bqkmd->bqkgm', qb, kg).astype(jnp.float32) * scale
        p_sel = _masked_softmax(s, smask)
        o_sel = jnp.einsum('bqkgm,bqkmd->bqkgd', p_sel.astype(vg.dtype), vg)
        kwb = lax.dynamic_slice_in_dim(k_win, s0, WINDOW + Q_BLOCK, axis=1)
        vwb = lax.dynamic_slice_in_dim(v_win, s0, WINDOW + Q_BLOCK, axis=1)
        kp = (s0 + win_off)[None, :]
        wmask = (kp <= t[:, None]) & (kp > t[:, None] - WINDOW) & (kp >= 0)
        s = jnp.einsum('bqkgd,bmkd->bqkgm', qb, kwb).astype(jnp.float32) * scale
        p_win = _masked_softmax(s, wmask[None, :, None, None, :])
        o_win = jnp.einsum('bqkgm,bmkd->bqkgd', p_win.astype(vwb.dtype), vwb)
        o = gb[..., 0:1] * o_cmp + gb[..., 1:2] * o_sel + gb[..., 2:3] * o_win
        return o.reshape(B, Q_BLOCK, H * Dh)

    out = lax.map(block, jnp.arange(S // Q_BLOCK))
    return out.transpose(1, 0, 2, 3).reshape(B, S, H * Dh)

def _retention(q, k, v):
    B, S, Hr, Dk = q.shape
    Dv = v.shape[-1]
    C = RET_CHUNK
    nc = S // C
    log_g = jnp.log1p(-jnp.exp2(-5.0 - jnp.arange(Hr, dtype=jnp.float32)))
    i = jnp.arange(C, dtype=jnp.float32)
    diff = i[:, None] - i[None, :]
    decay_in = jnp.where(diff >= 0, jnp.exp(log_g[:, None, None] * jnp.maximum(diff, 0.0)), 0.0)
    decay_q = jnp.exp(log_g[:, None] * (i + 1.0))[..., None]
    decay_k = jnp.exp(log_g[:, None] * (C - 1.0 - i))[..., None]
    decay_c = jnp.exp(log_g * C)[:, None, None]

    def to_chunks(a):
        return a.reshape(B, nc, C, Hr, a.shape[-1]).transpose(1, 0, 3, 2, 4).astype(jnp.float32)

    def step(R, inp):
        qi, ki, vi = inp
        inner = jnp.einsum('bhid,bhjd->bhij', qi, ki) * decay_in
        o = jnp.einsum('bhij,bhje->bhie', inner, vi) + jnp.einsum('bhid,bhde->bhie', qi, R) * decay_q
        R = R * decay_c + jnp.einsum('bhjd,bhje->bhde', ki * decay_k, vi)
        return R, o

    R0 = jnp.zeros((B, Hr, Dk, Dv), jnp.float32)
    _, o = lax.scan(step, R0, (to_chunks(q), to_chunks(k), to_chunks(v)))
    return o.transpose(1, 0, 3, 2, 4).reshape(B, S, Hr, Dv)

def setup_inputs(seed: int = 0) -> dict:
    key = jax.random.key(seed)
    ks = jax.random.split(key, 20)
    f32 = jnp.float32
    L = DEPTH
    nrm = lambda k, shape, s: jax.random.normal(k, shape, f32) * s
    gain = lambda k: 1.0 + 0.1 * jax.random.normal(k, (L, D_MODEL), f32)
    cmp_in = CMP_BLOCK * HEAD_DIM_A
    return {
        "x": jax.random.normal(ks[0], (BATCH, SEQ, D_MODEL), f32),
        "g_pre_mix": gain(ks[1]),
        "w_in": nrm(ks[2], (L, D_MODEL, N_IN), D_MODEL ** -0.5),
        "cmp_pos_k": nrm(ks[3], (L, CMP_BLOCK, HEAD_DIM_A), 0.1),
        "cmp_w1_k": nrm(ks[4], (L, cmp_in, CMP_HIDDEN), cmp_in ** -0.5),
        "cmp_w2_k": nrm(ks[5], (L, CMP_HIDDEN, HEAD_DIM_A), CMP_HIDDEN ** -0.5),
        "cmp_pos_v": nrm(ks[6], (L, CMP_BLOCK, HEAD_DIM_A), 0.1),
        "cmp_w1_v": nrm(ks[7], (L, cmp_in, CMP_HIDDEN), cmp_in ** -0.5),
        "cmp_w2_v": nrm(ks[8], (L, CMP_HIDDEN, HEAD_DIM_A), CMP_HIDDEN ** -0.5),
        "w_branch_a": nrm(ks[9], (L, N_HEADS_A * HEAD_DIM_A, D_MODEL), (N_HEADS_A * HEAD_DIM_A) ** -0.5),
        "w_branch_b": nrm(ks[10], (L, N_HEADS_R * VAL_DIM_R, D_MODEL), (N_HEADS_R * VAL_DIM_R) ** -0.5),
        "w_out": nrm(ks[11], (L, D_MODEL, D_MODEL), D_MODEL ** -0.5),
        "g_post_mix": gain(ks[12]),
        "g_pre_ffn": gain(ks[13]),
        "w_ffn_gate": nrm(ks[14], (L, D_MODEL, D_FF), D_MODEL ** -0.5),
        "w_ffn_up": nrm(ks[15], (L, D_MODEL, D_FF), D_MODEL ** -0.5),
        "w_ffn_down": nrm(ks[16], (L, D_FF, D_MODEL), D_FF ** -0.5),
        "g_post_ffn": gain(ks[17]),
    }

def reference(x, g_pre_mix, w_in, cmp_pos_k, cmp_w1_k, cmp_w2_k, cmp_pos_v, cmp_w1_v, cmp_w2_v,
              w_branch_a, w_branch_b, w_out, g_post_mix, g_pre_ffn, w_ffn_gate, w_ffn_up,
              w_ffn_down, g_post_ffn):
    B, S, _ = x.shape
    pos = jnp.arange(S, dtype=jnp.float32)
    for l in range(DEPTH):
        h = _rmsnorm(x, g_pre_mix[l])
        z = h @ w_in[l]
        q_a, kv_a, ga_logit, q_r, k_r, v_r, g_r, m_logit = jnp.split(z, IN_SPLITS, axis=-1)
        q_a = _rope(q_a.reshape(B, S, N_HEADS_A, HEAD_DIM_A), pos)
        kv_a = kv_a.reshape(B, S, 6, N_KV_A, HEAD_DIM_A)
        kc = _rope(kv_a[:, :, 0], pos)
        vc = kv_a[:, :, 1]
        ksl = _rope(kv_a[:, :, 2], pos)
        vsl = kv_a[:, :, 3]
        kw = _rope(kv_a[:, :, 4], pos)
        vw = kv_a[:, :, 5]
        gates_a = jax.nn.sigmoid(ga_logit).reshape(B, S, N_HEADS_A, 3)
        y_a = _nsa(q_a, kc, vc, ksl, vsl, kw, vw, gates_a,
                   cmp_pos_k[l], cmp_w1_k[l], cmp_w2_k[l], cmp_pos_v[l], cmp_w1_v[l], cmp_w2_v[l])
        q_r = _rope(q_r.reshape(B, S, N_HEADS_R, KEY_DIM_R), pos) * (KEY_DIM_R ** -0.5)
        k_r = _rope(k_r.reshape(B, S, N_HEADS_R, KEY_DIM_R), pos)
        ret = _retention(q_r, k_r, v_r.reshape(B, S, N_HEADS_R, VAL_DIM_R))
        ret = (ret - jnp.mean(ret, -1, keepdims=True)) * lax.rsqrt(jnp.var(ret, -1, keepdims=True) + EPS)
        y_r = (jax.nn.silu(g_r.astype(jnp.float32)) * ret.reshape(B, S, -1)).astype(x.dtype)
        m_a, m_b = jnp.split(jax.nn.sigmoid(m_logit), 2, axis=-1)
        mix = (m_a * (y_a @ w_branch_a[l]) + m_b * (y_r @ w_branch_b[l])) @ w_out[l]
        x = x + _rmsnorm(mix, g_post_mix[l])
        h = _rmsnorm(x, g_pre_ffn[l])
        f = (jax.nn.silu(h @ w_ffn_gate[l]) * (h @ w_ffn_up[l])) @ w_ffn_down[l]
        x = x + _rmsnorm(f, g_post_ffn[l])
    return x


_drawn_inputs = setup_inputs


def setup_inputs(seed=0):
    import zlib

    import numpy as np

    out = dict(_drawn_inputs(seed))
    spreads = {}
    factors = {'cmp_pos_k': 8.0}
    for name, (base, spread) in spreads.items():
        noise = np.random.default_rng([zlib.crc32(name.encode()), seed]).standard_normal(out[name].shape)
        drawn = base * np.exp(spread * noise) if base else spread * noise
        out[name] = __import__('jax').numpy.asarray(drawn.astype(out[name].dtype))
    for name, factor in factors.items():
        out[name] = (out[name] * factor).astype(out[name].dtype)
    return out
```

```python
from contextlib import ExitStack

import concourse.bass as bass
from concourse import mybir

F32 = mybir.dt.float32
FR = mybir.dt.float32r
ALU = mybir.AluOpType
ACT = mybir.ActivationFunctionType
AX = mybir.AxisListType

P = 128
S = 1024
D = 1024
KC = D // P
SC = S // P
HALF = 512
DH = 64
KV = 2
NCMP = 64
RH = 4
DV = 256
FF = 2816 // P
EPS = 1e-6
ATT_SCALE = DH ** -0.5
RET_SCALE = 128 ** -0.5
PAIRS = 8

B_RET = 6
B_KV = RH * B_RET
B_Q0 = B_KV + 8
B_PAIR = B_Q0 + 1
B_WB = B_PAIR + 3 * PAIRS
B_WA = B_WB + KC
B_WO = B_WA + KC
B_FFN = B_WO + KC
N_BLOCKS = B_FFN + 3 * FF


def groups_of(qi):
    sel = [("sel", kb, kb * P) for kb in range(qi + 1)]
    lo = max(0, qi - 4)
    win = [("win", kb, (kb - lo) * P) for kb in range(lo, qi + 1)] + [("cmp", None, 5 * P)]
    return [sel[a:a + 4] for a in range(0, len(sel), 4)] + [win[a:a + 4] for a in range(0, len(win), 4)]


def layer(nc, x_d, wst_d, norm_d, rope_a_d, rope_r_d, ret_d, mask_d, w1_d, pos_d, w2k_d, w2v_d, out_d):
    yr_d = nc.dram_tensor("y_ret_T", (KC, P, S), F32).ap()
    ya_d = nc.dram_tensor("y_att_T", (KC, P, S), F32).ap()
    ml_d = nc.dram_tensor("merge_logits_T", (2 * KC, P, S), F32).ap()

    with ExitStack() as ctx:
        def sem(name):
            return ctx.enter_context(nc.semaphore(name))

        def tile(scope, name, shape, dt=F32):
            return scope.enter_context(nc.sbuf_tensor(name, [P, *shape], dt))

        XH = tile(ctx, "act_hi", [KC, S], FR)
        XL = tile(ctx, "act_lo", [KC, S], FR)
        wraw = tile(ctx, "w_raw", [2, 1024])
        wh = tile(ctx, "w_hi", [2, 1024], FR)
        wl = tile(ctx, "w_lo", [2, 1024], FR)
        ident = tile(ctx, "ident", [P])
        zero = tile(ctx, "zero", [1])
        ss = tile(ctx, "sum_sq", [SC])
        ms = tile(ctx, "mean_sq", [SC])
        rms = tile(ctx, "rms", [SC])
        rstd = tile(ctx, "rstd", [SC])
        ps = ctx.enter_context(nc.psum_tensor("ps", [P, 8, HALF], F32))

        sc0 = ExitStack()
        xs = tile(sc0, "x_rows", [SC, D])
        g0 = tile(sc0, "g_pre_mix", [D])
        xn = tile(sc0, "x_normed", [2, D])
        sc0.close()
        scr = ExitStack()
        rcos = tile(scr, "ret_cos", [S])
        rsin = tile(scr, "ret_sin", [S])
        rraw = tile(scr, "ret_raw", [2, S])
        rswp = tile(scr, "ret_swapped", [S])
        rqh = tile(scr, "ret_q_hi", [S], FR)
        rql = tile(scr, "ret_q_lo", [S], FR)
        rkh = tile(scr, "ret_k_hi", [S], FR)
        rkl = tile(scr, "ret_k_lo", [S], FR)
        vh = tile(scr, "ret_v_hi", [SC, DV], FR)
        vl = tile(scr, "ret_v_lo", [SC, DV], FR)
        knh = tile(scr, "ret_kdec_hi", [SC, P], FR)
        knl = tile(scr, "ret_kdec_lo", [SC, P], FR)
        silu_g = tile(scr, "ret_silu_g", [2, S])
        ro = tile(scr, "ret_out", [SC, DV])
        ry = tile(scr, "ret_y_T", [2, S])
        hc = tile(scr, "ret_decays", [P + 4])
        im = tile(scr, "ret_inner", [2, P])
        imh = tile(scr, "ret_inner_hi", [2, P], FR)
        iml = tile(scr, "ret_inner_lo", [2, P], FR)
        R = tile(scr, "ret_state", [DV])
        Rh = tile(scr, "ret_state_hi", [2, DV], FR)
        Rl = tile(scr, "ret_state_lo", [2, DV], FR)
        t2 = tile(scr, "ret_cross", [2, DV])
        bst = tile(scr, "ret_bn", [SC, 6])
        mv = tile(scr, "ret_mean_var", [SC, 2])
        ve = tile(scr, "ret_var_eps", [SC])
        rsd = tile(scr, "ret_std", [SC])
        rrs = tile(scr, "ret_rstd", [SC])
        scr.close()
        sca = ExitStack()
        acos = tile(sca, "att_cos", [S])
        asin = tile(sca, "att_sin", [S])
        kk = tile(sca, "keys_hi_twice", [2, KV, S], FR)
        kl = tile(sca, "keys_lo", [2, KV, S], FR)
        Vh = tile(sca, "values_hi", [SC, 2 * KV * DH], FR)
        Vl = tile(sca, "values_lo", [SC, 2 * KV * DH], FR)
        kch = tile(sca, "cmp_keys_hi", [KV, NCMP], FR)
        kcl = tile(sca, "cmp_keys_lo", [KV, NCMP], FR)
        vch = tile(sca, "cmp_values_hi", [KV, DH], FR)
        vcl = tile(sca, "cmp_values_lo", [KV, DH], FR)
        gates = tile(sca, "gates", [SC, 48])
        qhi = tile(sca, "q_hi", [S], FR)
        qlo = tile(sca, "q_lo", [S], FR)
        maskr = tile(sca, "masks_r", [2 * P + SC * NCMP], FR)
        identr = tile(sca, "ident_r", [P], FR)
        scf = ExitStack()
        maskf = tile(scf, "masks_f32", [2 * P + SC * NCMP + 1])
        fraw = tile(scf, "kv_raw", [2, S])
        fswp = tile(scf, "kv_swapped", [S])
        kcs = tile(scf, "cmp_in_k", [KV, S + 16])
        vcs = tile(scf, "cmp_in_v", [KV, S + 16])
        w1 = tile(scf, "cmp_w1", [2, 16, P])
        w2k = tile(scf, "cmp_w2_k_twice", [P])
        w2v = tile(scf, "cmp_w2_v", [DH])
        pos = tile(scf, "cmp_pos", [2, 16])
        hb = tile(scf, "cmp_bias", [2])
        hid = fswp[:, 0:2 * P].rearrange("p (t n) -> p t n", t=2)
        scf.close()
        raw = tile(sca, "q_raw", [S])
        swp = tile(sca, "q_swapped", [S])
        qst = tile(sca, "q_hi_over_lo", [2, S], FR)
        Ps = tile(sca, "probs_sel", [2, S])
        Pw = tile(sca, "probs_win_cmp", [2, 6 * P])
        PTh = tile(sca, "probs_T_hi", [2, HALF], FR)
        PTl = tile(sca, "probs_T_lo", [2, HALF], FR)
        fm = tile(sca, "merge_half", [HALF])
        yT = tile(sca, "att_y_T", [S])
        yn = tile(sca, "att_y", [2, P])
        og = tile(sca, "att_gated", [3, 2, DH])
        mx = tile(sca, "row_max", [2, 3])
        nm = tile(sca, "neg_max", [2, 3])
        ls = tile(sca, "row_sum", [2, 3, 2])
        lm = tile(sca, "row_sum_held", [6])
        li = tile(sca, "row_sum_inv", [6])
        rg = tile(sca, "row_weight", [6])
        sca.close()
        scm = ExitStack()
        x2 = tile(scm, "x_mid", [SC, D])
        ring2 = tile(scm, "loaded_rows", [2, S])
        mt = tile(scm, "merge_gate", [2, S])
        scm1 = ExitStack()
        YH = tile(scm1, "mix_hi", [KC, S], FR)
        YL = tile(scm1, "mix_lo", [KC, S], FR)
        tmp = tile(scm1, "branch_gated", [S])
        scm1.close()
        xn2 = tile(scm, "x_mid_normed", [2, D])
        sg = tile(scm, "silu_gate", [S])
        ff = tile(scm, "ffn_hidden", [S])
        FH = tile(scm, "ffn_hidden_hi", [2, S], FR)
        FL = tile(scm, "ffn_hidden_lo", [2, S], FR)
        acc = tile(scm, "ffn_out", [SC, D])
        gc = tile(scm, "g_post_ffn", [D])
        scm.close()

        x_loaded = [sem(f"x_loaded{i}") for i in range(SC)]
        consts_loaded = sem("consts_loaded")
        ret_consts_loaded = sem("ret_consts_loaded")
        att_consts_loaded = sem("att_consts_loaded")
        block_loaded = [sem("block_loaded0"), sem("block_loaded1")]
        block_hi = sem("block_hi")
        block_split = sem("block_split")
        blocks_multiplied = sem("blocks_multiplied")
        zero_set = sem("zero_set")
        act_passed = sem("act_passed")
        dve_passed = sem("dve_passed")

        block = ctx.enter_context(nc.Block())

        def matmul3(out, wh_, wl_, xh_, xl_, first, last):
            nc.tensor.matmul(out, wh_, xh_, start=first, stop=False)
            nc.tensor.matmul(out, wh_, xl_, start=False, stop=False)
            return nc.tensor.matmul(out, wl_, xh_, start=False, stop=last)

        def t_job(pe, slot, n, xh, xl, bank, k_ready=None):
            pe.wait_ge(block_split, n)
            for k in range(KC):
                if k_ready is not None:
                    pe.wait_ge(k_ready, k + 1)
                w_h, w_l = wh[:, slot, k * P:(k + 1) * P], wl[:, slot, k * P:(k + 1) * P]
                for w, x in ((w_h, xh), (w_h, xl), (w_l, xh)):
                    for half in range(2):
                        mm = nc.tensor.matmul(ps[:, bank + half, :], w, x[:, k, half * HALF:(half + 1) * HALF],
                                              start=(k == 0 and w is w_h and x is xh),
                                              stop=(k == KC - 1 and w is w_l))
            mm.then_inc(blocks_multiplied, 1)

        s1_sq, s1_ms, s1_rms, s1_rstd = sem("s1_sq"), sem("s1_ms"), sem("s1_rms"), sem("s1_rstd")
        s1_xn, s1_tr, s1_hi, s1_lo = sem("s1_xn"), sem("s1_tr"), sem("s1_hi"), sem("s1_lo")

        def norm_T_act(act, hi, tr, hi_sem):
            for t in range(2 * SC):
                s, g = divmod(t, 2)
                act.wait_ge(tr, t + 1)
                nc.scalar.activation(hi[:, 4 * g:4 * g + 4, s * P:(s + 1) * P],
                                     ps[:, t % 4, :].rearrange("p (k n) -> p k n", k=4), ACT.Copy).then_inc(hi_sem, 1)

        def norm_T_dve(dve, rows, gain, out, r_sem, xn_sem, tr, hi, lo, hi_sem, lo_sem):
            for s in range(SC):
                dve.wait_ge(r_sem, 1)
                if s >= 2:
                    dve.wait_ge(tr, 2 * (s - 1))
                nc.vector.scalar_tensor_tensor(out=out[:, s % 2, :], in0=rows[:, s, :], scalar=rstd[:, s:s + 1],
                                               in1=gain[:], op0=ALU.mult, op1=ALU.mult).then_inc(xn_sem, 1)
                if s >= 1:
                    norm_lo(dve, s - 1, hi, lo, hi_sem, lo_sem)
            norm_lo(dve, SC - 1, hi, lo, hi_sem, lo_sem)

        def norm_lo(dve, s, hi, lo, hi_sem, lo_sem):
            for g in range(2):
                t = 2 * s + g
                dve.wait_ge(hi_sem, t + 1)
                at = (slice(None), slice(4 * g, 4 * g + 4), slice(s * P, (s + 1) * P))
                nc.vector.tensor_tensor(lo[at], ps[:, t % 4, :].rearrange("p (k n) -> p k n", k=4),
                                        hi[at].bitcast(F32), ALU.subtract).then_inc(lo_sem, 1)

        def norm_T_pe(pe, rows, xn_sem, tr, lo_sem):
            for t in range(2 * SC):
                s, g = divmod(t, 2)
                pe.wait_ge(xn_sem, s + 1)
                if t >= 4:
                    pe.wait_ge(lo_sem, t - 3)
                for k in range(4):
                    mm = nc.tensor.transpose(ps[:, t % 4, k * P:(k + 1) * P],
                                             rows[:, s % 2, (4 * g + k) * P:(4 * g + k + 1) * P], ident[:])
                mm.then_inc(tr, 1)

        def mean_sq_dve(dve, sq_sem, ms_sem, rms_sem, rstd_sem):
            dve.wait_ge(sq_sem, SC)
            nc.vector.tensor_scalar(ms[:], ss[:], 1.0 / D, EPS, ALU.mult, ALU.add).then_inc(ms_sem, 1)
            dve.wait_ge(rms_sem, 1)
            nc.vector.reciprocal(rstd[:], rms[:]).then_inc(rstd_sem, 1)

        def squares_act(act, rows, junk, sq_sem, ready, junk_free=None):
            for s in range(SC):
                ready(s)
                if s >= 1:
                    act.wait_ge(sq_sem, s)
                nc.scalar.activation(junk, rows[:, s, :], ACT.Square, accum_out=ss[:, s:s + 1]).then_inc(sq_sem, 1)

        def s1_act(act):
            squares_act(act, xs, xn[:, 0, :], s1_sq, lambda s: act.wait_ge(x_loaded[s], 16))
            act.wait_ge(s1_ms, 1)
            nc.scalar.activation(rms[:], ms[:], ACT.Sqrt).then_inc(s1_rms, 1)
            norm_T_act(act, XH, s1_tr, s1_hi)

        def s1_dve(dve):
            mean_sq_dve(dve, s1_sq, s1_ms, s1_rms, s1_rstd)
            dve.wait_ge(consts_loaded, 32)
            norm_T_dve(dve, xs, g0, xn, s1_rstd, s1_xn, s1_tr, XH, XL, s1_hi, s1_lo)

        def s1_pe(pe):
            pe.wait_ge(consts_loaded, 32)
            norm_T_pe(pe, xn, s1_xn, s1_tr, s1_lo)

        r_v_acc, r_v_hi, r_v_lo = sem("r_v_acc"), sem("r_v_hi"), sem("r_v_lo")
        r_raw, r_swp, r_rope = sem("r_raw"), sem("r_swp"), sem("r_rope")
        r_rh, r_rl, r_silu = sem("r_rope_hi"), sem("r_rope_lo"), sem("r_silu")
        r_hc = sem("r_decays_loaded")
        r_kt, r_kn_hi, r_kn_lo = sem("r_kt"), sem("r_kn_hi"), sem("r_kn_lo")
        r_inner, r_u, r_o = sem("r_inner"), sem("r_u"), sem("r_o")
        r_im, r_im_hi, r_im_lo = sem("r_im"), sem("r_im_hi"), sem("r_im_lo")
        r_R, r_R_hi, r_R_lo = sem("r_R"), sem("r_R_hi"), sem("r_R_lo")
        r_t2, r_oacc = sem("r_t2"), sem("r_oacc")
        r_bn, r_mv, r_ve, r_std, r_rs = sem("r_bn"), sem("r_mv"), sem("r_ve"), sem("r_std"), sem("r_rs")
        r_xn, r_yt, r_y, r_y_stored = sem("r_xn"), sem("r_yt"), sem("r_y"), sem("r_y_stored")
        decT, dk, dq, dc = hc[:, 0:P], hc[:, P:P + 1], hc[:, P + 1:P + 2], hc[:, P + 2:P + 3]

        def ret_pe(pe):
            pe.wait_ge(s1_lo, 2 * SC)
            with pe.Fori(0, RH) as h:
                pe.wait_ge(r_y, h * 4 + 4)
                for j in range(2):
                    pe.wait_ge(block_split, h * B_RET + (j + 1))
                    for k4 in range(4):
                        k = 4 * j + k4
                        for s in range(SC):
                            xh_, xl_ = XH[:, k, s * P:(s + 1) * P], XL[:, k, s * P:(s + 1) * P]
                            mm = matmul3(ps[:, s, 0:DV], xh_, xl_, wh[:, j, k4 * DV:(k4 + 1) * DV],
                                         wl[:, j, k4 * DV:(k4 + 1) * DV], k == 0, k == KC - 1)
                            if k == KC - 1 and s < SC - 1:
                                mm.then_inc(r_v_acc, 1)
                    mm.then_inc(blocks_multiplied, 1)
                for j in range(4):
                    pe.wait_ge(r_v_lo, h * 8 + 2 * (j + 1))
                    t_job(pe, j % 2, h * B_RET + (3 + j), XH, XL, 2 * j)
                pe.wait_ge(r_rope, h * 6 + 6)
                pe.wait_ge(r_raw, h * 2 + 1)
                for g in range(2):
                    for c in range(4):
                        mm = nc.tensor.transpose(ps[:, g, c * P:(c + 1) * P],
                                                 rraw[:, 1, (4 * g + c) * P:(4 * g + c + 1) * P], ident[:])
                    mm.then_inc(r_kt, 1)

                def inner_and_update(c):
                    at = slice(c * P, (c + 1) * P)
                    if c >= 2:
                        pe.wait_ge(r_im, h * 8 + (c - 1))
                    matmul3(ps[:, 2 + c % 2, 0:P], rkh[:, at], rkl[:, at], rqh[:, at], rql[:, at],
                            True, True).then_inc(r_inner, 1)
                    if c < SC - 1:
                        pe.wait_ge(r_kn_lo, h * 2 + (c // 4 + 1))
                        if c >= 2:
                            pe.wait_ge(r_R, h * 7 + (c - 1))
                        matmul3(ps[:, 4 + c % 2, 0:DV], knh[:, c, :], knl[:, c, :], vh[:, c, :], vl[:, c, :],
                                True, True).then_inc(r_u, 1)

                pe.wait_ge(r_rl, h * 2 + 2)
                pe.wait_ge(r_silu, h * 2 + 2)
                inner_and_update(0)
                for c in range(SC):
                    if c + 1 < SC:
                        inner_and_update(c + 1)
                    at = slice(c * P, (c + 1) * P)
                    if c >= 2:
                        pe.wait_ge(r_oacc, h * 8 + (c - 1))
                    if c >= 1:
                        pe.wait_ge(r_R_lo, h * 7 + c)
                        matmul3(ps[:, 6 + c % 2, DV:2 * DV], rqh[:, at], rql[:, at], Rh[:, (c - 1) % 2, :],
                                Rl[:, (c - 1) % 2, :], True, True)
                    pe.wait_ge(r_im_lo, h * 8 + (c + 1))
                    matmul3(ps[:, 6 + c % 2, 0:DV], imh[:, c % 2, :], iml[:, c % 2, :], vh[:, c, :], vl[:, c, :],
                            True, True).then_inc(r_o, 1)
                pe.wait_ge(r_im, h * 8 + 8)
                for e in range(2):
                    for q in range(2):
                        pe.wait_ge(r_xn, h * 8 + 4 * (q + 1))
                        for c in range(4):
                            mm = nc.tensor.transpose(ps[:, 2 * e + q, c * P:(c + 1) * P],
                                                     ro[:, 4 * q + c, e * P:(e + 1) * P], ident[:])
                        mm.then_inc(r_yt, 1)

        def ret_act(act):
            act.wait_ge(s1_lo, 2 * SC)
            act.dma_start(rcos[:], rope_r_d[0]).then_inc(ret_consts_loaded, 16)
            act.dma_start(rsin[:], rope_r_d[1]).then_inc(ret_consts_loaded, 16)
            with act.Fori(0, RH) as h:
                act.dma_start(hc[:], ret_d[bass.ds(h, 1)].rearrange("a p n -> p (a n)")).then_inc(r_hc, 16)
                for s in range(SC):
                    if s < SC - 1:
                        act.wait_ge(r_v_acc, h * 7 + (s + 1))
                    else:
                        act.wait_ge(blocks_multiplied, h * B_RET + 2)
                    nc.scalar.activation(vh[:, s, :], ps[:, s, 0:DV], ACT.Copy).then_inc(r_v_hi, 1)
                for j in range(2):
                    act.wait_ge(blocks_multiplied, h * B_RET + (3 + j))
                    nc.scalar.activation(rraw[:, j, :], ps[:, 2 * j:2 * j + 2, :].rearrange("p a n -> p (a n)"),
                                         ACT.Copy, scale=RET_SCALE if j == 0 else 1.0).then_inc(r_raw, 1)
                    act.wait_ge(r_raw, h * 2 + (j + 1))
                    if j == 1:
                        act.wait_ge(r_rope, h * 6 + 3)
                    for a in range(2):
                        act.dma_start(rswp[64 * a:64 * a + 64, :], rraw[64 - 64 * a:128 - 64 * a, j, :])\
                            .then_inc(r_swp, 16)
                    if j == 1:
                        nc.scalar.activation(rqh[:], rraw[:, 0, :], ACT.Copy).then_inc(r_rh, 1)
                for j in range(2):
                    act.wait_ge(blocks_multiplied, h * B_RET + (5 + j))
                    nc.scalar.activation(silu_g[:, j, :], ps[:, 4 + 2 * j:6 + 2 * j, :].rearrange("p a n -> p (a n)"),
                                         ACT.Silu).then_inc(r_silu, 1)
                    if j == 0:
                        act.wait_ge(r_rope, h * 6 + 6)
                        nc.scalar.activation(rkh[:], rraw[:, 1, :], ACT.Copy).then_inc(r_rh, 1)
                act.wait_ge(r_hc, h * 16 + 16)
                for g in range(2):
                    act.wait_ge(r_kt, h * 2 + (g + 1))
                    nc.scalar.activation(knh[:, 4 * g:4 * g + 4, :], ps[:, g, :].rearrange("p (c n) -> p c n", c=4),
                                         ACT.Copy, scale=dk).then_inc(r_kn_hi, 1)
                for c in range(SC):
                    act.wait_ge(r_im, h * 8 + (c + 1))
                    if c >= 2:
                        act.wait_ge(r_o, h * 8 + (c - 1))
                    nc.scalar.activation(imh[:, c % 2, :], im[:, c % 2, :], ACT.Copy).then_inc(r_im_hi, 1)
                    if c < SC - 1:
                        act.wait_ge(r_R, h * 7 + (c + 1))
                        if c >= 2:
                            act.wait_ge(r_o, h * 8 + c)
                        nc.scalar.activation(Rh[:, c % 2, :], R[:], ACT.Copy).then_inc(r_R_hi, 1)
                    if c >= 1:
                        act.wait_ge(r_o, h * 8 + (c + 1))
                        if c >= 3:
                            act.wait_ge(r_oacc, h * 8 + (c - 1))
                        nc.scalar.activation(t2[:, c % 2, :], ps[:, 6 + c % 2, DV:2 * DV], ACT.Copy, scale=dq)\
                            .then_inc(r_t2, 1)
                act.wait_ge(r_ve, h + 1)
                nc.scalar.activation(rsd[:], ve[:], ACT.Sqrt).then_inc(r_std, 1)
                act.wait_ge(r_y, h * 4 + 8)
                act.dma_start(yr_d[bass.ds(h * 2, 2)].rearrange("a p n -> p a n"), ry[:]).then_inc(r_y_stored, 16)

        def ret_dve(dve):
            nc.vector.sem_inc(r_y, 4)
            nc.vector.sem_inc(r_y_stored, 16)
            dve.wait_ge(ret_consts_loaded, 32)
            with dve.Fori(0, RH) as h:
                for s in range(SC):
                    dve.wait_ge(r_v_hi, h * 8 + (s + 1))
                    nc.vector.tensor_tensor(vl[:, s, :], ps[:, s, 0:DV], vh[:, s, :].bitcast(F32), ALU.subtract)\
                        .then_inc(r_v_lo, 1)
                for j in range(2):
                    dve.wait_ge(r_swp, h * 64 + 32 * (j + 1))
                    nc.vector.tensor_tensor(rraw[:, j, :], rraw[:, j, :], rcos[:], ALU.mult).then_inc(r_rope, 1)
                    nc.vector.tensor_tensor(rswp[:], rswp[:], rsin[:], ALU.mult).then_inc(r_rope, 1)
                    dve.wait_ge(r_rope, h * 6 + (3 * j + 2))
                    nc.vector.tensor_tensor(rraw[:, j, :], rraw[:, j, :], rswp[:], ALU.add).then_inc(r_rope, 1)
                for j, (hi, lo) in enumerate(((rqh, rql), (rkh, rkl))):
                    dve.wait_ge(r_rh, h * 2 + (j + 1))
                    nc.vector.tensor_tensor(lo[:], rraw[:, j, :], hi[:].bitcast(F32), ALU.subtract).then_inc(r_rl, 1)
                dve.wait_ge(r_hc, h * 16 + 16)
                for g in range(2):
                    dve.wait_ge(r_kn_hi, h * 2 + (g + 1))
                    nc.vector.scalar_tensor_tensor(
                        out=knl[:, 4 * g:4 * g + 4, :].rearrange("p c n -> p (c n)"), in0=ps[:, g, :], scalar=dk,
                        in1=knh[:, 4 * g:4 * g + 4, :].rearrange("p c n -> p (c n)").bitcast(F32),
                        op0=ALU.mult, op1=ALU.subtract).then_inc(r_kn_lo, 1)
                for c in range(SC):
                    dve.wait_ge(r_inner, h * 8 + (c + 1))
                    nc.vector.tensor_tensor(im[:, c % 2, :], ps[:, 2 + c % 2, 0:P], decT, ALU.mult).then_inc(r_im, 1)
                    if c < SC - 1:
                        dve.wait_ge(r_u, h * 7 + (c + 1))
                        if c == 0:
                            nc.vector.tensor_copy(R[:], ps[:, 4, 0:DV]).then_inc(r_R, 1)
                        else:
                            nc.vector.scalar_tensor_tensor(out=R[:], in0=R[:], scalar=dc, in1=ps[:, 4 + c % 2, 0:DV],
                                                           op0=ALU.mult, op1=ALU.add).then_inc(r_R, 1)
                    dve.wait_ge(r_im_hi, h * 8 + (c + 1))
                    nc.vector.tensor_tensor(iml[:, c % 2, :], im[:, c % 2, :], imh[:, c % 2, :].bitcast(F32),
                                            ALU.subtract).then_inc(r_im_lo, 1)
                    if c < SC - 1:
                        dve.wait_ge(r_R_hi, h * 7 + (c + 1))
                        nc.vector.tensor_tensor(Rl[:, c % 2, :], R[:], Rh[:, c % 2, :].bitcast(F32),
                                                ALU.subtract).then_inc(r_R_lo, 1)
                    if c == 0:
                        dve.wait_ge(r_o, h * 8 + 1)
                        nc.vector.tensor_copy(ro[:, 0, :], ps[:, 6, 0:DV]).then_inc(r_oacc, 1)
                    else:
                        dve.wait_ge(r_t2, h * 7 + c)
                        nc.vector.tensor_tensor(ro[:, c, :], ps[:, 6 + c % 2, 0:DV], t2[:, c % 2, :], ALU.add)\
                            .then_inc(r_oacc, 1)
                    if c >= 1:
                        dve.wait_ge(r_oacc, h * 8 + c)
                        nc.vector.bn_stats(bst[:, c - 1, :], ro[:, c - 1, :]).then_inc(r_bn, 1)
                dve.wait_ge(r_oacc, h * 8 + 8)
                nc.vector.bn_stats(bst[:, 7, :], ro[:, 7, :]).then_inc(r_bn, 1)
                dve.wait_ge(r_bn, h * 8 + 8)
                nc.vector.sem_inc(dve_passed, 1)
                for c in range(SC):
                    nc.vector.bn_aggr(mv[:, c, :], bst[:, c, :]).then_inc(r_mv, 1)
                dve.wait_ge(r_mv, h * 8 + 8)
                nc.vector.tensor_scalar(ve[:], mv[:, :, 1], EPS, None, ALU.add).then_inc(r_ve, 1)
                dve.wait_ge(r_std, h + 1)
                nc.vector.reciprocal(rrs[:], rsd[:]).then_inc(r_rs, 1)
                dve.wait_ge(r_rs, h + 1)
                for c in range(SC):
                    nc.vector.tensor_scalar(ro[:, c, :], ro[:, c, :], mv[:, c, 0:1], rrs[:, c:c + 1],
                                            ALU.subtract, ALU.mult).then_inc(r_xn, 1)
                dve.wait_ge(r_y_stored, h * 16 + 16)
                for e in range(2):
                    for q in range(2):
                        dve.wait_ge(r_yt, h * 4 + (2 * e + q + 1))
                        at = slice(q * HALF, (q + 1) * HALF)
                        nc.vector.tensor_tensor(ry[:, e, at], ps[:, 2 * e + q, :], silu_g[:, e, at], ALU.mult)\
                            .then_inc(r_y, 1)

        a_raw, a_swp, a_rope = sem("a_raw"), sem("a_swapped"), sem("a_rope")
        a_vcs, a_kcs, a_kk = sem("a_cmp_v_in"), sem("a_cmp_k_in"), sem("a_keys_placed")
        a_pad, a_mask = sem("a_pad"), sem("a_mask")
        a_hi, a_lo, a_vh, a_vl = sem("a_key_hi"), sem("a_key_lo"), sem("a_value_hi"), sem("a_value_lo")
        a_gate, a_gv = sem("a_gate"), sem("a_gate_valid")
        a_mlp, a_hb, a_hid = sem("a_mlp"), sem("a_mlp_bias"), sem("a_hidden")
        a_cmp, a_chi, a_clo = sem("a_cmp"), sem("a_cmp_hi"), sem("a_cmp_lo")
        CMPM = 2 * P
        VALID = CMPM + SC * NCMP

        def bank_of(s):
            return (s + 4) % 8

        def fixed_pe(pe):
            t_job(pe, 0, B_KV + 1, XH, XL, 4)
            t_job(pe, 1, B_KV + 2, XH, XL, 6)
            pe.wait_ge(r_y, 4 * RH + 4)
            t_job(pe, 0, B_KV + 3, XH, XL, 0)
            t_job(pe, 1, B_KV + 4, XH, XL, 2)
            for j in range(4):
                pe.wait_ge(block_split, B_KV + 5 + j)
                for k2 in range(2):
                    k = 2 * j + k2
                    for s in range(SC):
                        if k == 0 and s % 2 == 0:
                            pe.wait_ge(a_raw, s // 2 + 1)
                        at = slice(k2 * HALF, k2 * HALF + 304)
                        mm = matmul3(ps[:, bank_of(s), 0:304], XH[:, k, s * P:(s + 1) * P], XL[:, k, s * P:(s + 1) * P],
                                     wh[:, j % 2, at], wl[:, j % 2, at], k == 0, k == KC - 1)
                mm.then_inc(blocks_multiplied, 1)
            pe.wait_ge(att_consts_loaded, 7 * 16)
            pe.wait_ge(a_pad, 6)
            pe.wait_ge(a_vl, 1)
            pe.wait_ge(a_gate, 1)
            for t, (src, ready) in enumerate(((kcs, a_kcs), (vcs, a_vcs))):
                pe.wait_ge(ready, 64)
                for jj in range(16):
                    mm = nc.tensor.matmul(ps[:, 4 + t, 0:P].rearrange("p (v n) -> p v n", v=KV), w1[:, t, jj, :],
                                          src[:, :, 2 * jj:2 * jj + 16 * (NCMP - 1) + 1:16],
                                          start=(jj == 0), stop=(jj == 15))
                mm.then_inc(a_mlp, 1)
                for jj in range(16):
                    mm = nc.tensor.matmul(ps[:, 6, t:t + 1], w1[:, t, jj, :], pos[:, t, jj:jj + 1],
                                          start=(jj == 0), stop=(jj == 15))
                mm.then_inc(a_mlp, 1)
            pe.wait_ge(a_hid, 1)
            nc.tensor.matmul(ps[:, 7, 0:P], w2k[:], hid[:, 0, :], start=True, stop=True).then_inc(a_cmp, 1)
            pe.wait_ge(a_hid, 2)
            pe.wait_ge(a_vl, 2)
            pe.wait_ge(a_gate, 2)
            for v in range(KV):
                mm = nc.tensor.matmul(ps[0:NCMP, 0, v * DH:(v + 1) * DH], hid[:, 1, v * NCMP:(v + 1) * NCMP], w2v[:],
                                      start=True, stop=True)
            mm.then_inc(a_cmp, 1)

        def swap32(act, dst, src, done):
            for a in range(4):
                b = a ^ 1
                act.dma_start(dst[32 * a:32 * a + 32], src[32 * b:32 * b + 32]).then_inc(done, 16)

        def place_cmp(act, dst, src, done):
            for v in range(KV):
                act.dma_start(dst[0:64, v, 0:S], src[64 * v:64 * v + 64, :]).then_inc(done, 16)
                act.dma_start(dst[64:128, v, 0:S - 1], src[64 * v:64 * v + 64, 1:S]).then_inc(done, 16)

        def place_keys(act, br):
            for v in range(KV):
                for a in range(2):
                    act.dma_start(kk[64 * a:64 * a + 64, br, v, :].bitcast(F32), qhi[64 * v:64 * v + 64, :].bitcast(F32)).then_inc(a_kk, 16)
                act.dma_start(kl[0:64, br, v, :].bitcast(F32), qlo[64 * v:64 * v + 64, :].bitcast(F32)).then_inc(a_kk, 16)

        def two_banks(b):
            return ps[:, b:b + 2, :].rearrange("p a n -> p (a n)")

        def fixed_act(act):
            act.wait_ge(r_y_stored, 16 * (RH + 1))
            for dst, src in ((acos[:], rope_a_d[0]), (asin[:], rope_a_d[1]), (maskf[:], mask_d),
                             (w1[:], w1_d), (pos[:], pos_d), (w2k[:], w2k_d), (w2v[:], w2v_d)):
                act.dma_start(dst, src).then_inc(att_consts_loaded, 16)
            act.wait_ge(blocks_multiplied, B_KV + 1)
            nc.scalar.activation(fraw[:, 0, :], two_banks(4), ACT.Copy).then_inc(a_raw, 1)
            act.wait_ge(a_raw, 1)
            swap32(act, fswp, fraw[:, 0, :], a_swp)
            act.wait_ge(blocks_multiplied, B_KV + 2)
            nc.scalar.activation(fraw[:, 1, :], two_banks(6), ACT.Copy).then_inc(a_raw, 1)
            act.wait_ge(a_raw, 2)
            place_cmp(act, vcs, fraw[:, 1, :], a_vcs)
            act.wait_ge(a_rope, 3)
            place_cmp(act, kcs, fraw[:, 0, :], a_kcs)
            act.wait_ge(blocks_multiplied, B_KV + 3)
            act.wait_ge(a_kcs, 64)
            nc.scalar.activation(fraw[:, 0, :], two_banks(0), ACT.Copy).then_inc(a_raw, 1)
            act.wait_ge(a_raw, 3)
            swap32(act, fswp, fraw[:, 0, :], a_swp)
            act.wait_ge(blocks_multiplied, B_KV + 4)
            act.wait_ge(a_vcs, 64)
            nc.scalar.activation(fraw[:, 1, :], two_banks(2), ACT.Copy).then_inc(a_raw, 1)
            act.wait_ge(a_rope, 6)
            nc.scalar.activation(qhi[:], fraw[:, 0, :], ACT.Copy).then_inc(a_hi, 1)
            act.wait_ge(a_raw, 4)
            swap32(act, fswp, fraw[:, 1, :], a_swp)
            act.wait_ge(a_hi, 1)
            act.wait_ge(a_lo, 1)
            place_keys(act, 0)
            act.wait_ge(a_rope, 9)
            act.wait_ge(a_kk, 96)
            nc.scalar.activation(qhi[:], fraw[:, 1, :], ACT.Copy).then_inc(a_hi, 1)
            act.wait_ge(a_hi, 2)
            act.wait_ge(a_lo, 2)
            place_keys(act, 1)
            act.wait_ge(blocks_multiplied, B_KV + 8)
            for g, b in ((0, 4), (1, 0)):
                nc.scalar.activation(Vh[:, 4 * g:4 * g + 4, :], ps[:, b:b + 4, 0:256], ACT.Copy).then_inc(a_vh, 1)
            for g, b in ((0, 4), (1, 0)):
                act.wait_ge(a_vl, g + 1)
                nc.scalar.activation(gates[:, 4 * g:4 * g + 4, :], ps[:, b:b + 4, 256:304], ACT.Sigmoid)\
                    .then_inc(a_gate, 1)
            for t in range(2):
                act.wait_ge(a_mlp, 4)
                nc.scalar.activation(hb[:, t:t + 1], ps[:, 6, t:t + 1], ACT.Copy).then_inc(a_hb, 1)
                act.wait_ge(a_hb, t + 1)
                nc.scalar.activation(hid[:, t, :], ps[:, 4 + t, 0:P], ACT.Gelu_apprx_tanh, bias=hb[:, t:t + 1])\
                    .then_inc(a_hid, 1)
            act.wait_ge(a_cmp, 1)
            nc.scalar.activation(kch[:].rearrange("p v n -> p (v n)"), ps[:, 7, 0:P], ACT.Copy).then_inc(a_chi, 1)
            act.wait_ge(a_cmp, 2)
            nc.scalar.activation(vch[0:NCMP].rearrange("p v n -> p (v n)"), ps[0:NCMP, 0, 0:P], ACT.Copy)\
                .then_inc(a_chi, 1)

        def rope_dve(x, y, count):
            nc.vector.tensor_tensor(x, x, acos[:], ALU.mult).then_inc(a_rope, 1)
            nc.vector.tensor_tensor(y, y, asin[:], ALU.mult).then_inc(a_rope, 1)
            nc.vector.wait_ge(a_rope, count + 2)
            nc.vector.tensor_tensor(x, x, y, ALU.add).then_inc(a_rope, 1)

        def fixed_dve(dve):
            dve.wait_ge(att_consts_loaded, 7 * 16)
            for t in (kcs, vcs):
                nc.vector.memset(t[0:64, :, S:S + 16], 0.0).then_inc(a_pad, 1)
                nc.vector.memset(t[64:128, :, S - 1:S + 16], 0.0).then_inc(a_pad, 1)
            nc.vector.memset(vch[64:128].bitcast(F32), 0.0).then_inc(a_pad, 1)
            nc.vector.memset(vcl[64:128].bitcast(F32), 0.0).then_inc(a_pad, 1)
            nc.vector.tensor_copy(maskr[:], maskf[:, 0:VALID]).then_inc(a_mask, 1)
            nc.vector.tensor_copy(identr[:], ident[:]).then_inc(a_mask, 1)
            dve.wait_ge(a_swp, 64)
            rope_dve(fraw[:, 0, :], fswp[:], 0)
            dve.wait_ge(a_swp, 128)
            rope_dve(fraw[:, 0, :], fswp[:], 3)
            dve.wait_ge(a_hi, 1)
            nc.vector.tensor_tensor(qlo[:], fraw[:, 0, :], qhi[:].bitcast(F32), ALU.subtract).then_inc(a_lo, 1)
            dve.wait_ge(a_swp, 192)
            rope_dve(fraw[:, 1, :], fswp[:], 6)
            dve.wait_ge(a_hi, 2)
            nc.vector.tensor_tensor(qlo[:], fraw[:, 1, :], qhi[:].bitcast(F32), ALU.subtract).then_inc(a_lo, 1)
            for g, b in ((0, 4), (1, 0)):
                dve.wait_ge(a_vh, g + 1)
                nc.vector.tensor_tensor(Vl[:, 4 * g:4 * g + 4, :], ps[:, b:b + 4, 0:256],
                                        Vh[:, 4 * g:4 * g + 4, :].bitcast(F32), ALU.subtract).then_inc(a_vl, 1)
            dve.wait_ge(a_gate, 2)
            first = gates[:, 0, :].rearrange("p (n b h) -> p n b h", b=3, h=2)[:, :, 0, :]
            nc.vector.tensor_scalar(first, first, maskf[:, VALID:VALID + 1], None, ALU.mult).then_inc(a_gv, 1)
            dve.wait_ge(a_chi, 1)
            nc.vector.tensor_tensor(kcl[:].rearrange("p v n -> p (v n)"), ps[:, 7, 0:P],
                                    kch[:].rearrange("p v n -> p (v n)").bitcast(F32), ALU.subtract).then_inc(a_clo, 1)
            dve.wait_ge(a_chi, 2)
            nc.vector.tensor_tensor(vcl[0:NCMP].rearrange("p v n -> p (v n)"), ps[0:NCMP, 0, 0:P],
                                    vch[0:NCMP].rearrange("p v n -> p (v n)").bitcast(F32), ALU.subtract)\
                .then_inc(a_clo, 1)
            nc.vector.memset(Pw[:, :, 5 * P + NCMP:6 * P], 0.0).then_inc(a_pad, 1)

        UNITS = 2 * SC
        GROUPS = [groups_of(u // 2) for u in range(UNITS)]
        GOFF = [sum(len(g) for g in GROUPS[:u]) for u in range(UNITS + 1)]
        NG = GOFF[-1]
        FILL = 3 * 48
        BR = {"cmp": 0, "sel": 1, "win": 2}
        TURNS = []
        for u_ in range(UNITS):
            TURNS += [("g", GOFF[u_] + g_) for g_ in range(len(GROUPS[u_]))]
            if u_ >= 2 and u_ % 2 == 0:
                TURNS.append(("y", u_ // 2 - 1))
        TURNS.append(("y", SC - 1))
        assert NG % 2 == 0 and len(TURNS) % 2 == 0
        O_BANK, F_BANK, T_BANK = 6, 7, 4

        q_swp, q_steps, q_roped, q_asm = sem("q_swapped"), sem("q_rope_steps"), sem("q_roped"), sem("q_placed")
        fill_half, fill_out, m_stored = sem("fill_half"), sem("fill_out"), sem("merge_logits_stored")
        att_s, att_mx, att_nm, att_exp = sem("att_scores"), sem("att_max"), sem("att_neg_max"), sem("att_exp")
        att_tr, att_hi, att_lo, att_pv = sem("att_turned"), sem("att_pt_hi"), sem("att_pt_lo"), sem("att_pv")
        att_c, att_og, att_y = sem("att_weights"), sem("att_gated_sem"), sem("att_y_rows")
        att_yt, att_yc, y_stored = sem("att_y_turned"), sem("att_y_copied"), sem("y_att_stored")

        def fill_pe(pe, base, done, slot0, m0, m1):
            for m in range(m0, m1):
                blk, half, r = m // 48, m // 24 % 2, m % 24
                k, pas = divmod(r, 3)
                slot = (slot0 + blk) % 2
                if r == 0:
                    if half == 0:
                        pe.wait_ge(block_split, base + (blk + 1))
                    pe.wait_ge(fill_out, done + (2 * blk + half))
                w = (wl if pas == 2 else wh)[:, slot, k * P:(k + 1) * P]
                x = (XL if pas == 1 else XH)[:, k, half * HALF:(half + 1) * HALF]
                mm = nc.tensor.matmul(ps[:, F_BANK, :], w, x, start=(r == 0), stop=(r == 23))
                if r == 23:
                    mm.then_inc(blocks_multiplied if half else fill_half, 1)

        def scores_pe(pe, n, kv, u):
            qi, h = divmod(u, 2)
            q2 = qst[:, h, qi * P:(qi + 1) * P]
            q1 = qst[0:64, h, qi * P:(qi + 1) * P]

            def block(out, k_hi, k_lo, masks):
                nc.tensor.matmul(out, q2, k_hi, start=True, stop=False)
                for col, w, m in masks:
                    nc.tensor.matmul(out[:, col:col + w], identr[:], m, start=False, stop=False)
                return nc.tensor.matmul(out, q1, k_lo, start=False, stop=True)

            diag, edge = maskr[:, 0:P], maskr[:, P:2 * P]
            if u >= 1:
                pe.wait_ge(att_exp, n * 48 + (3 * u - 2))
            for g in range(qi // 4 + 1):
                a, b = g * HALF, min((g + 1) * HALF, (qi + 1) * P)
                mm = block(ps[:, g, 0:b - a], kk[:, 0, kv, a:b], kl[0:64, 0, kv, a:b],
                           [(qi % 4 * P, P, diag)] if g == qi // 4 else [])
            mm.then_inc(att_s, 1)
            if u >= 1:
                pe.wait_ge(att_exp, n * 48 + 3 * u)
            lo = max(0, qi - 4)
            nb = qi - lo + 1
            for g in range((nb + 3) // 4):
                a, b = (lo + 4 * g) * P, (lo + min(nb, 4 * g + 4)) * P
                masks = [(0, P, edge)] if qi >= 4 and g == 0 else []
                if g == (nb - 1) // 4:
                    masks.append(((nb - 1) % 4 * P, P, diag))
                block(ps[:, 2 + g, 0:b - a], kk[:, 1, kv, a:b], kl[0:64, 1, kv, a:b], masks)
            block(ps[:, 3, P:P + NCMP], kch[:, kv, :], kcl[0:64, kv, :],
                  [(0, NCMP, maskr[:, CMPM + qi * NCMP:CMPM + (qi + 1) * NCMP])]).then_inc(att_s, 1)

        def bank_free(pe, n, turn):
            if turn >= 2:
                kind, i = TURNS[turn - 2]
                pe.wait_ge(att_lo if kind == "g" else att_yc, n * (NG if kind == "g" else SC) + (i + 1))

        def turn_pe(pe, n, u, g):
            turn = TURNS.index(("g", GOFF[u] + g))
            group = GROUPS[u][g]
            pe.wait_ge(att_exp, n * 48 + (3 * u + (1 if group[0][0] == "sel" else 3)))
            bank_free(pe, n, turn)
            for j, (kind, _, col) in enumerate(group):
                probs = Ps if kind == "sel" else Pw
                mm = nc.tensor.transpose(ps[:, T_BANK + turn % 2, j * P:(j + 1) * P],
                                         probs[:, u % 2, col:col + P], ident[:])
            mm.then_inc(att_tr, 1)

        def pv_pe(pe, n, kv, u, g):
            qi, h = divmod(u, 2)
            seq = GOFF[u] + g
            if g == 0 and h == 0 and qi >= 1:
                pe.wait_ge(att_og, n * SC + qi)
            pe.wait_ge(att_lo, n * NG + (seq + 1))
            last_kb = {"sel": qi, "win": qi, "cmp": None}
            for j, (kind, kb, _) in enumerate(GROUPS[u][g]):
                first = kind == "cmp" or kb == (0 if kind == "sel" else max(0, qi - 4))
                out = ps[:, O_BANK, (BR[kind] * 2 + h) * DH:(BR[kind] * 2 + h + 1) * DH]
                if kind == "cmp":
                    v_h, v_l = vch[:, kv, :], vcl[:, kv, :]
                else:
                    at = slice((BR[kind] - 1) * P + kv * DH, (BR[kind] - 1) * P + (kv + 1) * DH)
                    v_h, v_l = Vh[:, kb, at], Vl[:, kb, at]
                mm = matmul3(out, PTh[:, seq % 2, j * P:(j + 1) * P], PTl[:, seq % 2, j * P:(j + 1) * P], v_h, v_l,
                             first, kb == last_kb[kind])
            mm.then_inc(att_pv, 1)

        def y_pe(pe, n, qi):
            turn = TURNS.index(("y", qi))
            pe.wait_ge(att_y, n * SC + (qi + 1))
            bank_free(pe, n, turn)
            nc.tensor.transpose(ps[:, T_BANK + turn % 2, 0:P], yn[:, qi % 2, :], ident[:]).then_inc(att_yt, 1)

        def att_pe(pe):
            fixed_pe(pe)
            pe.wait_ge(a_clo, 2)
            pe.wait_ge(block_split, B_Q0 + 1)
            for half in range(2):
                for k in range(KC):
                    if half == 1 and k == 0:
                        pe.wait_ge(fill_out, 1)
                    w_h, w_l = wh[:, 0, k * P:(k + 1) * P], wl[:, 0, k * P:(k + 1) * P]
                    at = slice(half * HALF, (half + 1) * HALF)
                    mm = matmul3(ps[:, F_BANK, :], w_h, w_l, XH[:, k, at], XL[:, k, at], k == 0, k == KC - 1)
                mm.then_inc(blocks_multiplied if half else fill_half, 1)
            pe.wait_ge(a_mask, 2)
            pe.wait_ge(a_kk, 192)
            pe.wait_ge(a_pad, 7)
            with pe.Fori(0, PAIRS // 2) as i:
                for kv in range(KV):
                    n = i * 2 + kv
                    pe.wait_ge(q_asm, n * 64 + 64)
                    scores_pe(pe, n, kv, 0)
                    filled = 0
                    for u in range(UNITS):
                        if u + 1 < UNITS:
                            scores_pe(pe, n, kv, u + 1)
                        ng = len(GROUPS[u])
                        turn_pe(pe, n, u, 0)
                        for g in range(ng):
                            if g + 1 < ng:
                                turn_pe(pe, n, u, g + 1)
                            upto = FILL * (GOFF[u] + g + 1) // NG
                            fill_pe(pe, n * 3 + B_PAIR, n * 6 + 2, (B_PAIR + 3 * kv) % 2, filled, upto)
                            filled = upto
                            pv_pe(pe, n, kv, u, g)
                        if u >= 2 and u % 2 == 0:
                            y_pe(pe, n, u // 2 - 1)
                    y_pe(pe, n, SC - 1)
                    pe.wait_ge(att_yc, n * SC + SC)

        def fill_act(act, n, j):
            blk, half = divmod(j, 2)
            at = slice(half * HALF, (half + 1) * HALF)
            if half == 0:
                act.wait_ge(fill_half, n * 3 + (blk + 2))
            else:
                act.wait_ge(blocks_multiplied, n * 3 + (B_PAIR + blk + 1))
            if blk == 0:
                nc.scalar.activation(raw[:, at], ps[:, F_BANK, :], ACT.Copy).then_inc(fill_out, 1)
                if half == 1:
                    act.wait_ge(fill_out, n * 6 + 4)
                    swap32(act, swp, raw, q_swp)
            else:
                act.wait_ge(m_stored, n * 64 + 16 * (2 * (blk - 1) + half + 1))
                nc.scalar.activation(fm[:], ps[:, F_BANK, :], ACT.Copy).then_inc(fill_out, 1)
                act.wait_ge(fill_out, n * 6 + (2 * blk + half + 3))
                act.dma_start(ml_d[bass.ds(n + (KC if blk == 2 else 0), 1), :, at].rearrange("a p n -> p (a n)"),
                              fm[:]).then_inc(m_stored, 16)

        def exp_act(act, n, u, part):
            qi, h = divmod(u, 2)

            def exp(kind, out, src):
                b = BR[kind]
                nc.scalar.activation(out, src, ACT.Exp, bias=nm[:, u % 2, b:b + 1], scale=ATT_SCALE,
                                     accum_out=ls[:, qi % 2, b, h:h + 1]).then_inc(att_exp, 1)

            if part == 0:
                act.wait_ge(att_nm, n * 32 + (2 * u + 1))
                exp("sel", Ps[:, u % 2, 0:(qi + 1) * P], two_banks(0)[:, 0:(qi + 1) * P])
            else:
                act.wait_ge(att_nm, n * 32 + (2 * u + 2))
                w = (min(qi, 4) + 1) * P
                exp("win", Pw[:, u % 2, 0:w], two_banks(2)[:, 0:w])
                exp("cmp", Pw[:, u % 2, 5 * P:5 * P + NCMP], ps[:, 3, P:P + NCMP])

        def hi_act(act, n, u, g):
            seq = GOFF[u] + g
            turn = TURNS.index(("g", seq))
            w = len(GROUPS[u][g]) * P
            act.wait_ge(att_tr, n * NG + (seq + 1))
            if seq >= 2:
                act.wait_ge(att_pv, n * NG + (seq - 1))
            nc.scalar.activation(PTh[:, seq % 2, 0:w], ps[:, T_BANK + turn % 2, 0:w], ACT.Copy).then_inc(att_hi, 1)

        def y_act(act, n, qi):
            turn = TURNS.index(("y", qi))
            act.wait_ge(att_yt, n * SC + (qi + 1))
            if qi == 0:
                act.wait_ge(y_stored, n * 16 + 16)
            nc.scalar.activation(yT[:, qi * P:(qi + 1) * P], ps[:, T_BANK + turn % 2, 0:P], ACT.Copy)\
                .then_inc(att_yc, 1)

        def place_q(act):
            for h in range(2):
                act.dma_start(qst[0:64, h, :].bitcast(F32), qhi[64 * h:64 * h + 64, :].bitcast(F32)).then_inc(q_asm, 16)
                act.dma_start(qst[64:128, h, :].bitcast(F32), qlo[64 * h:64 * h + 64, :].bitcast(F32)).then_inc(q_asm, 16)

        FILL_AT = [min(s_ for s_ in range(NG) if FILL * (s_ + 1) // NG >= 24 * (j + 1)) for j in range(6)]

        def att_act(act):
            fixed_act(act)
            nc.scalar.sem_inc(m_stored, 16)
            nc.scalar.sem_inc(y_stored, 16)
            act.wait_ge(a_pad, 7)
            for half in range(2):
                if half == 0:
                    act.wait_ge(fill_half, 1)
                else:
                    act.wait_ge(blocks_multiplied, B_Q0 + 1)
                nc.scalar.activation(raw[:, half * HALF:(half + 1) * HALF], ps[:, F_BANK, :], ACT.Copy)\
                    .then_inc(fill_out, 1)
            act.wait_ge(fill_out, 2)
            swap32(act, swp, raw, q_swp)
            act.wait_ge(q_roped, 1)
            place_q(act)
            with act.Fori(0, PAIRS // 2) as i:
                for kv in range(KV):
                    n = i * 2 + kv
                    exp_act(act, n, 0, 0)
                    exp_act(act, n, 0, 1)
                    for u in range(UNITS):
                        for g in range(max(2, len(GROUPS[u]))):
                            if g < len(GROUPS[u]):
                                hi_act(act, n, u, g)
                            if g < 2 and u + 1 < UNITS:
                                exp_act(act, n, u + 1, g)
                            for j in range(6):
                                at = FILL_AT[j] - GOFF[u]
                                if 0 <= at < len(GROUPS[u]) and g == min(at + 1, len(GROUPS[u]) - 1):
                                    fill_act(act, n, j)
                        if u >= 2 and u % 2 == 0:
                            y_act(act, n, u // 2 - 1)
                    y_act(act, n, SC - 1)
                    act.wait_ge(att_yc, n * SC + SC)
                    act.dma_start(ya_d[bass.ds(n, 1)].rearrange("a p n -> p (a n)"), yT[:]).then_inc(y_stored, 16)
                    act.wait_ge(q_roped, n + 2)
                    place_q(act)

        def max_dve(dve, n, u, part):
            qi = u // 2
            p = u % 2
            if part == 0:
                dve.wait_ge(att_s, n * 32 + (2 * u + 1))
                nc.vector.reduce_max(mx[:, p, 1:2], two_banks(0)[:, 0:(qi + 1) * P], AX.X).then_inc(att_mx, 1)
                dve.wait_ge(att_mx, n * 48 + (3 * u + 1))
                nc.vector.tensor_scalar(nm[:, p, 1:2], mx[:, p, 1:2], -ATT_SCALE, None, ALU.mult).then_inc(att_nm, 1)
            else:
                w = (min(qi, 4) + 1) * P
                dve.wait_ge(att_s, n * 32 + (2 * u + 2))
                nc.vector.reduce_max(mx[:, p, 2:3], two_banks(2)[:, 0:w], AX.X).then_inc(att_mx, 1)
                nc.vector.reduce_max(mx[:, p, 0:1], ps[:, 3, P:P + NCMP], AX.X).then_inc(att_mx, 1)
                dve.wait_ge(att_mx, n * 48 + (3 * u + 3))
                nc.vector.tensor_scalar(nm[:, p, 0:3:2], mx[:, p, 0:3:2], -ATT_SCALE, None, ALU.mult)\
                    .then_inc(att_nm, 1)

        def lo_dve(dve, n, u, g):
            seq = GOFF[u] + g
            turn = TURNS.index(("g", seq))
            w = len(GROUPS[u][g]) * P
            dve.wait_ge(att_hi, n * NG + (seq + 1))
            nc.vector.tensor_tensor(PTl[:, seq % 2, 0:w], ps[:, T_BANK + turn % 2, 0:w],
                                    PTh[:, seq % 2, 0:w].bitcast(F32), ALU.subtract).then_inc(att_lo, 1)

        def combine_dve(dve, n, i, kv, qi):
            dve.wait_ge(att_pv, n * NG + GOFF[2 * qi + 2])
            nc.vector.tensor_scalar(lm[:], ls[:, qi % 2].rearrange("p b h -> p (b h)"), 1e-30, None, ALU.max)\
                .then_inc(att_c, 1)
            dve.wait_ge(att_c, n * 24 + (3 * qi + 1))
            nc.vector.reciprocal(li[:], lm[:]).then_inc(att_c, 1)
            dve.wait_ge(att_c, n * 24 + (3 * qi + 2))
            nc.vector.tensor_tensor(rg[:], li[:], gates[:, qi, bass.ds(i * 12 + 6 * kv, 6)], ALU.mult)\
                .then_inc(att_c, 1)
            dve.wait_ge(att_c, n * 24 + (3 * qi + 3))
            nc.vector.tensor_tensor(og[:].rearrange("p b h d -> p (b h) d"),
                                    ps[:, O_BANK, 0:6 * DH].rearrange("p (c d) -> p c d", c=6),
                                    rg[:].unsqueeze(2).to_broadcast([P, 6, DH]), ALU.mult).then_inc(att_og, 1)
            dve.wait_ge(att_og, n * SC + (qi + 1))
            nc.vector.tensor_reduce(yn[:, qi % 2, :], og[:].rearrange("p b h d -> p (h d) b"), AX.X, ALU.add)\
                .then_inc(att_y, 1)

        def att_dve(dve):
            fixed_dve(dve)
            dve.wait_ge(a_gv, 1)
            with dve.Fori(0, PAIRS // 2) as i:
                for kv in range(KV):
                    n = i * 2 + kv
                    max_dve(dve, n, 0, 0)
                    max_dve(dve, n, 0, 1)
                    for u in range(UNITS):
                        if u + 1 < UNITS:
                            max_dve(dve, n, u + 1, 0)
                        if u >= 2 and u % 2 == 0:
                            combine_dve(dve, n, i, kv, u // 2 - 1)
                        for g in range(max(2, len(GROUPS[u]))):
                            if g < len(GROUPS[u]):
                                lo_dve(dve, n, u, g)
                            if g == 0 and u + 1 < UNITS:
                                max_dve(dve, n, u + 1, 1)
                    combine_dve(dve, n, i, kv, SC - 1)

        def rope_pool(pool, r):
            tt = nc.gpsimd.tensor_tensor
            pool.wait_ge(q_swp, r * 64 + 64)
            tt(raw[:], raw[:], acos[:], ALU.mult).then_inc(q_steps, 1)
            tt(swp[:], swp[:], asin[:], ALU.mult).then_inc(q_steps, 1)
            pool.wait_ge(q_steps, r * 4 + 2)
            tt(raw[:], raw[:], swp[:], ALU.add).then_inc(q_steps, 1)
            pool.wait_ge(q_steps, r * 4 + 3)

        def rope_pool_split(pool, r):
            tt = nc.gpsimd.tensor_tensor
            tt(qhi[:], raw[:], zero[:].to_broadcast([P, S]), ALU.add).then_inc(q_steps, 1)
            pool.wait_ge(q_steps, r * 4 + 4)
            tt(qlo[:], raw[:], qhi[:].bitcast(F32), ALU.subtract).then_inc(q_roped, 1)

        def att_pool(pool, split):
            pool.wait_ge(att_consts_loaded, 7 * 16)
            pool.wait_ge(a_kk, 192)
            rope_pool(pool, 0)
            rope_pool_split(pool, 0)
            with pool.Fori(0, PAIRS // 2) as i:
                for kv in range(KV):
                    n = i * 2 + kv
                    for j in range(3):
                        if j == 2:
                            rope_pool(pool, n + 1)
                            pool.wait_ge(q_asm, n * 64 + 64)
                            rope_pool_split(pool, n + 1)
                        b = B_PAIR + 1 + 3 * kv + j
                        split(b % 2, i * 6 + b, i * 3 + (b // 2 + 1))
        m_ld = [sem("y_chunk_loaded0"), sem("y_chunk_loaded1")]
        m_hi, m_lo = sem("m_y_hi"), sem("m_y_lo")
        mt_ld = [sem("gate_loaded0"), sem("gate_loaded1")]
        m_gate, m_out, m_tmp, m_sum = sem("m_gate"), sem("m_out"), sem("m_gated_a"), sem("m_sum")
        x_hi, x_lo = sem("mix_hi_done"), sem("mix_lo_done")

        def merge_pe(pe):
            for xh, xl, b0, ready in ((YH, YL, B_WB, 0), (XH, XL, B_WA, KC)):
                pe.wait_ge(m_lo, ready + 1)
                with pe.Fori(0, 2) as i:
                    for j in range(4):
                        pe.wait_ge(m_out, i * 4 + (ready + j + 1))
                        if j == 0:
                            pe.wait_ge(block_split, i * 4 + (b0 + 1))
                        merge_job(pe, (b0 + j) % 2, i * 4 + (b0 + j + 1), xh, xl, 2 * j, ready)

        def merge_job(pe, slot, n, xh, xl, bank, ready):
            pe.wait_ge(block_split, n)
            for k in range(KC):
                pe.wait_ge(m_lo, ready + k + 1)
                w_h, w_l = wh[:, slot, k * P:(k + 1) * P], wl[:, slot, k * P:(k + 1) * P]
                for w, x in ((w_h, xh), (w_h, xl), (w_l, xh)):
                    for half in range(2):
                        mm = nc.tensor.matmul(ps[:, bank + half, :], w, x[:, k, half * HALF:(half + 1) * HALF],
                                              start=(k == 0 and w is w_h and x is xh),
                                              stop=(k == KC - 1 and w is w_l))
            mm.then_inc(blocks_multiplied, 1)

        def merge_act(act):
            act.wait_ge(q_asm, (PAIRS + 1) * 64)
            act.wait_ge(y_stored, (PAIRS + 1) * 16)
            act.wait_ge(m_stored, (4 * PAIRS + 1) * 16)

            def load_y(k):
                if k >= 2:
                    act.wait_ge(m_lo, k - 1)
                act.dma_start(ring2[:, k % 2, :], (yr_d if k < KC else ya_d)[k % KC]).then_inc(m_ld[k % 2], 16)

            def split_y(k):
                act.wait_ge(m_ld[k % 2], 16 * (k // 2 + 1))
                dst = YH if k < KC else XH
                nc.scalar.activation(dst[:, k % KC, :], ring2[:, k % 2, :], ACT.Copy).then_inc(m_hi, 1)
                if k + 2 < 2 * KC:
                    load_y(k + 2)

            def load_gate(n):
                if n >= 2:
                    act.wait_ge(m_out, 4 + n - 1)
                act.dma_start(mt[:, n % 2, :], ml_d[n]).then_inc(mt_ld[n % 2], 16)

            load_y(0)
            load_y(1)
            load_gate(0)
            load_gate(1)
            for k in range(KC):
                split_y(k)
            for n in range(2 * KC):
                act.wait_ge(mt_ld[n % 2], 16 * (n // 2 + 1))
                nc.scalar.activation(mt[:, n % 2, :], mt[:, n % 2, :], ACT.Sigmoid).then_inc(m_gate, 1)
                if n < KC:
                    split_y(KC + n)
                else:
                    act.wait_ge(m_sum, n - KC + 1)
                    nc.scalar.activation(YH[:, n - KC, :], x2[:, n - KC, :], ACT.Copy).then_inc(x_hi, 1)
                if n + 2 < 2 * KC:
                    load_gate(n + 2)
            out_act(act)

        def merge_dve(dve):
            nc.vector.sem_inc(m_out, 4)

            def split_y(k):
                dve.wait_ge(m_hi, k + 1)
                hi, lo = (YH, YL) if k < KC else (XH, XL)
                nc.vector.tensor_tensor(lo[:, k % KC, :], ring2[:, k % 2, :], hi[:, k % KC, :].bitcast(F32),
                                        ALU.subtract).then_inc(m_lo, 1)

            for k in range(KC):
                split_y(k)
            for n in range(2 * KC):
                if n < KC:
                    split_y(KC + n)
                dve.wait_ge(m_gate, n + 1)
                dve.wait_ge(blocks_multiplied, B_WB + n + 1)
                if n < KC:
                    nc.vector.tensor_tensor(x2[:, n, :], two_banks(2 * (n % 4)), mt[:, n % 2, :], ALU.mult)\
                        .then_inc(m_out, 1)
                    continue
                k = n - KC
                if k >= 1:
                    dve.wait_ge(m_sum, k)
                nc.vector.tensor_tensor(tmp[:], two_banks(2 * (n % 4)), mt[:, n % 2, :], ALU.mult).then_inc(m_out, 1)
                dve.wait_ge(m_out, 4 + n + 1)
                nc.vector.tensor_tensor(x2[:, k, :], x2[:, k, :], tmp[:], ALU.add).then_inc(m_sum, 1)
                dve.wait_ge(x_hi, k + 1)
                nc.vector.tensor_tensor(YL[:, k, :], x2[:, k, :], YH[:, k, :].bitcast(F32), ALU.subtract)\
                    .then_inc(x_lo, 1)
            out_dve(dve)

        o_out, o_gain, o_x = sem("o_out"), sem("o_gains_loaded"), [sem("x_again0"), sem("x_again1")]
        o_sq, o_ms, o_rms, o_rstd = sem("o_sq"), sem("o_ms"), sem("o_rms"), sem("o_rstd")
        o_nrm, o_x2 = sem("o_normed"), sem("o_x_mid")
        p_sq, p_ms, p_rms, p_rstd = sem("p_sq"), sem("p_ms"), sem("p_rms"), sem("p_rstd")
        p_xn, p_tr, p_hi, p_lo = sem("p_xn"), sem("p_tr"), sem("p_hi"), sem("p_lo")

        def out_pe(pe):
            pe.wait_ge(x_lo, KC)
            for nh in range(2):
                for j in range(4):
                    b = B_WO + 4 * nh + j
                    pe.wait_ge(block_split, b + 1)
                    for k2 in range(2):
                        k = 2 * j + k2
                        for s in range(SC):
                            if nh == 1 and k == 0:
                                pe.wait_ge(o_out, s + 1)
                            at = slice(k2 * HALF, (k2 + 1) * HALF)
                            mm = matmul3(ps[:, s, :], YH[:, k, s * P:(s + 1) * P], YL[:, k, s * P:(s + 1) * P],
                                         wh[:, b % 2, at], wl[:, b % 2, at], k == 0, k == KC - 1)
                    mm.then_inc(blocks_multiplied, 1)
            pe.wait_ge(o_out, 2 * SC)
            norm_T_pe(pe, xn2, p_xn, p_tr, p_lo)

        def out_act(act):
            act.wait_ge(m_out, 4 + 2 * KC)
            act.dma_start(mt[:, 0, :], norm_d[1]).then_inc(o_gain, 16)
            act.dma_start(mt[:, 1, :], norm_d[2]).then_inc(o_gain, 16)
            act.wait_ge(m_lo, 2 * KC)
            for s in range(2):
                act.dma_start(ring2[:, s, :], x_d[s * P:(s + 1) * P, :]).then_inc(o_x[s], 16)
            act.wait_ge(x_lo, KC)
            for nh in range(2):
                act.wait_ge(blocks_multiplied, B_WO + 4 * (nh + 1))
                for s in range(SC):
                    nc.scalar.activation(x2[:, s, nh * HALF:(nh + 1) * HALF], ps[:, s, :], ACT.Copy).then_inc(o_out, 1)
            squares_act(act, x2, xn2[:, 0, :], o_sq, lambda s: act.wait_ge(o_out, SC + s + 1))
            act.wait_ge(o_ms, 1)
            nc.scalar.activation(rms[:], ms[:], ACT.Sqrt).then_inc(o_rms, 1)
            for s in range(SC):
                if s + 2 < SC:
                    act.wait_ge(o_x2, s + 1)
                    act.dma_start(ring2[:, s % 2, :], x_d[(s + 2) * P:(s + 3) * P, :]).then_inc(o_x[s % 2], 16)
            act.wait_ge(o_sq, SC)
            squares_act(act, x2, xn2[:, 0, :], p_sq, lambda s: act.wait_ge(o_x2, s + 1))
            act.wait_ge(p_ms, 1)
            nc.scalar.activation(rms[:], ms[:], ACT.Sqrt).then_inc(p_rms, 1)
            norm_T_act(act, XH, p_tr, p_hi)

        def out_dve(dve):
            mean_sq_dve(dve, o_sq, o_ms, o_rms, o_rstd)
            dve.wait_ge(o_rstd, 1)
            dve.wait_ge(o_gain, 32)
            for s in range(SC):
                nc.vector.scalar_tensor_tensor(out=x2[:, s, :], in0=x2[:, s, :], scalar=rstd[:, s:s + 1],
                                               in1=mt[:, 0, :], op0=ALU.mult, op1=ALU.mult).then_inc(o_nrm, 1)
                dve.wait_ge(o_nrm, s + 1)
                dve.wait_ge(o_x[s % 2], 16 * (s // 2 + 1))
                nc.vector.tensor_tensor(x2[:, s, :], x2[:, s, :], ring2[:, s % 2, :], ALU.add).then_inc(o_x2, 1)
            mean_sq_dve(dve, p_sq, p_ms, p_rms, p_rstd)
            norm_T_dve(dve, x2, mt[:, 1, :], xn2, p_rstd, p_xn, p_tr, XH, XL, p_hi, p_lo)
        f_silu, f_mul, f_hi, f_lo = sem("f_silu"), sem("f_mul"), sem("f_hi"), sem("f_lo")
        f_down, f_add = sem("f_down"), sem("f_add")
        f_gain = sem("f_gain_loaded")
        e_sq, e_ms, e_rms, e_rstd = sem("e_sq"), sem("e_ms"), sem("e_rms"), sem("e_rstd")
        e_nrm, e_y, out_stored = sem("e_normed"), sem("e_y"), sem("out_stored")
        DOWN = 2 * SC

        def ffn_gate_up_pe(pe, c, b, slot, first=False):
            if not first:
                pe.wait_ge(f_silu, c)
            t_job(pe, slot, b + 1, XH, XL, 0)
            if not first:
                pe.wait_ge(f_mul, c)
            t_job(pe, 1 - slot, b + 2, XH, XL, 2)

        def ffn_down_pe(pe, c, odd, b, slot, first=False):
            pe.wait_ge(block_split, b + 1)
            pe.wait_ge(f_lo, c + 1)
            for t in range(DOWN):
                s, nh = divmod(t, 2)
                if not (first and t < 4):
                    pe.wait_ge(f_add, c * DOWN + (t - 3))
                at = slice(nh * HALF, (nh + 1) * HALF)
                mm = matmul3(ps[:, 4 + t % 4, :], FH[:, odd, s * P:(s + 1) * P], FL[:, odd, s * P:(s + 1) * P],
                             wh[:, slot, at], wl[:, slot, at], True, True)
                mm.then_inc(f_down if t < DOWN - 1 else blocks_multiplied, 1)

        def ffn_pe(pe):
            out_pe(pe)
            pe.wait_ge(p_lo, 2 * SC)
            b = B_FFN
            ffn_gate_up_pe(pe, 0, b, b % 2, True)
            ffn_gate_up_pe(pe, 1, b + 2, b % 2)
            ffn_down_pe(pe, 0, 0, b + 4, b % 2, True)
            with pe.Fori(0, FF // 2 - 1) as i:
                for j in range(2):
                    c = i * 2 + (2 + j)
                    bj = i * 6 + (b + 5 + 3 * j)
                    slot = (b + 5 + 3 * j) % 2
                    ffn_gate_up_pe(pe, c, bj, slot)
                    ffn_down_pe(pe, i * 2 + (1 + j), 1 - j, bj + 2, slot)
            ffn_down_pe(pe, FF - 1, (FF - 1) % 2, N_BLOCKS - 1, (N_BLOCKS - 1) % 2)

        def ffn_chunk_act(act, c, odd, gate_block):
            act.wait_ge(blocks_multiplied, gate_block + 1)
            nc.scalar.activation(sg[:], two_banks(0), ACT.Silu).then_inc(f_silu, 1)
            act.wait_ge(f_mul, c + 1)
            nc.scalar.activation(FH[:, odd, :], ff[:], ACT.Copy).then_inc(f_hi, 1)

        def ffn_act(act):
            act.dma_start(gc[:], norm_d[3]).then_inc(f_gain, 16)
            ffn_chunk_act(act, 0, 0, B_FFN)
            ffn_chunk_act(act, 1, 1, B_FFN + 2)
            with act.Fori(0, FF // 2 - 1) as i:
                for j in range(2):
                    ffn_chunk_act(act, i * 2 + (2 + j), j, i * 6 + (B_FFN + 5 + 3 * j))
            squares_act(act, acc, xn2[:, 0, :], e_sq, lambda s: act.wait_ge(f_add, (FF - 1) * DOWN + 2 * s + 2))
            act.wait_ge(e_ms, 1)
            nc.scalar.activation(rms[:], ms[:], ACT.Sqrt).then_inc(e_rms, 1)
            for s in range(SC):
                act.wait_ge(e_y, s + 1)
                act.dma_start(out_d[s * P:(s + 1) * P, :], acc[:, s, :]).then_inc(out_stored, 16)
            act.wait_ge(out_stored, SC * 16)

        def ffn_mul_dve(dve, c, gate_block, later=True):
            dve.wait_ge(f_silu, c + 1)
            dve.wait_ge(blocks_multiplied, gate_block + 2)
            if later:
                dve.wait_ge(f_lo, c)
            nc.vector.tensor_tensor(ff[:], two_banks(2), sg[:], ALU.mult).then_inc(f_mul, 1)

        def ffn_lo_dve(dve, c, odd):
            dve.wait_ge(f_hi, c + 1)
            nc.vector.tensor_tensor(FL[:, odd, :], ff[:], FH[:, odd, :].bitcast(F32), ALU.subtract).then_inc(f_lo, 1)

        def ffn_add_dve(dve, c, down_block, t, first=False):
            s, nh = divmod(t, 2)
            if t < DOWN - 1:
                dve.wait_ge(f_down, c * (DOWN - 1) + (t + 1))
            else:
                dve.wait_ge(blocks_multiplied, down_block + 1)
            tile_ = acc[:, s, nh * HALF:(nh + 1) * HALF]
            if first:
                nc.vector.tensor_copy(tile_, ps[:, 4 + t % 4, :]).then_inc(f_add, 1)
            else:
                dve.wait_ge(f_add, c * DOWN + (t + 1 - DOWN))
                nc.vector.tensor_tensor(tile_, tile_, ps[:, 4 + t % 4, :], ALU.add).then_inc(f_add, 1)

        def ffn_dve(dve):
            ffn_mul_dve(dve, 0, B_FFN, False)
            ffn_lo_dve(dve, 0, 0)
            ffn_mul_dve(dve, 1, B_FFN + 2)
            ffn_lo_dve(dve, 1, 1)
            for t in range(DOWN):
                ffn_add_dve(dve, 0, B_FFN + 4, t, True)
            with dve.Fori(0, FF // 2 - 1) as i:
                for j in range(2):
                    gate_block = i * 6 + (B_FFN + 5 + 3 * j)
                    ffn_mul_dve(dve, i * 2 + (2 + j), gate_block)
                    for t in range(DOWN):
                        ffn_add_dve(dve, i * 2 + (1 + j), gate_block + 2, t)
                        if t == 2:
                            ffn_lo_dve(dve, i * 2 + (2 + j), j)
            for t in range(DOWN):
                ffn_add_dve(dve, FF - 1, N_BLOCKS - 1, t)
            mean_sq_dve(dve, e_sq, e_ms, e_rms, e_rstd)
            dve.wait_ge(e_rstd, 1)
            dve.wait_ge(f_gain, 16)
            for s in range(SC):
                nc.vector.scalar_tensor_tensor(out=acc[:, s, :], in0=acc[:, s, :], scalar=rstd[:, s:s + 1],
                                               in1=gc[:], op0=ALU.mult, op1=ALU.mult).then_inc(e_nrm, 1)
                dve.wait_ge(e_nrm, s + 1)
                nc.vector.tensor_tensor(acc[:, s, :], acc[:, s, :], x2[:, s, :], ALU.add).then_inc(e_y, 1)

        @block.sync
        def _(sp):
            for s in range(SC):
                sp.dma_start(xs[:, s, :], x_d[s * P:(s + 1) * P, :]).then_inc(x_loaded[s], 16)
                if s < 2:
                    sp.dma_start(wraw[:, s, :], wst_d[s]).then_inc(block_loaded[s], 16)
            with sp.Fori(0, (N_BLOCKS - 3) // 2) as i:
                for j in range(2):
                    sp.wait_ge(block_split, i * 2 + (j + 1))
                    sp.dma_start(wraw[:, j, :], wst_d[bass.ds(i * 2 + (2 + j), 1)].rearrange("a p n -> p (a n)"))\
                        .then_inc(block_loaded[j], 16)
            sp.wait_ge(block_split, N_BLOCKS - 2)
            sp.dma_start(wraw[:, 0, :], wst_d[N_BLOCKS - 1]).then_inc(block_loaded[0], 16)

        @block.gpsimd
        def _(pool):
            nc.gpsimd.memset(zero[:], 0.0).then_inc(zero_set, 1)
            pool.wait_ge(zero_set, 1)

            def split(slot, b, loads, reused=True):
                pool.wait_ge(block_loaded[slot], loads * 16)
                if reused:
                    pool.wait_ge(blocks_multiplied, b - 1)
                nc.gpsimd.tensor_tensor(wh[:, slot, :], wraw[:, slot, :], zero[:].to_broadcast([P, 1024]),
                                        ALU.add).then_inc(block_hi, 1)
                pool.wait_ge(block_hi, b + 1)
                nc.gpsimd.tensor_tensor(wl[:, slot, :], wraw[:, slot, :], wh[:, slot, :].bitcast(F32),
                                        ALU.subtract).then_inc(block_split, 1)

            split(0, 0, 1, False)
            split(1, 1, 1, False)
            with pool.Fori(0, B_Q0 // 2) as i:
                for j in range(2):
                    split(j, i * 2 + (2 + j), i + 2)
            att_pool(pool, split)
            first = B_WB + 1
            with pool.Fori(0, (N_BLOCKS - 1 - first) // 2) as i:
                for j in range(2):
                    split(j, i * 2 + (first + j), i + (first // 2 + 1))
            split(0, N_BLOCKS - 1, N_BLOCKS // 2 + 1)

        @block.tensor
        def _(pe):
            s1_pe(pe)
            ret_pe(pe)
            att_pe(pe)
            merge_pe(pe)
            ffn_pe(pe)

        @block.scalar
        def _(act):
            act.dma_start(ident[:], norm_d[4, :, 0:P]).then_inc(consts_loaded, 16)
            act.dma_start(g0[:], norm_d[0]).then_inc(consts_loaded, 16)
            s1_act(act)
            ret_act(act)
            att_act(act)
            merge_act(act)
            ffn_act(act)

        @block.vector
        def _(dve):
            s1_dve(dve)
            ret_dve(dve)
            att_dve(dve)
            merge_dve(dve)
            ffn_dve(dve)


def kernel(**inputs):
    import numpy as np
    import concourse.bacc as bacc
    from concourse.bass_utils import run_bass_kernel_spmd

    a = {k: np.asarray(v) for k, v in inputs.items()}
    w_in = a["w_in"][0]
    widths = (1024, 768, 48, 512, 512, 1024, 1024, 2048)
    ends = np.cumsum(widths)
    wq, wkv, wg, wqr, wkr, wvr, wgr, wm = (w_in[:, e - w:e] for e, w in zip(ends, widths))

    def t_blocks(w):
        return list(w.reshape(KC, P, -1, P).transpose(2, 1, 0, 3).reshape(-1, P, 1024))

    def row_blocks(w, n):
        per = 1024 // n
        return list(w.reshape(KC // per, per, P, n).transpose(0, 2, 1, 3).reshape(-1, P, 1024))

    q, kv = t_blocks(wq), t_blocks(wkv)
    qr, kr, gr, m = t_blocks(wqr), t_blocks(wkr), t_blocks(wgr), t_blocks(wm)
    order = [0, 4, 1, 5, 2, 6, 3, 7]
    gate_w = wg.reshape(D, PAIRS, 2, 3)[:, order].transpose(0, 1, 3, 2).reshape(D, 48)
    vsg = np.zeros((D, HALF), np.float32)
    vsg[:, 0:P], vsg[:, P:2 * P], vsg[:, 2 * P:2 * P + 48] = wkv[:, 3 * P:4 * P], wkv[:, 5 * P:6 * P], gate_w
    blocks = []
    for h in range(RH):
        blocks += row_blocks(wvr[:, h * DV:(h + 1) * DV], DV) + [qr[h], kr[h], gr[2 * h], gr[2 * h + 1]]
    blocks += [kv[0], kv[1], kv[2], kv[4]] + row_blocks(vsg, HALF)
    blocks.append(q[0])
    for n in range(PAIRS):
        blocks += [q[order[min(n + 1, PAIRS - 1)]], m[KC + n], m[n]]
    blocks += t_blocks(a["w_branch_b"][0])
    blocks += t_blocks(a["w_branch_a"][0].reshape(PAIRS, P, D)[order].reshape(D, D))
    wo = a["w_out"][0]
    blocks += row_blocks(wo[:, :HALF], HALF) + row_blocks(wo[:, HALF:], HALF)
    gate, up, down = t_blocks(a["w_ffn_gate"][0]), t_blocks(a["w_ffn_up"][0]), a["w_ffn_down"][0].reshape(FF, P, D)
    for c in range(FF):
        blocks += [gate[c], up[c]] + ([down[c - 1]] if c else [])
    blocks.append(down[FF - 1])
    assert len(blocks) == N_BLOCKS

    norm = np.zeros((5, P, D), np.float32)
    for i, name in enumerate(("g_pre_mix", "g_post_mix", "g_pre_ffn", "g_post_ffn")):
        norm[i] = np.broadcast_to(a[name][0], (P, D))
    norm[4, :, :P] = np.eye(P)

    def rope(d):
        half = d // 2
        inv = np.float32(10000.0) ** (-np.arange(half, dtype=np.float32) * np.float32(2.0) / np.float32(d))
        ang = (inv[:, None] * np.arange(S, dtype=np.float32)[None, :]).astype(np.float32).astype(np.float64)
        cos, sin = np.cos(ang), np.sin(ang)
        t = np.stack([np.concatenate([cos, cos]), np.concatenate([-sin, sin])])
        return np.ascontiguousarray(np.tile(t, (1, P // d, 1)).astype(np.float32))

    log_g = np.log1p(-np.exp2(-5.0 - np.arange(RH)))
    i = np.arange(P)
    ret = np.zeros((RH, P, P + 4), np.float32)
    diff = i[None, :] - i[:, None]
    for h in range(RH):
        ret[h, :, :P] = np.where(diff >= 0, np.exp(log_g[h] * np.maximum(diff, 0)), 0.0)
        ret[h, :, P] = np.exp(log_g[h] * (P - 1.0 - i))
        ret[h, :, P + 1] = np.exp(log_g[h] * (i + 1.0))
        ret[h, :, P + 2] = np.exp(log_g[h] * P)
    neg = np.float32(-1e30)
    t = np.arange(S).reshape(SC, P).T
    cmp_end = np.arange(NCMP) * 16 + 31
    mask = np.zeros((P, 2 * P + SC * NCMP + 1), np.float32)
    mask[:, 0:P] = np.where(i[None, :] > i[:, None], neg, 0)
    mask[:, P:2 * P] = np.where(i[None, :] <= i[:, None], neg, 0)
    seen = (cmp_end[None, None, :] <= t[:, :, None]) & (np.arange(NCMP) < NCMP - 1)
    mask[:, 2 * P:-1] = np.where(seen, 0, neg).reshape(P, -1)
    mask[:, -1] = i >= 31

    arrays = {
        "x": a["x"][0],
        "weights": np.stack(blocks),
        "norm": norm,
        "rope_a": rope(DH),
        "rope_r": rope(128),
        "ret": ret,
        "mask": mask,
        "w1": np.stack([a[f"cmp_w1_{c}"][0].reshape(16, P, P).transpose(1, 0, 2) for c in "kv"], 1),
        "pos": np.stack([a[f"cmp_pos_{c}"][0].reshape(16, P).T for c in "kv"], 1),
        "w2k": np.concatenate([a["cmp_w2_k"][0]] * 2, 1),
        "w2v": a["cmp_w2_v"][0],
    }
    nc = bacc.Bacc("TRN2", target_bir_lowering=False, num_devices=1)
    args = []
    for name in arrays:
        arrays[name] = np.ascontiguousarray(arrays[name])
        args.append(nc.dram_tensor(name, arrays[name].shape, F32, kind="ExternalInput").ap())
    args.append(nc.dram_tensor("out", (S, D), F32, kind="ExternalOutput").ap())
    layer(nc, *args)
    r = run_bass_kernel_spmd(nc, [arrays], core_ids=[0])
    return r.results[0]["out"].reshape(1, S, D)
```

```python
from contextlib import ExitStack

import concourse.bass as bass
from concourse import mybir

F32 = mybir.dt.float32
FR = mybir.dt.float32r
ALU = mybir.AluOpType
ACT = mybir.ActivationFunctionType
AX = mybir.AxisListType

P = 128
S = 1024
D = 1024
KC = D // P
SC = S // P
HALF = 512
DH = 64
KV = 2
NCMP = 64
RH = 4
DV = 256
FF = 2816 // P
EPS = 1e-6
ATT_SCALE = DH ** -0.5
RET_SCALE = 128 ** -0.5
PAIRS = 8

B_RET = 6
B_KV = RH * B_RET
B_Q0 = B_KV + 8
B_PAIR = B_Q0 + 1
B_WB = B_PAIR + 3 * PAIRS
B_WA = B_WB + KC
B_WO = B_WA + KC
B_FFN = B_WO + KC
N_BLOCKS = B_FFN + 3 * FF


def groups_of(qi):
    sel = [("sel", kb, kb * P) for kb in range(qi + 1)]
    lo = max(0, qi - 4)
    win = [("win", kb, (kb - lo) * P) for kb in range(lo, qi + 1)] + [("cmp", None, 5 * P)]
    return [sel[a:a + 4] for a in range(0, len(sel), 4)] + [win[a:a + 4] for a in range(0, len(win), 4)]


def layer(nc, x_d, wst_d, norm_d, rope_a_d, rope_r_d, ret_d, mask_d, w1_d, pos_d, w2k_d, w2v_d, out_d):
    yr_d = nc.dram_tensor("y_ret_T", (KC, P, S), F32).ap()
    ya_d = nc.dram_tensor("y_att_T", (KC, P, S), F32).ap()
    ml_d = nc.dram_tensor("merge_logits_T", (2 * KC, P, S), F32).ap()

    with ExitStack() as ctx:
        def sem(name):
            return ctx.enter_context(nc.semaphore(name))

        def tile(scope, name, shape, dt=F32):
            return scope.enter_context(nc.sbuf_tensor(name, [P, *shape], dt))

        XH = tile(ctx, "act_hi", [KC, S], FR)
        XL = tile(ctx, "act_lo", [KC, S], FR)
        wraw = tile(ctx, "w_raw", [2, 1024])
        wh = tile(ctx, "w_hi", [2, 1024], FR)
        wl = tile(ctx, "w_lo", [2, 1024], FR)
        ident = tile(ctx, "ident", [P])
        zero = tile(ctx, "zero", [1])
        ss = tile(ctx, "sum_sq", [SC])
        ms = tile(ctx, "mean_sq", [SC])
        rms = tile(ctx, "rms", [SC])
        rstd = tile(ctx, "rstd", [SC])
        ps = ctx.enter_context(nc.psum_tensor("ps", [P, 8, HALF], F32))

        sc0 = ExitStack()
        xs = tile(sc0, "x_rows", [SC, D])
        g0 = tile(sc0, "g_pre_mix", [D])
        xn = tile(sc0, "x_normed", [2, D])
        sc0.close()
        scr = ExitStack()
        rcos = tile(scr, "ret_cos", [S])
        rsin = tile(scr, "ret_sin", [S])
        rraw = tile(scr, "ret_raw", [2, S])
        rswp = tile(scr, "ret_swapped", [S])
        rqh = tile(scr, "ret_q_hi", [S], FR)
        rql = tile(scr, "ret_q_lo", [S], FR)
        rkh = tile(scr, "ret_k_hi", [S], FR)
        rkl = tile(scr, "ret_k_lo", [S], FR)
        vh = tile(scr, "ret_v_hi", [SC, DV], FR)
        vl = tile(scr, "ret_v_lo", [SC, DV], FR)
        knh = tile(scr, "ret_kdec_hi", [SC, P], FR)
        knl = tile(scr, "ret_kdec_lo", [SC, P], FR)
        silu_g = tile(scr, "ret_silu_g", [2, S])
        ro = tile(scr, "ret_out", [SC, DV])
        ry = tile(scr, "ret_y_T", [2, S])
        hc = tile(scr, "ret_decays", [P + 4])
        im = tile(scr, "ret_inner", [2, P])
        imh = tile(scr, "ret_inner_hi", [2, P], FR)
        iml = tile(scr, "ret_inner_lo", [2, P], FR)
        R = tile(scr, "ret_state", [DV])
        Rh = tile(scr, "ret_state_hi", [2, DV], FR)
        Rl = tile(scr, "ret_state_lo", [2, DV], FR)
        t2 = tile(scr, "ret_cross", [2, DV])
        bst = tile(scr, "ret_bn", [SC, 6])
        mv = tile(scr, "ret_mean_var", [SC, 2])
        ve = tile(scr, "ret_var_eps", [SC])
        rsd = tile(scr, "ret_std", [SC])
        rrs = tile(scr, "ret_rstd", [SC])
        scr.close()
        sca = ExitStack()
        acos = tile(sca, "att_cos", [S])
        asin = tile(sca, "att_sin", [S])
        kk = tile(sca, "keys_hi_twice", [2, KV, S], FR)
        kl = tile(sca, "keys_lo", [2, S], FR)
        Vh = tile(sca, "values_hi", [SC, 2 * KV * DH], FR)
        Vl = tile(sca, "values_lo", [SC, 2 * KV * DH], FR)
        kch = tile(sca, "cmp_keys_hi", [KV, NCMP], FR)
        kcl = tile(sca, "cmp_keys_lo", [KV, NCMP], FR)
        vch = tile(sca, "cmp_values_hi", [KV, DH], FR)
        vcl = tile(sca, "cmp_values_lo", [KV, DH], FR)
        gates = tile(sca, "gates", [SC, 48])
        qhi = tile(sca, "q_hi", [S], FR)
        qlo = tile(sca, "q_lo", [S], FR)
        maskr = tile(sca, "masks_r", [2 * P + SC * NCMP], FR)
        identr = tile(sca, "ident_r", [P], FR)
        scf = ExitStack()
        maskf = tile(scf, "masks_f32", [2 * P + SC * NCMP + 1])
        fraw = tile(scf, "kv_raw", [2, S])
        fswp = tile(scf, "kv_swapped", [S])
        kcs = tile(scf, "cmp_in_k", [KV, S + 16])
        vcs = tile(scf, "cmp_in_v", [KV, S + 16])
        w1 = tile(scf, "cmp_w1", [2, 16, P])
        w2k = tile(scf, "cmp_w2_k_twice", [P])
        w2v = tile(scf, "cmp_w2_v", [DH])
        pos = tile(scf, "cmp_pos", [2, 16])
        hb = tile(scf, "cmp_bias", [2])
        hid = fswp[:, 0:2 * P].rearrange("p (t n) -> p t n", t=2)
        scf.close()
        raw = tile(sca, "q_raw", [S])
        swp = qlo[:].bitcast(F32)
        qst = tile(sca, "q_hi_over_lo", [2, 2, S], FR)
        Ps = tile(sca, "probs_sel", [2, S])
        Pw = tile(sca, "probs_win_cmp", [2, 6 * P])
        PTh = tile(sca, "probs_T_hi", [3, HALF], FR)
        PTl = tile(sca, "probs_T_lo", [3, HALF], FR)
        fm = tile(sca, "merge_half", [HALF])
        yT = tile(sca, "att_y_T", [S])
        yn = tile(sca, "att_y", [2, P])
        og = tile(sca, "att_gated", [3, DH])
        mx = tile(sca, "row_max", [2, 3])
        nm = tile(sca, "neg_max", [2, 3])
        ls = tile(sca, "row_sum", [2, 3])
        lm = tile(sca, "row_sum_held", [2, 3])
        li = tile(sca, "row_sum_inv", [2, 3])
        rg = tile(sca, "row_weight", [2, 3])
        sca.close()
        scm = ExitStack()
        x2 = tile(scm, "x_mid", [SC, D])
        ring2 = tile(scm, "loaded_rows", [2, S])
        mt = tile(scm, "merge_gate", [2, S])
        scm1 = ExitStack()
        YH = tile(scm1, "mix_hi", [KC, S], FR)
        YL = tile(scm1, "mix_lo", [KC, S], FR)
        tmp = tile(scm1, "branch_gated", [S])
        scm1.close()
        xn2 = tile(scm, "x_mid_normed", [2, D])
        sg = tile(scm, "silu_gate", [S])
        ff = tile(scm, "ffn_hidden", [S])
        FH = tile(scm, "ffn_hidden_hi", [2, S], FR)
        FL = tile(scm, "ffn_hidden_lo", [2, S], FR)
        acc = tile(scm, "ffn_out", [SC, D])
        gc = tile(scm, "g_post_ffn", [D])
        scm.close()

        x_loaded = [sem(f"x_loaded{i}") for i in range(SC)]
        consts_loaded = sem("consts_loaded")
        ret_consts_loaded = sem("ret_consts_loaded")
        att_consts_loaded = sem("att_consts_loaded")
        block_loaded = [sem("block_loaded0"), sem("block_loaded1")]
        block_hi = sem("block_hi")
        block_split = sem("block_split")
        blocks_multiplied = sem("blocks_multiplied")
        zero_set = sem("zero_set")
        act_passed = sem("act_passed")
        dve_passed = sem("dve_passed")

        block = ctx.enter_context(nc.Block())

        def matmul3(out, wh_, wl_, xh_, xl_, first, last):
            nc.tensor.matmul(out, wh_, xh_, start=first, stop=False)
            nc.tensor.matmul(out, wh_, xl_, start=False, stop=False)
            return nc.tensor.matmul(out, wl_, xh_, start=False, stop=last)

        def t_job(pe, slot, n, xh, xl, bank, k_ready=None):
            pe.wait_ge(block_split, n)
            for k in range(KC):
                if k_ready is not None:
                    pe.wait_ge(k_ready, k + 1)
                w_h, w_l = wh[:, slot, k * P:(k + 1) * P], wl[:, slot, k * P:(k + 1) * P]
                for w, x in ((w_h, xh), (w_h, xl), (w_l, xh)):
                    for half in range(2):
                        mm = nc.tensor.matmul(ps[:, bank + half, :], w, x[:, k, half * HALF:(half + 1) * HALF],
                                              start=(k == 0 and w is w_h and x is xh),
                                              stop=(k == KC - 1 and w is w_l))
            mm.then_inc(blocks_multiplied, 1)

        s1_sq, s1_ms, s1_rms, s1_rstd = sem("s1_sq"), sem("s1_ms"), sem("s1_rms"), sem("s1_rstd")
        s1_xn, s1_tr, s1_hi, s1_lo = sem("s1_xn"), sem("s1_tr"), sem("s1_hi"), sem("s1_lo")

        def norm_T_act(act, hi, tr, hi_sem):
            for t in range(2 * SC):
                s, g = divmod(t, 2)
                act.wait_ge(tr, t + 1)
                nc.scalar.activation(hi[:, 4 * g:4 * g + 4, s * P:(s + 1) * P],
                                     ps[:, t % 4, :].rearrange("p (k n) -> p k n", k=4), ACT.Copy).then_inc(hi_sem, 1)

        def norm_T_dve(dve, rows, gain, out, r_sem, xn_sem, tr, hi, lo, hi_sem, lo_sem):
            for s in range(SC):
                dve.wait_ge(r_sem, 1)
                if s >= 2:
                    dve.wait_ge(tr, 2 * (s - 1))
                nc.vector.scalar_tensor_tensor(out=out[:, s % 2, :], in0=rows[:, s, :], scalar=rstd[:, s:s + 1],
                                               in1=gain[:], op0=ALU.mult, op1=ALU.mult).then_inc(xn_sem, 1)
                if s >= 1:
                    norm_lo(dve, s - 1, hi, lo, hi_sem, lo_sem)
            norm_lo(dve, SC - 1, hi, lo, hi_sem, lo_sem)

        def norm_lo(dve, s, hi, lo, hi_sem, lo_sem):
            for g in range(2):
                t = 2 * s + g
                dve.wait_ge(hi_sem, t + 1)
                at = (slice(None), slice(4 * g, 4 * g + 4), slice(s * P, (s + 1) * P))
                nc.vector.tensor_tensor(lo[at], ps[:, t % 4, :].rearrange("p (k n) -> p k n", k=4),
                                        hi[at].bitcast(F32), ALU.subtract).then_inc(lo_sem, 1)

        def norm_T_pe(pe, rows, xn_sem, tr, lo_sem):
            for t in range(2 * SC):
                s, g = divmod(t, 2)
                pe.wait_ge(xn_sem, s + 1)
                if t >= 4:
                    pe.wait_ge(lo_sem, t - 3)
                for k in range(4):
                    mm = nc.tensor.transpose(ps[:, t % 4, k * P:(k + 1) * P],
                                             rows[:, s % 2, (4 * g + k) * P:(4 * g + k + 1) * P], ident[:])
                mm.then_inc(tr, 1)

        def mean_sq_dve(dve, sq_sem, ms_sem, rms_sem, rstd_sem):
            dve.wait_ge(sq_sem, SC)
            nc.vector.tensor_scalar(ms[:], ss[:], 1.0 / D, EPS, ALU.mult, ALU.add).then_inc(ms_sem, 1)
            dve.wait_ge(rms_sem, 1)
            nc.vector.reciprocal(rstd[:], rms[:]).then_inc(rstd_sem, 1)

        def squares_act(act, rows, junk, sq_sem, ready, junk_free=None):
            for s in range(SC):
                ready(s)
                if s >= 1:
                    act.wait_ge(sq_sem, s)
                nc.scalar.activation(junk, rows[:, s, :], ACT.Square, accum_out=ss[:, s:s + 1]).then_inc(sq_sem, 1)

        def s1_act(act):
            squares_act(act, xs, xn[:, 0, :], s1_sq, lambda s: act.wait_ge(x_loaded[s], 16))
            act.wait_ge(s1_ms, 1)
            nc.scalar.activation(rms[:], ms[:], ACT.Sqrt).then_inc(s1_rms, 1)
            norm_T_act(act, XH, s1_tr, s1_hi)

        def s1_dve(dve):
            mean_sq_dve(dve, s1_sq, s1_ms, s1_rms, s1_rstd)
            dve.wait_ge(consts_loaded, 32)
            norm_T_dve(dve, xs, g0, xn, s1_rstd, s1_xn, s1_tr, XH, XL, s1_hi, s1_lo)

        def s1_pe(pe):
            pe.wait_ge(consts_loaded, 32)
            norm_T_pe(pe, xn, s1_xn, s1_tr, s1_lo)

        r_v_acc, r_v_hi, r_v_lo = sem("r_v_acc"), sem("r_v_hi"), sem("r_v_lo")
        r_raw, r_swp, r_rope = sem("r_raw"), sem("r_swp"), sem("r_rope")
        r_rh, r_rl, r_silu = sem("r_rope_hi"), sem("r_rope_lo"), sem("r_silu")
        r_hc = sem("r_decays_loaded")
        r_kt, r_kn_hi, r_kn_lo = sem("r_kt"), sem("r_kn_hi"), sem("r_kn_lo")
        r_inner, r_u, r_o = sem("r_inner"), sem("r_u"), sem("r_o")
        r_im, r_im_hi, r_im_lo = sem("r_im"), sem("r_im_hi"), sem("r_im_lo")
        r_R, r_R_hi, r_R_lo = sem("r_R"), sem("r_R_hi"), sem("r_R_lo")
        r_t2, r_oacc = sem("r_t2"), sem("r_oacc")
        r_bn, r_mv, r_ve, r_std, r_rs = sem("r_bn"), sem("r_mv"), sem("r_ve"), sem("r_std"), sem("r_rs")
        r_xn, r_yt, r_y, r_y_stored = sem("r_xn"), sem("r_yt"), sem("r_y"), sem("r_y_stored")
        decT, dk, dq, dc = hc[:, 0:P], hc[:, P:P + 1], hc[:, P + 1:P + 2], hc[:, P + 2:P + 3]

        def ret_pe(pe):
            pe.wait_ge(s1_lo, 2 * SC)
            with pe.Fori(0, RH) as h:
                pe.wait_ge(r_y, h * 4 + 4)
                for j in range(2):
                    pe.wait_ge(block_split, h * B_RET + (j + 1))
                    for k4 in range(4):
                        k = 4 * j + k4
                        for s in range(SC):
                            xh_, xl_ = XH[:, k, s * P:(s + 1) * P], XL[:, k, s * P:(s + 1) * P]
                            mm = matmul3(ps[:, s, 0:DV], xh_, xl_, wh[:, j, k4 * DV:(k4 + 1) * DV],
                                         wl[:, j, k4 * DV:(k4 + 1) * DV], k == 0, k == KC - 1)
                            if k == KC - 1 and s < SC - 1:
                                mm.then_inc(r_v_acc, 1)
                    mm.then_inc(blocks_multiplied, 1)
                for j in range(4):
                    pe.wait_ge(r_v_lo, h * 8 + 2 * (j + 1))
                    t_job(pe, j % 2, h * B_RET + (3 + j), XH, XL, 2 * j)
                pe.wait_ge(r_rope, h * 6 + 6)
                pe.wait_ge(r_raw, h * 2 + 1)
                for g in range(2):
                    for c in range(4):
                        mm = nc.tensor.transpose(ps[:, g, c * P:(c + 1) * P],
                                                 rraw[:, 1, (4 * g + c) * P:(4 * g + c + 1) * P], ident[:])
                    mm.then_inc(r_kt, 1)

                def inner_and_update(c):
                    at = slice(c * P, (c + 1) * P)
                    if c >= 2:
                        pe.wait_ge(r_im, h * 8 + (c - 1))
                    matmul3(ps[:, 2 + c % 2, 0:P], rkh[:, at], rkl[:, at], rqh[:, at], rql[:, at],
                            True, True).then_inc(r_inner, 1)
                    if c < SC - 1:
                        pe.wait_ge(r_kn_lo, h * 2 + (c // 4 + 1))
                        if c >= 2:
                            pe.wait_ge(r_R, h * 7 + (c - 1))
                        matmul3(ps[:, 4 + c % 2, 0:DV], knh[:, c, :], knl[:, c, :], vh[:, c, :], vl[:, c, :],
                                True, True).then_inc(r_u, 1)

                pe.wait_ge(r_rl, h * 2 + 2)
                pe.wait_ge(r_silu, h * 2 + 2)
                inner_and_update(0)
                for c in range(SC):
                    if c + 1 < SC:
                        inner_and_update(c + 1)
                    at = slice(c * P, (c + 1) * P)
                    if c >= 2:
                        pe.wait_ge(r_oacc, h * 8 + (c - 1))
                    if c >= 1:
                        pe.wait_ge(r_R_lo, h * 7 + c)
                        matmul3(ps[:, 6 + c % 2, DV:2 * DV], rqh[:, at], rql[:, at], Rh[:, (c - 1) % 2, :],
                                Rl[:, (c - 1) % 2, :], True, True)
                    pe.wait_ge(r_im_lo, h * 8 + (c + 1))
                    matmul3(ps[:, 6 + c % 2, 0:DV], imh[:, c % 2, :], iml[:, c % 2, :], vh[:, c, :], vl[:, c, :],
                            True, True).then_inc(r_o, 1)
                pe.wait_ge(r_im, h * 8 + 8)
                for e in range(2):
                    for q in range(2):
                        pe.wait_ge(r_xn, h * 8 + 4 * (q + 1))
                        for c in range(4):
                            mm = nc.tensor.transpose(ps[:, 2 * e + q, c * P:(c + 1) * P],
                                                     ro[:, 4 * q + c, e * P:(e + 1) * P], ident[:])
                        mm.then_inc(r_yt, 1)

        def ret_act(act):
            act.wait_ge(s1_lo, 2 * SC)
            act.dma_start(rcos[:], rope_r_d[0]).then_inc(ret_consts_loaded, 16)
            act.dma_start(rsin[:], rope_r_d[1]).then_inc(ret_consts_loaded, 16)
            with act.Fori(0, RH) as h:
                act.dma_start(hc[:], ret_d[bass.ds(h, 1)].rearrange("a p n -> p (a n)")).then_inc(r_hc, 16)
                for s in range(SC):
                    if s < SC - 1:
                        act.wait_ge(r_v_acc, h * 7 + (s + 1))
                    else:
                        act.wait_ge(blocks_multiplied, h * B_RET + 2)
                    nc.scalar.activation(vh[:, s, :], ps[:, s, 0:DV], ACT.Copy).then_inc(r_v_hi, 1)
                for j in range(2):
                    act.wait_ge(blocks_multiplied, h * B_RET + (3 + j))
                    nc.scalar.activation(rraw[:, j, :], ps[:, 2 * j:2 * j + 2, :].rearrange("p a n -> p (a n)"),
                                         ACT.Copy, scale=RET_SCALE if j == 0 else 1.0).then_inc(r_raw, 1)
                    act.wait_ge(r_raw, h * 2 + (j + 1))
                    if j == 1:
                        act.wait_ge(r_rope, h * 6 + 3)
                    for a in range(2):
                        act.dma_start(rswp[64 * a:64 * a + 64, :], rraw[64 - 64 * a:128 - 64 * a, j, :])\
                            .then_inc(r_swp, 16)
                    if j == 1:
                        nc.scalar.activation(rqh[:], rraw[:, 0, :], ACT.Copy).then_inc(r_rh, 1)
                for j in range(2):
                    act.wait_ge(blocks_multiplied, h * B_RET + (5 + j))
                    nc.scalar.activation(silu_g[:, j, :], ps[:, 4 + 2 * j:6 + 2 * j, :].rearrange("p a n -> p (a n)"),
                                         ACT.Silu).then_inc(r_silu, 1)
                    if j == 0:
                        act.wait_ge(r_rope, h * 6 + 6)
                        nc.scalar.activation(rkh[:], rraw[:, 1, :], ACT.Copy).then_inc(r_rh, 1)
                act.wait_ge(r_hc, h * 16 + 16)
                for g in range(2):
                    act.wait_ge(r_kt, h * 2 + (g + 1))
                    nc.scalar.activation(knh[:, 4 * g:4 * g + 4, :], ps[:, g, :].rearrange("p (c n) -> p c n", c=4),
                                         ACT.Copy, scale=dk).then_inc(r_kn_hi, 1)
                for c in range(SC):
                    act.wait_ge(r_im, h * 8 + (c + 1))
                    if c >= 2:
                        act.wait_ge(r_o, h * 8 + (c - 1))
                    nc.scalar.activation(imh[:, c % 2, :], im[:, c % 2, :], ACT.Copy).then_inc(r_im_hi, 1)
                    if c < SC - 1:
                        act.wait_ge(r_R, h * 7 + (c + 1))
                        if c >= 2:
                            act.wait_ge(r_o, h * 8 + c)
                        nc.scalar.activation(Rh[:, c % 2, :], R[:], ACT.Copy).then_inc(r_R_hi, 1)
                    if c >= 1:
                        act.wait_ge(r_o, h * 8 + (c + 1))
                        if c >= 3:
                            act.wait_ge(r_oacc, h * 8 + (c - 1))
                        nc.scalar.activation(t2[:, c % 2, :], ps[:, 6 + c % 2, DV:2 * DV], ACT.Copy, scale=dq)\
                            .then_inc(r_t2, 1)
                act.wait_ge(r_ve, h + 1)
                nc.scalar.activation(rsd[:], ve[:], ACT.Sqrt).then_inc(r_std, 1)
                act.wait_ge(r_y, h * 4 + 8)
                act.dma_start(yr_d[bass.ds(h * 2, 2)].rearrange("a p n -> p a n"), ry[:]).then_inc(r_y_stored, 16)

        def ret_dve(dve):
            nc.vector.sem_inc(r_y, 4)
            nc.vector.sem_inc(r_y_stored, 16)
            dve.wait_ge(ret_consts_loaded, 32)
            with dve.Fori(0, RH) as h:
                for s in range(SC):
                    dve.wait_ge(r_v_hi, h * 8 + (s + 1))
                    nc.vector.tensor_tensor(vl[:, s, :], ps[:, s, 0:DV], vh[:, s, :].bitcast(F32), ALU.subtract)\
                        .then_inc(r_v_lo, 1)
                for j in range(2):
                    dve.wait_ge(r_swp, h * 64 + 32 * (j + 1))
                    nc.vector.tensor_tensor(rraw[:, j, :], rraw[:, j, :], rcos[:], ALU.mult).then_inc(r_rope, 1)
                    nc.vector.tensor_tensor(rswp[:], rswp[:], rsin[:], ALU.mult).then_inc(r_rope, 1)
                    dve.wait_ge(r_rope, h * 6 + (3 * j + 2))
                    nc.vector.tensor_tensor(rraw[:, j, :], rraw[:, j, :], rswp[:], ALU.add).then_inc(r_rope, 1)
                for j, (hi, lo) in enumerate(((rqh, rql), (rkh, rkl))):
                    dve.wait_ge(r_rh, h * 2 + (j + 1))
                    nc.vector.tensor_tensor(lo[:], rraw[:, j, :], hi[:].bitcast(F32), ALU.subtract).then_inc(r_rl, 1)
                dve.wait_ge(r_hc, h * 16 + 16)
                for g in range(2):
                    dve.wait_ge(r_kn_hi, h * 2 + (g + 1))
                    nc.vector.scalar_tensor_tensor(
                        out=knl[:, 4 * g:4 * g + 4, :].rearrange("p c n -> p (c n)"), in0=ps[:, g, :], scalar=dk,
                        in1=knh[:, 4 * g:4 * g + 4, :].rearrange("p c n -> p (c n)").bitcast(F32),
                        op0=ALU.mult, op1=ALU.subtract).then_inc(r_kn_lo, 1)
                for c in range(SC):
                    dve.wait_ge(r_inner, h * 8 + (c + 1))
                    nc.vector.tensor_tensor(im[:, c % 2, :], ps[:, 2 + c % 2, 0:P], decT, ALU.mult).then_inc(r_im, 1)
                    if c < SC - 1:
                        dve.wait_ge(r_u, h * 7 + (c + 1))
                        if c == 0:
                            nc.vector.tensor_copy(R[:], ps[:, 4, 0:DV]).then_inc(r_R, 1)
                        else:
                            nc.vector.scalar_tensor_tensor(out=R[:], in0=R[:], scalar=dc, in1=ps[:, 4 + c % 2, 0:DV],
                                                           op0=ALU.mult, op1=ALU.add).then_inc(r_R, 1)
                    dve.wait_ge(r_im_hi, h * 8 + (c + 1))
                    nc.vector.tensor_tensor(iml[:, c % 2, :], im[:, c % 2, :], imh[:, c % 2, :].bitcast(F32),
                                            ALU.subtract).then_inc(r_im_lo, 1)
                    if c < SC - 1:
                        dve.wait_ge(r_R_hi, h * 7 + (c + 1))
                        nc.vector.tensor_tensor(Rl[:, c % 2, :], R[:], Rh[:, c % 2, :].bitcast(F32),
                                                ALU.subtract).then_inc(r_R_lo, 1)
                    if c == 0:
                        dve.wait_ge(r_o, h * 8 + 1)
                        nc.vector.tensor_copy(ro[:, 0, :], ps[:, 6, 0:DV]).then_inc(r_oacc, 1)
                    else:
                        dve.wait_ge(r_t2, h * 7 + c)
                        nc.vector.tensor_tensor(ro[:, c, :], ps[:, 6 + c % 2, 0:DV], t2[:, c % 2, :], ALU.add)\
                            .then_inc(r_oacc, 1)
                    if c >= 1:
                        dve.wait_ge(r_oacc, h * 8 + c)
                        nc.vector.bn_stats(bst[:, c - 1, :], ro[:, c - 1, :]).then_inc(r_bn, 1)
                dve.wait_ge(r_oacc, h * 8 + 8)
                nc.vector.bn_stats(bst[:, 7, :], ro[:, 7, :]).then_inc(r_bn, 1)
                dve.wait_ge(r_bn, h * 8 + 8)
                nc.vector.sem_inc(dve_passed, 1)
                for c in range(SC):
                    nc.vector.bn_aggr(mv[:, c, :], bst[:, c, :]).then_inc(r_mv, 1)
                dve.wait_ge(r_mv, h * 8 + 8)
                nc.vector.tensor_scalar(ve[:], mv[:, :, 1], EPS, None, ALU.add).then_inc(r_ve, 1)
                dve.wait_ge(r_std, h + 1)
                nc.vector.reciprocal(rrs[:], rsd[:]).then_inc(r_rs, 1)
                dve.wait_ge(r_rs, h + 1)
                for c in range(SC):
                    nc.vector.tensor_scalar(ro[:, c, :], ro[:, c, :], mv[:, c, 0:1], rrs[:, c:c + 1],
                                            ALU.subtract, ALU.mult).then_inc(r_xn, 1)
                dve.wait_ge(r_y_stored, h * 16 + 16)
                for e in range(2):
                    for q in range(2):
                        dve.wait_ge(r_yt, h * 4 + (2 * e + q + 1))
                        at = slice(q * HALF, (q + 1) * HALF)
                        nc.vector.tensor_tensor(ry[:, e, at], ps[:, 2 * e + q, :], silu_g[:, e, at], ALU.mult)\
                            .then_inc(r_y, 1)

        a_raw, a_swp, a_rope = sem("a_raw"), sem("a_swapped"), sem("a_rope")
        a_vcs, a_kcs, a_kk = sem("a_cmp_v_in"), sem("a_cmp_k_in"), sem("a_keys_placed")
        a_pad, a_mask = sem("a_pad"), sem("a_mask")
        a_hi, a_lo, a_vh, a_vl = sem("a_key_hi"), sem("a_key_lo"), sem("a_value_hi"), sem("a_value_lo")
        a_gate, a_gv = sem("a_gate"), sem("a_gate_valid")
        a_mlp, a_hb, a_hid = sem("a_mlp"), sem("a_mlp_bias"), sem("a_hidden")
        a_cmp, a_chi, a_clo = sem("a_cmp"), sem("a_cmp_hi"), sem("a_cmp_lo")
        CMPM = 2 * P
        VALID = CMPM + SC * NCMP

        def bank_of(s):
            return (s + 4) % 8

        def fixed_pe(pe):
            t_job(pe, 0, B_KV + 1, XH, XL, 4)
            t_job(pe, 1, B_KV + 2, XH, XL, 6)
            pe.wait_ge(r_y, 4 * RH + 4)
            t_job(pe, 0, B_KV + 3, XH, XL, 0)
            t_job(pe, 1, B_KV + 4, XH, XL, 2)
            for j in range(4):
                pe.wait_ge(block_split, B_KV + 5 + j)
                for k2 in range(2):
                    k = 2 * j + k2
                    for s in range(SC):
                        if k == 0 and s % 2 == 0:
                            pe.wait_ge(a_raw, s // 2 + 1)
                        at = slice(k2 * HALF, k2 * HALF + 304)
                        mm = matmul3(ps[:, bank_of(s), 0:304], XH[:, k, s * P:(s + 1) * P], XL[:, k, s * P:(s + 1) * P],
                                     wh[:, j % 2, at], wl[:, j % 2, at], k == 0, k == KC - 1)
                mm.then_inc(blocks_multiplied, 1)
            pe.wait_ge(att_consts_loaded, 7 * 16)
            pe.wait_ge(a_pad, 6)
            pe.wait_ge(a_vl, 1)
            pe.wait_ge(a_gate, 1)
            for t, (src, ready) in enumerate(((kcs, a_kcs), (vcs, a_vcs))):
                pe.wait_ge(ready, 64)
                for jj in range(16):
                    mm = nc.tensor.matmul(ps[:, 4 + t, 0:P].rearrange("p (v n) -> p v n", v=KV), w1[:, t, jj, :],
                                          src[:, :, 2 * jj:2 * jj + 16 * (NCMP - 1) + 1:16],
                                          start=(jj == 0), stop=(jj == 15))
                mm.then_inc(a_mlp, 1)
                for jj in range(16):
                    mm = nc.tensor.matmul(ps[:, 6, t:t + 1], w1[:, t, jj, :], pos[:, t, jj:jj + 1],
                                          start=(jj == 0), stop=(jj == 15))
                mm.then_inc(a_mlp, 1)
            pe.wait_ge(a_hid, 1)
            nc.tensor.matmul(ps[:, 7, 0:P], w2k[:], hid[:, 0, :], start=True, stop=True).then_inc(a_cmp, 1)
            pe.wait_ge(a_hid, 2)
            pe.wait_ge(a_vl, 2)
            pe.wait_ge(a_gate, 2)
            for v in range(KV):
                mm = nc.tensor.matmul(ps[0:NCMP, 0, v * DH:(v + 1) * DH], hid[:, 1, v * NCMP:(v + 1) * NCMP], w2v[:],
                                      start=True, stop=True)
            mm.then_inc(a_cmp, 1)

        def swap32(act, dst, src, done):
            for a in range(4):
                b = a ^ 1
                act.dma_start(dst[32 * a:32 * a + 32], src[32 * b:32 * b + 32]).then_inc(done, 16)

        def place_cmp(act, dst, src, done):
            for v in range(KV):
                act.dma_start(dst[0:64, v, 0:S], src[64 * v:64 * v + 64, :]).then_inc(done, 16)
                act.dma_start(dst[64:128, v, 0:S - 1], src[64 * v:64 * v + 64, 1:S]).then_inc(done, 16)

        def place_keys(act, br):
            for v in range(KV):
                for a in range(2):
                    act.dma_start(kk[64 * a:64 * a + 64, br, v, :].bitcast(F32), qhi[64 * v:64 * v + 64, :].bitcast(F32)).then_inc(a_kk, 16)

        def two_banks(b):
            return ps[:, b:b + 2, :].rearrange("p a n -> p (a n)")

        def fixed_act(act):
            act.wait_ge(r_y_stored, 16 * (RH + 1))
            for dst, src in ((acos[:], rope_a_d[0]), (asin[:], rope_a_d[1]), (maskf[:], mask_d),
                             (w1[:], w1_d), (pos[:], pos_d), (w2k[:], w2k_d), (w2v[:], w2v_d)):
                act.dma_start(dst, src).then_inc(att_consts_loaded, 16)
            act.wait_ge(blocks_multiplied, B_KV + 1)
            nc.scalar.activation(fraw[:, 0, :], two_banks(4), ACT.Copy).then_inc(a_raw, 1)
            act.wait_ge(a_raw, 1)
            swap32(act, fswp, fraw[:, 0, :], a_swp)
            act.wait_ge(blocks_multiplied, B_KV + 2)
            nc.scalar.activation(fraw[:, 1, :], two_banks(6), ACT.Copy).then_inc(a_raw, 1)
            act.wait_ge(a_raw, 2)
            place_cmp(act, vcs, fraw[:, 1, :], a_vcs)
            act.wait_ge(a_rope, 3)
            place_cmp(act, kcs, fraw[:, 0, :], a_kcs)
            act.wait_ge(blocks_multiplied, B_KV + 3)
            act.wait_ge(a_kcs, 64)
            nc.scalar.activation(fraw[:, 0, :], two_banks(0), ACT.Copy).then_inc(a_raw, 1)
            act.wait_ge(a_raw, 3)
            swap32(act, fswp, fraw[:, 0, :], a_swp)
            act.wait_ge(blocks_multiplied, B_KV + 4)
            act.wait_ge(a_vcs, 64)
            nc.scalar.activation(fraw[:, 1, :], two_banks(2), ACT.Copy).then_inc(a_raw, 1)
            act.wait_ge(a_rope, 6)
            nc.scalar.activation(qhi[:], fraw[:, 0, :], ACT.Copy).then_inc(a_hi, 1)
            act.wait_ge(a_raw, 4)
            swap32(act, fswp, fraw[:, 1, :], a_swp)
            act.wait_ge(a_hi, 1)
            act.wait_ge(a_lo, 1)
            place_keys(act, 0)
            act.wait_ge(a_rope, 9)
            act.wait_ge(a_kk, 64)
            nc.scalar.activation(qhi[:], fraw[:, 1, :], ACT.Copy).then_inc(a_hi, 1)
            act.wait_ge(a_hi, 2)
            act.wait_ge(a_lo, 2)
            place_keys(act, 1)
            act.wait_ge(blocks_multiplied, B_KV + 8)
            for g, b in ((0, 4), (1, 0)):
                nc.scalar.activation(Vh[:, 4 * g:4 * g + 4, :], ps[:, b:b + 4, 0:256], ACT.Copy).then_inc(a_vh, 1)
            for g, b in ((0, 4), (1, 0)):
                act.wait_ge(a_vl, g + 1)
                nc.scalar.activation(gates[:, 4 * g:4 * g + 4, :], ps[:, b:b + 4, 256:304], ACT.Sigmoid)\
                    .then_inc(a_gate, 1)
            for t in range(2):
                act.wait_ge(a_mlp, 4)
                nc.scalar.activation(hb[:, t:t + 1], ps[:, 6, t:t + 1], ACT.Copy).then_inc(a_hb, 1)
                act.wait_ge(a_hb, t + 1)
                nc.scalar.activation(hid[:, t, :], ps[:, 4 + t, 0:P], ACT.Gelu_apprx_tanh, bias=hb[:, t:t + 1])\
                    .then_inc(a_hid, 1)
            act.wait_ge(a_cmp, 1)
            nc.scalar.activation(kch[:].rearrange("p v n -> p (v n)"), ps[:, 7, 0:P], ACT.Copy).then_inc(a_chi, 1)
            act.wait_ge(a_cmp, 2)
            nc.scalar.activation(vch[0:NCMP].rearrange("p v n -> p (v n)"), ps[0:NCMP, 0, 0:P], ACT.Copy)\
                .then_inc(a_chi, 1)

        def rope_dve(x, y, count):
            nc.vector.tensor_tensor(x, x, acos[:], ALU.mult).then_inc(a_rope, 1)
            nc.vector.tensor_tensor(y, y, asin[:], ALU.mult).then_inc(a_rope, 1)
            nc.vector.wait_ge(a_rope, count + 2)
            nc.vector.tensor_tensor(x, x, y, ALU.add).then_inc(a_rope, 1)

        def fixed_dve(dve):
            dve.wait_ge(att_consts_loaded, 7 * 16)
            for t in (kcs, vcs):
                nc.vector.memset(t[0:64, :, S:S + 16], 0.0).then_inc(a_pad, 1)
                nc.vector.memset(t[64:128, :, S - 1:S + 16], 0.0).then_inc(a_pad, 1)
            nc.vector.memset(vch[64:128].bitcast(F32), 0.0).then_inc(a_pad, 1)
            nc.vector.memset(vcl[64:128].bitcast(F32), 0.0).then_inc(a_pad, 1)
            nc.vector.tensor_copy(maskr[:], maskf[:, 0:VALID]).then_inc(a_mask, 1)
            nc.vector.tensor_copy(identr[:], ident[:]).then_inc(a_mask, 1)
            dve.wait_ge(a_swp, 64)
            rope_dve(fraw[:, 0, :], fswp[:], 0)
            dve.wait_ge(a_swp, 128)
            rope_dve(fraw[:, 0, :], fswp[:], 3)
            dve.wait_ge(a_hi, 1)
            nc.vector.tensor_tensor(kl[:, 0, :], fraw[:, 0, :], qhi[:].bitcast(F32), ALU.subtract).then_inc(a_lo, 1)
            dve.wait_ge(a_swp, 192)
            rope_dve(fraw[:, 1, :], fswp[:], 6)
            dve.wait_ge(a_hi, 2)
            nc.vector.tensor_tensor(kl[:, 1, :], fraw[:, 1, :], qhi[:].bitcast(F32), ALU.subtract).then_inc(a_lo, 1)
            for g, b in ((0, 4), (1, 0)):
                dve.wait_ge(a_vh, g + 1)
                nc.vector.tensor_tensor(Vl[:, 4 * g:4 * g + 4, :], ps[:, b:b + 4, 0:256],
                                        Vh[:, 4 * g:4 * g + 4, :].bitcast(F32), ALU.subtract).then_inc(a_vl, 1)
            dve.wait_ge(a_gate, 2)
            first = gates[:, 0, :].rearrange("p (m b) -> p m b", b=3)[:, :, 0]
            nc.vector.tensor_scalar(first, first, maskf[:, VALID:VALID + 1], None, ALU.mult).then_inc(a_gv, 1)
            dve.wait_ge(a_chi, 1)
            nc.vector.tensor_tensor(kcl[:].rearrange("p v n -> p (v n)"), ps[:, 7, 0:P],
                                    kch[:].rearrange("p v n -> p (v n)").bitcast(F32), ALU.subtract).then_inc(a_clo, 1)
            dve.wait_ge(a_chi, 2)
            nc.vector.tensor_tensor(vcl[0:NCMP].rearrange("p v n -> p (v n)"), ps[0:NCMP, 0, 0:P],
                                    vch[0:NCMP].rearrange("p v n -> p (v n)").bitcast(F32), ALU.subtract)\
                .then_inc(a_clo, 1)
            nc.vector.memset(Pw[:, :, 5 * P + NCMP:6 * P], 0.0).then_inc(a_pad, 1)

        UNITS = 2 * SC
        GROUPS = [groups_of(u // 2) for u in range(UNITS)]
        GOFF = [sum(len(g) for g in GROUPS[:u]) for u in range(UNITS + 1)]
        NG = GOFF[-1]
        FILL = 3 * 48
        BR = {"cmp": 0, "sel": 1, "win": 2}
        UNIT_OF = [u_ for u_ in range(UNITS) for _ in GROUPS[u_]]
        WIN0 = [len([g_ for g_ in GROUPS[u_] if g_[0][0] == "sel"]) for u_ in range(UNITS)]
        assert NG % 2 == 0
        SHARE = [9 - 1.7 * len(g_) for gs in GROUPS for g_ in gs]
        FILL_TO, FILL_AT = [], []
        for s_ in range(NG):
            last_ = FILL_TO[-1] if s_ else 0
            want_ = int((FILL - 24) * sum(SHARE[:s_ + 1]) / sum(SHARE) + 0.5)
            FILL_TO.append(min(want_, (last_ // 24 + 1) * 24))
            if FILL_TO[-1] % 24 == 0 and FILL_TO[-1] > last_:
                FILL_AT.append(s_)
        assert len(FILL_AT) == 5 and FILL_AT[-1] < NG and FILL_TO[-1] == FILL - 24
        GATED_AT = [GOFF[u_ + 1] + 1 for u_ in range(UNITS)]
        Y_AT = [GOFF[2 * q_ + 2] + 2 for q_ in range(SC)]
        TURNS = []
        for s_ in range(NG):
            TURNS += [("g", s_)] + ([("y", Y_AT.index(s_))] if s_ in Y_AT else [])
        TURNS.append(("y", SC - 1))
        assert len(TURNS) % 2 == 0
        O_BANK, F_BANK, T_BANK = 6, 7, 4

        q_swp, q_steps, q_roped, q_asm = sem("q_swapped"), sem("q_rope_steps"), sem("q_roped"), sem("q_placed")
        fill_half, fill_out, m_stored = sem("fill_half"), sem("fill_out"), sem("merge_logits_stored")
        att_s, att_mx, att_nm, att_exp = sem("att_scores"), sem("att_max"), sem("att_neg_max"), sem("att_exp")
        att_tr, att_hi, att_lo, att_pv = sem("att_turned"), sem("att_pt_hi"), sem("att_pt_lo"), sem("att_pv")
        att_c, att_og, att_y = sem("att_weights"), sem("att_gated_sem"), sem("att_y_rows")
        att_yt, att_yc, y_stored = sem("att_y_turned"), sem("att_y_copied"), sem("y_att_stored")

        def fill_pe(pe, base, done, slot0, m0, m1):
            for m in range(m0, m1):
                blk, half, r = m // 48, m // 24 % 2, m % 24
                k, pas = divmod(r, 3)
                slot = (slot0 + blk) % 2
                if r == 0:
                    if half == 0:
                        pe.wait_ge(block_split, base + (blk + 1))
                    pe.wait_ge(fill_out, done + (2 * blk + half))
                w = (wl if pas == 2 else wh)[:, slot, k * P:(k + 1) * P]
                x = (XL if pas == 1 else XH)[:, k, half * HALF:(half + 1) * HALF]
                mm = nc.tensor.matmul(ps[:, F_BANK, :], w, x, start=(r == 0), stop=(r == 23))
                if r == 23:
                    mm.then_inc(blocks_multiplied if half else fill_half, 1)

        def scores_pe(pe, n, kv0, u, part):
            kv, (qi, h) = (kv0 + u // UNITS) % KV, divmod(u % UNITS, 2)
            q2 = qst[:, kv, h, qi * P:(qi + 1) * P]
            own = slice(64 * kv, 64 * kv + 64)
            q1 = qst[own, kv, h, qi * P:(qi + 1) * P]

            def block(out, k_hi, k_lo, masks):
                nc.tensor.matmul(out, q2, k_hi, start=True, stop=False)
                for col, w, m in masks:
                    nc.tensor.matmul(out[:, col:col + w], identr[:], m, start=False, stop=False)
                return nc.tensor.matmul(out, q1, k_lo, start=False, stop=True)

            diag, edge = maskr[:, 0:P], maskr[:, P:2 * P]
            if u >= 1:
                pe.wait_ge(att_exp, n * 48 + (3 * u - 2 if part == 0 else 3 * u))
            if part == 0:
                for g in range(qi // 4 + 1):
                    a, b = g * HALF, min((g + 1) * HALF, (qi + 1) * P)
                    mm = block(ps[:, g, 0:b - a], kk[:, 0, kv, a:b], kl[own, 0, a:b],
                               [(qi % 4 * P, P, diag)] if g == qi // 4 else [])
                mm.then_inc(att_s, 1)
                return
            lo = max(0, qi - 4)
            nb = qi - lo + 1
            for g in range((nb + 3) // 4):
                a, b = (lo + 4 * g) * P, (lo + min(nb, 4 * g + 4)) * P
                masks = [(0, P, edge)] if qi >= 4 and g == 0 else []
                if g == (nb - 1) // 4:
                    masks.append(((nb - 1) % 4 * P, P, diag))
                block(ps[:, 2 + g, 0:b - a], kk[:, 1, kv, a:b], kl[own, 1, a:b], masks)
            block(ps[:, 3, P:P + NCMP], kch[:, kv, :], kcl[own, kv, :],
                  [(0, NCMP, maskr[:, CMPM + qi * NCMP:CMPM + (qi + 1) * NCMP])]).then_inc(att_s, 1)

        def bank_free(pe, n, turn):
            if turn >= 2:
                kind, i = TURNS[turn - 2]
                pe.wait_ge(att_lo if kind == "g" else att_yc, n * (NG if kind == "g" else SC) + (i + 1))

        def turn_pe(pe, n, s):
            u = UNIT_OF[s]
            group = GROUPS[u][s - GOFF[u]]
            turn = TURNS.index(("g", s))
            pe.wait_ge(att_exp, n * 48 + (3 * u + (1 if group[0][0] == "sel" else 3)))
            bank_free(pe, n, turn)
            for j, (kind, _, col) in enumerate(group):
                probs = Ps if kind == "sel" else Pw
                mm = nc.tensor.transpose(ps[:, T_BANK + turn % 2, j * P:(j + 1) * P],
                                         probs[:, u % 2, col:col + P], ident[:])
            mm.then_inc(att_tr, 1)

        def pv_pe(pe, n, kv, s):
            u = UNIT_OF[s]
            qi, h = divmod(u, 2)
            if s == GOFF[u] and u >= 1:
                pe.wait_ge(att_og, n * UNITS + u)
            pe.wait_ge(att_lo, n * NG + (s + 1))
            last_kb = {"sel": qi, "win": qi, "cmp": None}
            for j, (kind, kb, _) in enumerate(GROUPS[u][s - GOFF[u]]):
                first = kind == "cmp" or kb == (0 if kind == "sel" else max(0, qi - 4))
                out = ps[:, O_BANK, (h * 3 + BR[kind]) * DH:(h * 3 + BR[kind] + 1) * DH]
                if kind == "cmp":
                    v_h, v_l = vch[:, kv, :], vcl[:, kv, :]
                else:
                    at = slice((BR[kind] - 1) * P + kv * DH, (BR[kind] - 1) * P + (kv + 1) * DH)
                    v_h, v_l = Vh[:, kb, at], Vl[:, kb, at]
                mm = matmul3(out, PTh[:, s % 3, j * P:(j + 1) * P], PTl[:, s % 3, j * P:(j + 1) * P], v_h, v_l,
                             first, kb == last_kb[kind])
            mm.then_inc(att_pv, 1)

        def y_pe(pe, n, qi):
            turn = TURNS.index(("y", qi))
            pe.wait_ge(att_y, n * UNITS + (2 * qi + 2))
            bank_free(pe, n, turn)
            nc.tensor.transpose(ps[:, T_BANK + turn % 2, 0:P], yn[:, qi % 2, :], ident[:]).then_inc(att_yt, 1)

        def att_pe(pe):
            fixed_pe(pe)
            pe.wait_ge(a_clo, 2)
            pe.wait_ge(block_split, B_Q0 + 1)
            for half in range(2):
                for k in range(KC):
                    if half == 1 and k == 0:
                        pe.wait_ge(fill_out, 1)
                    w_h, w_l = wh[:, 0, k * P:(k + 1) * P], wl[:, 0, k * P:(k + 1) * P]
                    at = slice(half * HALF, (half + 1) * HALF)
                    mm = matmul3(ps[:, F_BANK, :], w_h, w_l, XH[:, k, at], XL[:, k, at], k == 0, k == KC - 1)
                mm.then_inc(blocks_multiplied if half else fill_half, 1)
            pe.wait_ge(a_mask, 2)
            pe.wait_ge(a_kk, 128)
            pe.wait_ge(a_lo, 2)
            pe.wait_ge(a_pad, 7)
            pe.wait_ge(q_asm, 64)
            for part in range(2):
                scores_pe(pe, 0, 0, 0, part)
            with pe.Fori(0, PAIRS // 2) as i:
                for kv in range(KV):
                    n = i * 2 + kv

                    def fill(m0, m1):
                        fill_pe(pe, n * 3 + B_PAIR, n * 6 + 2, (B_PAIR + 3 * kv) % 2, m0, m1)

                    for s in range(NG):
                        u = UNIT_OF[s]
                        g = s - GOFF[u]
                        turn_pe(pe, n, s)
                        if g == 0:
                            if u == UNITS - 1:
                                pe.wait_ge(q_asm, n * 64 + 128)
                            scores_pe(pe, n, kv, u + 1, 0)
                        if g == WIN0[u]:
                            scores_pe(pe, n, kv, u + 1, 1)
                        if s >= 2:
                            pv_pe(pe, n, kv, s - 2)
                        fill(FILL_TO[s - 1] if s else 0, FILL_TO[s])
                        if s in Y_AT:
                            y_pe(pe, n, Y_AT.index(s))
                    pv_pe(pe, n, kv, NG - 2)
                    fill(FILL - 24, FILL - 12)
                    pv_pe(pe, n, kv, NG - 1)
                    fill(FILL - 12, FILL)
                    y_pe(pe, n, SC - 1)
                    pe.wait_ge(att_yc, n * SC + SC)

        def fill_act(act, n, j):
            blk, half = divmod(j, 2)
            at = slice(half * HALF, (half + 1) * HALF)
            if half == 0:
                act.wait_ge(fill_half, n * 3 + (blk + 2))
            else:
                act.wait_ge(blocks_multiplied, n * 3 + (B_PAIR + blk + 1))
            if blk == 0:
                nc.scalar.activation(raw[:, at], ps[:, F_BANK, :], ACT.Copy).then_inc(fill_out, 1)
                if half == 1:
                    act.wait_ge(fill_out, n * 6 + 4)
                    act.wait_ge(q_asm, n * 64 + 64)
                    swap32(act, swp, raw, q_swp)
            else:
                act.wait_ge(m_stored, n * 64 + 16 * (2 * (blk - 1) + half + 1))
                nc.scalar.activation(fm[:], ps[:, F_BANK, :], ACT.Copy).then_inc(fill_out, 1)
                act.wait_ge(fill_out, n * 6 + (2 * blk + half + 3))
                act.dma_start(ml_d[bass.ds(n + (KC if blk == 2 else 0), 1), :, at].rearrange("a p n -> p (a n)"),
                              fm[:]).then_inc(m_stored, 16)

        def exp_act(act, n, u, part):
            qi = u % UNITS // 2

            def exp(kind, out, src):
                b = BR[kind]
                nc.scalar.activation(out, src, ACT.Exp, bias=nm[:, u % 2, b:b + 1], scale=ATT_SCALE,
                                     accum_out=ls[:, u % 2, b:b + 1]).then_inc(att_exp, 1)

            if part == 0:
                act.wait_ge(att_nm, n * 32 + (2 * u + 1))
                exp("sel", Ps[:, u % 2, 0:(qi + 1) * P], two_banks(0)[:, 0:(qi + 1) * P])
            else:
                act.wait_ge(att_nm, n * 32 + (2 * u + 2))
                w = (min(qi, 4) + 1) * P
                exp("win", Pw[:, u % 2, 0:w], two_banks(2)[:, 0:w])
                exp("cmp", Pw[:, u % 2, 5 * P:5 * P + NCMP], ps[:, 3, P:P + NCMP])

        def hi_act(act, n, s):
            u = UNIT_OF[s]
            w = len(GROUPS[u][s - GOFF[u]]) * P
            act.wait_ge(att_tr, n * NG + (s + 1))
            if s >= 3:
                act.wait_ge(att_pv, n * NG + (s - 2))
            nc.scalar.activation(PTh[:, s % 3, 0:w], ps[:, T_BANK + TURNS.index(("g", s)) % 2, 0:w], ACT.Copy).then_inc(att_hi, 1)

        def y_act(act, n, qi):
            act.wait_ge(att_yt, n * SC + (qi + 1))
            if qi == 0:
                act.wait_ge(y_stored, n * 16 + 16)
            nc.scalar.activation(yT[:, qi * P:(qi + 1) * P], ps[:, T_BANK + TURNS.index(("y", qi)) % 2, 0:P], ACT.Copy)\
                .then_inc(att_yc, 1)

        def place_q(act, turn):
            for h in range(2):
                for a, part in ((64 * turn, qhi), (64 - 64 * turn, qlo)):
                    act.dma_start(qst[a:a + 64, turn, h, :].bitcast(F32),
                                  part[64 * h:64 * h + 64, :].bitcast(F32)).then_inc(q_asm, 16)

        def att_act(act):
            fixed_act(act)
            nc.scalar.sem_inc(m_stored, 16)
            nc.scalar.sem_inc(y_stored, 16)
            act.wait_ge(a_pad, 7)
            for half in range(2):
                if half == 0:
                    act.wait_ge(fill_half, 1)
                else:
                    act.wait_ge(blocks_multiplied, B_Q0 + 1)
                nc.scalar.activation(raw[:, half * HALF:(half + 1) * HALF], ps[:, F_BANK, :], ACT.Copy)\
                    .then_inc(fill_out, 1)
            act.wait_ge(fill_out, 2)
            swap32(act, swp, raw, q_swp)
            act.wait_ge(q_roped, 1)
            place_q(act, 0)
            for part in range(2):
                exp_act(act, 0, 0, part)
            with act.Fori(0, PAIRS // 2) as i:
                for kv in range(KV):
                    n = i * 2 + kv
                    for s in range(NG):
                        u = UNIT_OF[s]
                        g = s - GOFF[u]
                        if s - 1 in FILL_AT:
                            fill_act(act, n, FILL_AT.index(s - 1))
                        if s - 1 in Y_AT:
                            y_act(act, n, Y_AT.index(s - 1))
                        hi_act(act, n, s)
                        if g == 0 and u >= 1 and len(GROUPS[u - 1]) - 1 == WIN0[u - 1]:
                            exp_act(act, n, u, 1)
                        if g == 1:
                            exp_act(act, n, u + 1, 0)
                        if g > WIN0[u] and g == len(GROUPS[u]) - 1:
                            exp_act(act, n, u + 1, 1)
                        if s == GOFF[UNITS - 4]:
                            act.wait_ge(q_roped, n + 2)
                            place_q(act, 1 - kv)
                    if FILL_AT[-1] == NG - 1:
                        fill_act(act, n, 4)
                    fill_act(act, n, 5)
                    y_act(act, n, SC - 1)
                    act.wait_ge(att_yc, n * SC + SC)
                    act.dma_start(ya_d[bass.ds(n, 1)].rearrange("a p n -> p (a n)"), yT[:]).then_inc(y_stored, 16)

        def max_dve(dve, n, u, part):
            qi = u % UNITS // 2
            p = u % 2
            if part == 0:
                dve.wait_ge(att_s, n * 32 + (2 * u + 1))
                nc.vector.reduce_max(mx[:, p, 1:2], two_banks(0)[:, 0:(qi + 1) * P], AX.X).then_inc(att_mx, 1)
                dve.wait_ge(att_mx, n * 48 + (3 * u + 1))
                nc.vector.tensor_scalar(nm[:, p, 1:2], mx[:, p, 1:2], -ATT_SCALE, None, ALU.mult).then_inc(att_nm, 1)
            else:
                w = (min(qi, 4) + 1) * P
                dve.wait_ge(att_s, n * 32 + (2 * u + 2))
                nc.vector.reduce_max(mx[:, p, 2:3], two_banks(2)[:, 0:w], AX.X).then_inc(att_mx, 1)
                nc.vector.reduce_max(mx[:, p, 0:1], ps[:, 3, P:P + NCMP], AX.X).then_inc(att_mx, 1)
                dve.wait_ge(att_mx, n * 48 + (3 * u + 3))
                nc.vector.tensor_scalar(nm[:, p, 0:3:2], mx[:, p, 0:3:2], -ATT_SCALE, None, ALU.mult)\
                    .then_inc(att_nm, 1)

        def lo_dve(dve, n, s):
            u = UNIT_OF[s]
            w = len(GROUPS[u][s - GOFF[u]]) * P
            dve.wait_ge(att_hi, n * NG + (s + 1))
            nc.vector.tensor_tensor(PTl[:, s % 3, 0:w], ps[:, T_BANK + TURNS.index(("g", s)) % 2, 0:w],
                                    PTh[:, s % 3, 0:w].bitcast(F32), ALU.subtract).then_inc(att_lo, 1)

        def weights_dve(dve, n, i, kv, u):
            qi, h = divmod(u, 2)
            dve.wait_ge(att_exp, n * 48 + (3 * u + 3))
            nc.vector.tensor_scalar(lm[:, u % 2, :], ls[:, u % 2, :], 1e-30, None, ALU.max).then_inc(att_c, 1)
            dve.wait_ge(att_c, n * 48 + (3 * u + 1))
            nc.vector.reciprocal(li[:, u % 2, :], lm[:, u % 2, :]).then_inc(att_c, 1)
            dve.wait_ge(att_c, n * 48 + (3 * u + 2))
            nc.vector.tensor_tensor(rg[:, u % 2, :], li[:, u % 2, :],
                                    gates[:, qi, bass.ds(i * 12 + (6 * kv + 3 * h), 3)], ALU.mult).then_inc(att_c, 1)

        def gated_dve(dve, n, u):
            qi, h = divmod(u, 2)
            dve.wait_ge(att_pv, n * NG + GOFF[u + 1])
            dve.wait_ge(att_c, n * 48 + (3 * u + 3))
            nc.vector.tensor_tensor(og[:], ps[:, O_BANK, 3 * h * DH:3 * (h + 1) * DH].rearrange("p (c d) -> p c d", c=3),
                                    rg[:, u % 2, :].unsqueeze(2).to_broadcast([P, 3, DH]), ALU.mult).then_inc(att_og, 1)
            dve.wait_ge(att_og, n * UNITS + (u + 1))
            nc.vector.tensor_reduce(yn[:, qi % 2, h * DH:(h + 1) * DH], og[:].rearrange("p b d -> p d b"), AX.X, ALU.add)\
                .then_inc(att_y, 1)

        def att_dve(dve):
            fixed_dve(dve)
            dve.wait_ge(a_gv, 1)
            for part in range(2):
                max_dve(dve, 0, 0, part)
            with dve.Fori(0, PAIRS // 2) as i:
                for kv in range(KV):
                    n = i * 2 + kv
                    for s in range(NG):
                        u = UNIT_OF[s]
                        g = s - GOFF[u]
                        lo_dve(dve, n, s)
                        if s in GATED_AT:
                            gated_dve(dve, n, GATED_AT.index(s))
                        if g == 0:
                            max_dve(dve, n, u + 1, 0)
                        if g == WIN0[u]:
                            max_dve(dve, n, u + 1, 1)
                            weights_dve(dve, n, i, kv, u)
                    gated_dve(dve, n, UNITS - 1)

        def rope_pool(pool, r):
            tt = nc.gpsimd.tensor_tensor
            pool.wait_ge(q_swp, r * 64 + 64)
            tt(raw[:], raw[:], acos[:], ALU.mult).then_inc(q_steps, 1)
            tt(swp, swp, asin[:], ALU.mult).then_inc(q_steps, 1)
            pool.wait_ge(q_steps, r * 4 + 2)
            tt(raw[:], raw[:], swp, ALU.add).then_inc(q_steps, 1)
            pool.wait_ge(q_steps, r * 4 + 3)

        def rope_pool_split(pool, r):
            tt = nc.gpsimd.tensor_tensor
            tt(qhi[:], raw[:], zero[:].to_broadcast([P, S]), ALU.add).then_inc(q_steps, 1)
            pool.wait_ge(q_steps, r * 4 + 4)
            tt(qlo[:], raw[:], qhi[:].bitcast(F32), ALU.subtract).then_inc(q_roped, 1)

        def att_pool(pool, split):
            pool.wait_ge(att_consts_loaded, 7 * 16)
            pool.wait_ge(a_kk, 128)
            rope_pool(pool, 0)
            rope_pool_split(pool, 0)
            with pool.Fori(0, PAIRS // 2) as i:
                for kv in range(KV):
                    n = i * 2 + kv
                    for j in range(3):
                        if j == 2:
                            rope_pool(pool, n + 1)
                            pool.wait_ge(q_asm, n * 64 + 64)
                            rope_pool_split(pool, n + 1)
                        b = B_PAIR + 1 + 3 * kv + j
                        split(b % 2, i * 6 + b, i * 3 + (b // 2 + 1))
        m_ld = [sem("y_chunk_loaded0"), sem("y_chunk_loaded1")]
        m_hi, m_lo = sem("m_y_hi"), sem("m_y_lo")
        mt_ld = [sem("gate_loaded0"), sem("gate_loaded1")]
        m_gate, m_out, m_tmp, m_sum = sem("m_gate"), sem("m_out"), sem("m_gated_a"), sem("m_sum")
        x_hi, x_lo = sem("mix_hi_done"), sem("mix_lo_done")

        def merge_pe(pe):
            for xh, xl, b0, ready in ((YH, YL, B_WB, 0), (XH, XL, B_WA, KC)):
                pe.wait_ge(m_lo, ready + 1)
                with pe.Fori(0, 2) as i:
                    for j in range(4):
                        pe.wait_ge(m_out, i * 4 + (ready + j + 1))
                        if j == 0:
                            pe.wait_ge(block_split, i * 4 + (b0 + 1))
                        merge_job(pe, (b0 + j) % 2, i * 4 + (b0 + j + 1), xh, xl, 2 * j, ready)

        def merge_job(pe, slot, n, xh, xl, bank, ready):
            pe.wait_ge(block_split, n)
            for k in range(KC):
                pe.wait_ge(m_lo, ready + k + 1)
                w_h, w_l = wh[:, slot, k * P:(k + 1) * P], wl[:, slot, k * P:(k + 1) * P]
                for w, x in ((w_h, xh), (w_h, xl), (w_l, xh)):
                    for half in range(2):
                        mm = nc.tensor.matmul(ps[:, bank + half, :], w, x[:, k, half * HALF:(half + 1) * HALF],
                                              start=(k == 0 and w is w_h and x is xh),
                                              stop=(k == KC - 1 and w is w_l))
            mm.then_inc(blocks_multiplied, 1)

        def merge_act(act):
            act.wait_ge(q_asm, (PAIRS + 1) * 64)
            act.wait_ge(y_stored, (PAIRS + 1) * 16)
            act.wait_ge(m_stored, (4 * PAIRS + 1) * 16)

            def load_y(k):
                if k >= 2:
                    act.wait_ge(m_lo, k - 1)
                act.dma_start(ring2[:, k % 2, :], (yr_d if k < KC else ya_d)[k % KC]).then_inc(m_ld[k % 2], 16)

            def split_y(k):
                act.wait_ge(m_ld[k % 2], 16 * (k // 2 + 1))
                dst = YH if k < KC else XH
                nc.scalar.activation(dst[:, k % KC, :], ring2[:, k % 2, :], ACT.Copy).then_inc(m_hi, 1)
                if k + 2 < 2 * KC:
                    load_y(k + 2)

            def load_gate(n):
                if n >= 2:
                    act.wait_ge(m_out, 4 + n - 1)
                act.dma_start(mt[:, n % 2, :], ml_d[n]).then_inc(mt_ld[n % 2], 16)

            load_y(0)
            load_y(1)
            load_gate(0)
            load_gate(1)
            for k in range(KC):
                split_y(k)
            for n in range(2 * KC):
                act.wait_ge(mt_ld[n % 2], 16 * (n // 2 + 1))
                nc.scalar.activation(mt[:, n % 2, :], mt[:, n % 2, :], ACT.Sigmoid).then_inc(m_gate, 1)
                if n < KC:
                    split_y(KC + n)
                else:
                    act.wait_ge(m_sum, n - KC + 1)
                    nc.scalar.activation(YH[:, n - KC, :], x2[:, n - KC, :], ACT.Copy).then_inc(x_hi, 1)
                if n + 2 < 2 * KC:
                    load_gate(n + 2)
            out_act(act)

        def merge_dve(dve):
            nc.vector.sem_inc(m_out, 4)

            def split_y(k):
                dve.wait_ge(m_hi, k + 1)
                hi, lo = (YH, YL) if k < KC else (XH, XL)
                nc.vector.tensor_tensor(lo[:, k % KC, :], ring2[:, k % 2, :], hi[:, k % KC, :].bitcast(F32),
                                        ALU.subtract).then_inc(m_lo, 1)

            for k in range(KC):
                split_y(k)
            for n in range(2 * KC):
                if n < KC:
                    split_y(KC + n)
                dve.wait_ge(m_gate, n + 1)
                dve.wait_ge(blocks_multiplied, B_WB + n + 1)
                if n < KC:
                    nc.vector.tensor_tensor(x2[:, n, :], two_banks(2 * (n % 4)), mt[:, n % 2, :], ALU.mult)\
                        .then_inc(m_out, 1)
                    continue
                k = n - KC
                if k >= 1:
                    dve.wait_ge(m_sum, k)
                nc.vector.tensor_tensor(tmp[:], two_banks(2 * (n % 4)), mt[:, n % 2, :], ALU.mult).then_inc(m_out, 1)
                dve.wait_ge(m_out, 4 + n + 1)
                nc.vector.tensor_tensor(x2[:, k, :], x2[:, k, :], tmp[:], ALU.add).then_inc(m_sum, 1)
                dve.wait_ge(x_hi, k + 1)
                nc.vector.tensor_tensor(YL[:, k, :], x2[:, k, :], YH[:, k, :].bitcast(F32), ALU.subtract)\
                    .then_inc(x_lo, 1)
            out_dve(dve)

        o_out, o_gain, o_x = sem("o_out"), sem("o_gains_loaded"), [sem("x_again0"), sem("x_again1")]
        o_sq, o_ms, o_rms, o_rstd = sem("o_sq"), sem("o_ms"), sem("o_rms"), sem("o_rstd")
        o_nrm, o_x2 = sem("o_normed"), sem("o_x_mid")
        p_sq, p_ms, p_rms, p_rstd = sem("p_sq"), sem("p_ms"), sem("p_rms"), sem("p_rstd")
        p_xn, p_tr, p_hi, p_lo = sem("p_xn"), sem("p_tr"), sem("p_hi"), sem("p_lo")

        def out_pe(pe):
            pe.wait_ge(x_lo, KC)
            for nh in range(2):
                for j in range(4):
                    b = B_WO + 4 * nh + j
                    pe.wait_ge(block_split, b + 1)
                    for k2 in range(2):
                        k = 2 * j + k2
                        for s in range(SC):
                            if nh == 1 and k == 0:
                                pe.wait_ge(o_out, s + 1)
                            at = slice(k2 * HALF, (k2 + 1) * HALF)
                            mm = matmul3(ps[:, s, :], YH[:, k, s * P:(s + 1) * P], YL[:, k, s * P:(s + 1) * P],
                                         wh[:, b % 2, at], wl[:, b % 2, at], k == 0, k == KC - 1)
                    mm.then_inc(blocks_multiplied, 1)
            pe.wait_ge(o_out, 2 * SC)
            norm_T_pe(pe, xn2, p_xn, p_tr, p_lo)

        def out_act(act):
            act.wait_ge(m_out, 4 + 2 * KC)
            act.dma_start(mt[:, 0, :], norm_d[1]).then_inc(o_gain, 16)
            act.dma_start(mt[:, 1, :], norm_d[2]).then_inc(o_gain, 16)
            act.wait_ge(m_lo, 2 * KC)
            for s in range(2):
                act.dma_start(ring2[:, s, :], x_d[s * P:(s + 1) * P, :]).then_inc(o_x[s], 16)
            act.wait_ge(x_lo, KC)
            for nh in range(2):
                act.wait_ge(blocks_multiplied, B_WO + 4 * (nh + 1))
                for s in range(SC):
                    nc.scalar.activation(x2[:, s, nh * HALF:(nh + 1) * HALF], ps[:, s, :], ACT.Copy).then_inc(o_out, 1)
            squares_act(act, x2, xn2[:, 0, :], o_sq, lambda s: act.wait_ge(o_out, SC + s + 1))
            act.wait_ge(o_ms, 1)
            nc.scalar.activation(rms[:], ms[:], ACT.Sqrt).then_inc(o_rms, 1)
            for s in range(SC):
                if s + 2 < SC:
                    act.wait_ge(o_x2, s + 1)
                    act.dma_start(ring2[:, s % 2, :], x_d[(s + 2) * P:(s + 3) * P, :]).then_inc(o_x[s % 2], 16)
            act.wait_ge(o_sq, SC)
            squares_act(act, x2, xn2[:, 0, :], p_sq, lambda s: act.wait_ge(o_x2, s + 1))
            act.wait_ge(p_ms, 1)
            nc.scalar.activation(rms[:], ms[:], ACT.Sqrt).then_inc(p_rms, 1)
            norm_T_act(act, XH, p_tr, p_hi)

        def out_dve(dve):
            mean_sq_dve(dve, o_sq, o_ms, o_rms, o_rstd)
            dve.wait_ge(o_rstd, 1)
            dve.wait_ge(o_gain, 32)
            for s in range(SC):
                nc.vector.scalar_tensor_tensor(out=x2[:, s, :], in0=x2[:, s, :], scalar=rstd[:, s:s + 1],
                                               in1=mt[:, 0, :], op0=ALU.mult, op1=ALU.mult).then_inc(o_nrm, 1)
                dve.wait_ge(o_nrm, s + 1)
                dve.wait_ge(o_x[s % 2], 16 * (s // 2 + 1))
                nc.vector.tensor_tensor(x2[:, s, :], x2[:, s, :], ring2[:, s % 2, :], ALU.add).then_inc(o_x2, 1)
            mean_sq_dve(dve, p_sq, p_ms, p_rms, p_rstd)
            norm_T_dve(dve, x2, mt[:, 1, :], xn2, p_rstd, p_xn, p_tr, XH, XL, p_hi, p_lo)
        f_silu, f_mul, f_hi, f_lo = sem("f_silu"), sem("f_mul"), sem("f_hi"), sem("f_lo")
        f_down, f_add = sem("f_down"), sem("f_add")
        f_gain = sem("f_gain_loaded")
        e_sq, e_ms, e_rms, e_rstd = sem("e_sq"), sem("e_ms"), sem("e_rms"), sem("e_rstd")
        e_nrm, e_y, out_stored = sem("e_normed"), sem("e_y"), sem("out_stored")
        DOWN = 2 * SC

        def ffn_gate_up_pe(pe, c, b, slot, first=False):
            if not first:
                pe.wait_ge(f_silu, c)
            t_job(pe, slot, b + 1, XH, XL, 0)
            if not first:
                pe.wait_ge(f_mul, c)
            t_job(pe, 1 - slot, b + 2, XH, XL, 2)

        def ffn_down_pe(pe, c, odd, b, slot, first=False):
            pe.wait_ge(block_split, b + 1)
            pe.wait_ge(f_lo, c + 1)
            for t in range(DOWN):
                s, nh = divmod(t, 2)
                if not (first and t < 4):
                    pe.wait_ge(f_add, c * DOWN + (t - 3))
                at = slice(nh * HALF, (nh + 1) * HALF)
                mm = matmul3(ps[:, 4 + t % 4, :], FH[:, odd, s * P:(s + 1) * P], FL[:, odd, s * P:(s + 1) * P],
                             wh[:, slot, at], wl[:, slot, at], True, True)
                mm.then_inc(f_down if t < DOWN - 1 else blocks_multiplied, 1)

        def ffn_pe(pe):
            out_pe(pe)
            pe.wait_ge(p_lo, 2 * SC)
            b = B_FFN
            ffn_gate_up_pe(pe, 0, b, b % 2, True)
            ffn_gate_up_pe(pe, 1, b + 2, b % 2)
            ffn_down_pe(pe, 0, 0, b + 4, b % 2, True)
            with pe.Fori(0, FF // 2 - 1) as i:
                for j in range(2):
                    c = i * 2 + (2 + j)
                    bj = i * 6 + (b + 5 + 3 * j)
                    slot = (b + 5 + 3 * j) % 2
                    ffn_gate_up_pe(pe, c, bj, slot)
                    ffn_down_pe(pe, i * 2 + (1 + j), 1 - j, bj + 2, slot)
            ffn_down_pe(pe, FF - 1, (FF - 1) % 2, N_BLOCKS - 1, (N_BLOCKS - 1) % 2)

        def ffn_chunk_act(act, c, odd, gate_block):
            act.wait_ge(blocks_multiplied, gate_block + 1)
            nc.scalar.activation(sg[:], two_banks(0), ACT.Silu).then_inc(f_silu, 1)
            act.wait_ge(f_mul, c + 1)
            nc.scalar.activation(FH[:, odd, :], ff[:], ACT.Copy).then_inc(f_hi, 1)

        def ffn_act(act):
            act.dma_start(gc[:], norm_d[3]).then_inc(f_gain, 16)
            ffn_chunk_act(act, 0, 0, B_FFN)
            ffn_chunk_act(act, 1, 1, B_FFN + 2)
            with act.Fori(0, FF // 2 - 1) as i:
                for j in range(2):
                    ffn_chunk_act(act, i * 2 + (2 + j), j, i * 6 + (B_FFN + 5 + 3 * j))
            squares_act(act, acc, xn2[:, 0, :], e_sq, lambda s: act.wait_ge(f_add, (FF - 1) * DOWN + 2 * s + 2))
            act.wait_ge(e_ms, 1)
            nc.scalar.activation(rms[:], ms[:], ACT.Sqrt).then_inc(e_rms, 1)
            for s in range(SC):
                act.wait_ge(e_y, s + 1)
                act.dma_start(out_d[s * P:(s + 1) * P, :], acc[:, s, :]).then_inc(out_stored, 16)
            act.wait_ge(out_stored, SC * 16)

        def ffn_mul_dve(dve, c, gate_block, later=True):
            dve.wait_ge(f_silu, c + 1)
            dve.wait_ge(blocks_multiplied, gate_block + 2)
            if later:
                dve.wait_ge(f_lo, c)
            nc.vector.tensor_tensor(ff[:], two_banks(2), sg[:], ALU.mult).then_inc(f_mul, 1)

        def ffn_lo_dve(dve, c, odd):
            dve.wait_ge(f_hi, c + 1)
            nc.vector.tensor_tensor(FL[:, odd, :], ff[:], FH[:, odd, :].bitcast(F32), ALU.subtract).then_inc(f_lo, 1)

        def ffn_add_dve(dve, c, down_block, t, first=False):
            s, nh = divmod(t, 2)
            if t < DOWN - 1:
                dve.wait_ge(f_down, c * (DOWN - 1) + (t + 1))
            else:
                dve.wait_ge(blocks_multiplied, down_block + 1)
            tile_ = acc[:, s, nh * HALF:(nh + 1) * HALF]
            if first:
                nc.vector.tensor_copy(tile_, ps[:, 4 + t % 4, :]).then_inc(f_add, 1)
            else:
                dve.wait_ge(f_add, c * DOWN + (t + 1 - DOWN))
                nc.vector.tensor_tensor(tile_, tile_, ps[:, 4 + t % 4, :], ALU.add).then_inc(f_add, 1)

        def ffn_dve(dve):
            ffn_mul_dve(dve, 0, B_FFN, False)
            ffn_lo_dve(dve, 0, 0)
            ffn_mul_dve(dve, 1, B_FFN + 2)
            ffn_lo_dve(dve, 1, 1)
            for t in range(DOWN):
                ffn_add_dve(dve, 0, B_FFN + 4, t, True)
            with dve.Fori(0, FF // 2 - 1) as i:
                for j in range(2):
                    gate_block = i * 6 + (B_FFN + 5 + 3 * j)
                    ffn_mul_dve(dve, i * 2 + (2 + j), gate_block)
                    for t in range(DOWN):
                        ffn_add_dve(dve, i * 2 + (1 + j), gate_block + 2, t)
                        if t == 2:
                            ffn_lo_dve(dve, i * 2 + (2 + j), j)
            for t in range(DOWN):
                ffn_add_dve(dve, FF - 1, N_BLOCKS - 1, t)
            mean_sq_dve(dve, e_sq, e_ms, e_rms, e_rstd)
            dve.wait_ge(e_rstd, 1)
            dve.wait_ge(f_gain, 16)
            for s in range(SC):
                nc.vector.scalar_tensor_tensor(out=acc[:, s, :], in0=acc[:, s, :], scalar=rstd[:, s:s + 1],
                                               in1=gc[:], op0=ALU.mult, op1=ALU.mult).then_inc(e_nrm, 1)
                dve.wait_ge(e_nrm, s + 1)
                nc.vector.tensor_tensor(acc[:, s, :], acc[:, s, :], x2[:, s, :], ALU.add).then_inc(e_y, 1)

        @block.sync
        def _(sp):
            for s in range(SC):
                sp.dma_start(xs[:, s, :], x_d[s * P:(s + 1) * P, :]).then_inc(x_loaded[s], 16)
                if s < 2:
                    sp.dma_start(wraw[:, s, :], wst_d[s]).then_inc(block_loaded[s], 16)
            with sp.Fori(0, (N_BLOCKS - 3) // 2) as i:
                for j in range(2):
                    sp.wait_ge(block_split, i * 2 + (j + 1))
                    sp.dma_start(wraw[:, j, :], wst_d[bass.ds(i * 2 + (2 + j), 1)].rearrange("a p n -> p (a n)"))\
                        .then_inc(block_loaded[j], 16)
            sp.wait_ge(block_split, N_BLOCKS - 2)
            sp.dma_start(wraw[:, 0, :], wst_d[N_BLOCKS - 1]).then_inc(block_loaded[0], 16)

        @block.gpsimd
        def _(pool):
            nc.gpsimd.memset(zero[:], 0.0).then_inc(zero_set, 1)
            pool.wait_ge(zero_set, 1)

            def split(slot, b, loads, reused=True):
                pool.wait_ge(block_loaded[slot], loads * 16)
                if reused:
                    pool.wait_ge(blocks_multiplied, b - 1)
                nc.gpsimd.tensor_tensor(wh[:, slot, :], wraw[:, slot, :], zero[:].to_broadcast([P, 1024]),
                                        ALU.add).then_inc(block_hi, 1)
                pool.wait_ge(block_hi, b + 1)
                nc.gpsimd.tensor_tensor(wl[:, slot, :], wraw[:, slot, :], wh[:, slot, :].bitcast(F32),
                                        ALU.subtract).then_inc(block_split, 1)

            split(0, 0, 1, False)
            split(1, 1, 1, False)
            with pool.Fori(0, B_Q0 // 2) as i:
                for j in range(2):
                    split(j, i * 2 + (2 + j), i + 2)
            att_pool(pool, split)
            first = B_WB + 1
            with pool.Fori(0, (N_BLOCKS - 1 - first) // 2) as i:
                for j in range(2):
                    split(j, i * 2 + (first + j), i + (first // 2 + 1))
            split(0, N_BLOCKS - 1, N_BLOCKS // 2 + 1)

        @block.tensor
        def _(pe):
            s1_pe(pe)
            ret_pe(pe)
            att_pe(pe)
            merge_pe(pe)
            ffn_pe(pe)

        @block.scalar
        def _(act):
            act.dma_start(ident[:], norm_d[4, :, 0:P]).then_inc(consts_loaded, 16)
            act.dma_start(g0[:], norm_d[0]).then_inc(consts_loaded, 16)
            s1_act(act)
            ret_act(act)
            att_act(act)
            merge_act(act)
            ffn_act(act)

        @block.vector
        def _(dve):
            s1_dve(dve)
            ret_dve(dve)
            att_dve(dve)
            merge_dve(dve)
            ffn_dve(dve)


def kernel(**inputs):
    import numpy as np
    import concourse.bacc as bacc
    from concourse.bass_utils import run_bass_kernel_spmd

    a = {k: np.asarray(v) for k, v in inputs.items()}
    w_in = a["w_in"][0]
    widths = (1024, 768, 48, 512, 512, 1024, 1024, 2048)
    ends = np.cumsum(widths)
    wq, wkv, wg, wqr, wkr, wvr, wgr, wm = (w_in[:, e - w:e] for e, w in zip(ends, widths))

    def t_blocks(w):
        return list(w.reshape(KC, P, -1, P).transpose(2, 1, 0, 3).reshape(-1, P, 1024))

    def row_blocks(w, n):
        per = 1024 // n
        return list(w.reshape(KC // per, per, P, n).transpose(0, 2, 1, 3).reshape(-1, P, 1024))

    q, kv = t_blocks(wq), t_blocks(wkv)
    qr, kr, gr, m = t_blocks(wqr), t_blocks(wkr), t_blocks(wgr), t_blocks(wm)
    order = [0, 4, 1, 5, 2, 6, 3, 7]
    gate_w = wg.reshape(D, PAIRS, 2, 3)[:, order].reshape(D, 48)
    vsg = np.zeros((D, HALF), np.float32)
    vsg[:, 0:P], vsg[:, P:2 * P], vsg[:, 2 * P:2 * P + 48] = wkv[:, 3 * P:4 * P], wkv[:, 5 * P:6 * P], gate_w
    blocks = []
    for h in range(RH):
        blocks += row_blocks(wvr[:, h * DV:(h + 1) * DV], DV) + [qr[h], kr[h], gr[2 * h], gr[2 * h + 1]]
    blocks += [kv[0], kv[1], kv[2], kv[4]] + row_blocks(vsg, HALF)
    blocks.append(q[0])
    for n in range(PAIRS):
        blocks += [q[order[min(n + 1, PAIRS - 1)]], m[KC + n], m[n]]
    blocks += t_blocks(a["w_branch_b"][0])
    blocks += t_blocks(a["w_branch_a"][0].reshape(PAIRS, P, D)[order].reshape(D, D))
    wo = a["w_out"][0]
    blocks += row_blocks(wo[:, :HALF], HALF) + row_blocks(wo[:, HALF:], HALF)
    gate, up, down = t_blocks(a["w_ffn_gate"][0]), t_blocks(a["w_ffn_up"][0]), a["w_ffn_down"][0].reshape(FF, P, D)
    for c in range(FF):
        blocks += [gate[c], up[c]] + ([down[c - 1]] if c else [])
    blocks.append(down[FF - 1])
    assert len(blocks) == N_BLOCKS

    norm = np.zeros((5, P, D), np.float32)
    for i, name in enumerate(("g_pre_mix", "g_post_mix", "g_pre_ffn", "g_post_ffn")):
        norm[i] = np.broadcast_to(a[name][0], (P, D))
    norm[4, :, :P] = np.eye(P)

    def rope(d):
        half = d // 2
        inv = np.float32(10000.0) ** (-np.arange(half, dtype=np.float32) * np.float32(2.0) / np.float32(d))
        ang = (inv[:, None] * np.arange(S, dtype=np.float32)[None, :]).astype(np.float32).astype(np.float64)
        cos, sin = np.cos(ang), np.sin(ang)
        t = np.stack([np.concatenate([cos, cos]), np.concatenate([-sin, sin])])
        return np.ascontiguousarray(np.tile(t, (1, P // d, 1)).astype(np.float32))

    log_g = np.log1p(-np.exp2(-5.0 - np.arange(RH)))
    i = np.arange(P)
    ret = np.zeros((RH, P, P + 4), np.float32)
    diff = i[None, :] - i[:, None]
    for h in range(RH):
        ret[h, :, :P] = np.where(diff >= 0, np.exp(log_g[h] * np.maximum(diff, 0)), 0.0)
        ret[h, :, P] = np.exp(log_g[h] * (P - 1.0 - i))
        ret[h, :, P + 1] = np.exp(log_g[h] * (i + 1.0))
        ret[h, :, P + 2] = np.exp(log_g[h] * P)
    neg = np.float32(-1e30)
    t = np.arange(S).reshape(SC, P).T
    cmp_end = np.arange(NCMP) * 16 + 31
    mask = np.zeros((P, 2 * P + SC * NCMP + 1), np.float32)
    mask[:, 0:P] = np.where(i[None, :] > i[:, None], neg, 0)
    mask[:, P:2 * P] = np.where(i[None, :] <= i[:, None], neg, 0)
    seen = (cmp_end[None, None, :] <= t[:, :, None]) & (np.arange(NCMP) < NCMP - 1)
    mask[:, 2 * P:-1] = np.where(seen, 0, neg).reshape(P, -1)
    mask[:, -1] = i >= 31

    arrays = {
        "x": a["x"][0],
        "weights": np.stack(blocks),
        "norm": norm,
        "rope_a": rope(DH),
        "rope_r": rope(128),
        "ret": ret,
        "mask": mask,
        "w1": np.stack([a[f"cmp_w1_{c}"][0].reshape(16, P, P).transpose(1, 0, 2) for c in "kv"], 1),
        "pos": np.stack([a[f"cmp_pos_{c}"][0].reshape(16, P).T for c in "kv"], 1),
        "w2k": np.concatenate([a["cmp_w2_k"][0]] * 2, 1),
        "w2v": a["cmp_w2_v"][0],
    }
    nc = bacc.Bacc("TRN2", target_bir_lowering=False, num_devices=1)
    args = []
    for name in arrays:
        arrays[name] = np.ascontiguousarray(arrays[name])
        args.append(nc.dram_tensor(name, arrays[name].shape, F32, kind="ExternalInput").ap())
    args.append(nc.dram_tensor("out", (S, D), F32, kind="ExternalOutput").ap())
    layer(nc, *args)
    r = run_bass_kernel_spmd(nc, [arrays], core_ids=[0])
    return r.results[0]["out"].reshape(1, S, D)
```

```python
from contextlib import ExitStack

import concourse.bass as bass
from concourse import mybir

F32 = mybir.dt.float32
FR = mybir.dt.float32r
ALU = mybir.AluOpType
ACT = mybir.ActivationFunctionType
AX = mybir.AxisListType

P = 128
S = 1024
D = 1024
KC = D // P
SC = S // P
HALF = 512
DH = 64
KV = 2
NCMP = 64
RH = 4
DV = 256
FF = 2816 // P
EPS = 1e-6
ATT_SCALE = DH ** -0.5
RET_SCALE = 128 ** -0.5
PAIRS = 8

B_RET = 6
B_KV = RH * B_RET
B_Q0 = B_KV + 4
B_VG = B_Q0 + 1
B_PAIR = B_VG + 4
B_WB = B_PAIR + 3 * PAIRS
B_WA = B_WB + KC
B_WO = B_WA + KC
B_FFN = B_WO + KC
N_BLOCKS = B_FFN + 3 * FF


def groups_of(qi):
    sel = [("sel", kb, kb * P) for kb in range(qi + 1)]
    lo = max(0, qi - 4)
    win = [("win", kb, (kb - lo) * P) for kb in range(lo, qi + 1)] + [("cmp", None, 5 * P)]
    return [sel[a:a + 4] for a in range(0, len(sel), 4)] + [win[a:a + 4] for a in range(0, len(win), 4)]


def layer(nc, x_d, wst_d, norm_d, rope_a_d, rope_r_d, ret_d, mask_d, w1_d, pos_d, w2k_d, w2v_d, out_d):
    yr_d = nc.dram_tensor("y_ret_T", (KC, P, S), F32).ap()
    ya_d = nc.dram_tensor("y_att_T", (KC, P, S), F32).ap()
    ml_d = nc.dram_tensor("merge_logits_T", (2 * KC, P, S), F32).ap()

    with ExitStack() as ctx:
        def sem(name):
            return ctx.enter_context(nc.semaphore(name))

        def tile(scope, name, shape, dt=F32):
            return scope.enter_context(nc.sbuf_tensor(name, [P, *shape], dt))

        XH = tile(ctx, "act_hi", [KC, S], FR)
        XL = tile(ctx, "act_lo", [KC, S], FR)
        wraw = tile(ctx, "w_raw", [2, 1024])
        wh = tile(ctx, "w_hi", [2, 1024], FR)
        wl = tile(ctx, "w_lo", [2, 1024], FR)
        ident = tile(ctx, "ident", [P])
        zero = tile(ctx, "zero", [1])
        ss = tile(ctx, "sum_sq", [SC])
        ms = tile(ctx, "mean_sq", [SC])
        rms = tile(ctx, "rms", [SC])
        rstd = tile(ctx, "rstd", [SC])
        ss2 = tile(ctx, "sum_sq_right", [SC])
        ps = ctx.enter_context(nc.psum_tensor("ps", [P, 8, HALF], F32))

        sc0 = ExitStack()
        xs = tile(sc0, "x_rows", [SC, D])
        g0 = tile(sc0, "g_pre_mix", [D])
        xn = tile(sc0, "x_normed", [2, D])
        sq0 = tile(sc0, "x_squares", [D])
        sc0.close()
        scr = ExitStack()
        rcos = tile(scr, "ret_cos", [S])
        rsin = tile(scr, "ret_sin", [S])
        rraw = tile(scr, "ret_raw", [2, S])
        rswp = tile(scr, "ret_swapped", [S])
        rqh = tile(scr, "ret_q_hi", [S], FR)
        rql = tile(scr, "ret_q_lo", [S], FR)
        rkh = tile(scr, "ret_k_hi", [S], FR)
        rkl = tile(scr, "ret_k_lo", [S], FR)
        vh = tile(scr, "ret_v_hi", [SC, DV], FR)
        vl = tile(scr, "ret_v_lo", [SC, DV], FR)
        knh = tile(scr, "ret_kdec_hi", [SC, P], FR)
        knl = tile(scr, "ret_kdec_lo", [SC, P], FR)
        silu_g = tile(scr, "ret_silu_g", [2, S])
        ro = tile(scr, "ret_out", [SC, DV])
        ry = tile(scr, "ret_y_T", [2, S])
        hc = tile(scr, "ret_decays", [P + 4])
        im = tile(scr, "ret_inner", [2, P])
        imh = tile(scr, "ret_inner_hi", [2, P], FR)
        iml = tile(scr, "ret_inner_lo", [2, P], FR)
        R = tile(scr, "ret_state", [DV])
        Rh = tile(scr, "ret_state_hi", [2, DV], FR)
        Rl = tile(scr, "ret_state_lo", [2, DV], FR)
        t2 = tile(scr, "ret_cross", [2, DV])
        bst = tile(scr, "ret_bn", [SC, 6])
        mv = tile(scr, "ret_mean_var", [SC, 2])
        ve = tile(scr, "ret_var_eps", [SC])
        rsd = tile(scr, "ret_std", [SC])
        rrs = tile(scr, "ret_rstd", [SC])
        scr.close()
        sca = ExitStack()
        acos = tile(sca, "att_cos", [S])
        asin = tile(sca, "att_sin", [S])
        kk = tile(sca, "keys_hi_twice", [2, KV, S], FR)
        kl = tile(sca, "keys_lo", [2, S], FR)
        V = tile(sca, "values", [SC, 2 * KV, 2, DH], FR)
        kch = tile(sca, "cmp_keys_hi", [KV, NCMP], FR)
        kcl = tile(sca, "cmp_keys_lo", [KV, NCMP], FR)
        vc = tile(sca, "cmp_values", [KV, 2, DH], FR)
        gates = tile(sca, "gates", [SC, 48])
        qhi = tile(sca, "q_hi", [S], FR)
        qlo = tile(sca, "q_lo", [S], FR)
        maskr = tile(sca, "masks_r", [2 * P + SC * NCMP + 1], FR)
        identr = tile(sca, "ident_r", [P], FR)
        qst = [tile(sca, "q_even_pair", [2, S], FR)]
        scf = ExitStack()
        fraw = tile(scf, "kv_raw", [2, S])
        fswp = tile(scf, "kv_swapped", [S])
        POS0 = S + 16
        kcs = tile(scf, "cmp_in_k", [KV, POS0 + 32])
        vcs = tile(scf, "cmp_in_v", [KV, POS0 + 32])
        w1 = tile(scf, "cmp_w1", [2, 16, P])
        w2k = tile(scf, "cmp_w2_k_twice", [P])
        w2v = tile(scf, "cmp_w2_v", [DH])
        pos = tile(scf, "cmp_pos", [2, 16])
        hb = tile(scf, "cmp_bias", [2])
        hid = fswp[:, 0:2 * P].rearrange("p (t n) -> p t n", t=2)
        scf.close()
        raw = tile(sca, "q_raw", [S])
        swp = qlo[:].bitcast(F32)
        Ps = tile(sca, "probs_sel", [2, S])
        Pw = tile(sca, "probs_win_cmp", [2, 6 * P])
        qst.append(tile(sca, "q_odd_pair", [2, S], FR))
        PTh = tile(sca, "probs_T_hi", [3, HALF], FR)
        PTl = tile(sca, "probs_T_lo", [3, HALF], FR)
        fm = tile(sca, "merge_half", [HALF])
        yT = tile(sca, "att_y_T", [S])
        yn = tile(sca, "att_y", [2, P])
        og = tile(sca, "att_gated", [3, 2 * DH])
        mx = tile(sca, "row_max", [2, 3])
        nm = tile(sca, "neg_max", [2, 3])
        ls = tile(sca, "row_sum", [2, 3])
        lm = tile(sca, "row_sum_held", [2, 3])
        li = tile(sca, "row_sum_inv", [2, 3])
        rg = tile(sca, "row_weight", [2, 3])
        sca.close()
        scm = ExitStack()
        x2 = tile(scm, "x_mid", [SC, D])
        ring2 = tile(scm, "loaded_rows", [2, S])
        mt = tile(scm, "merge_gate", [2, S])
        scm1 = ExitStack()
        YH = tile(scm1, "mix_hi", [KC, S], FR)
        YL = tile(scm1, "mix_lo", [KC, S], FR)
        tmp = tile(scm1, "branch_gated", [S])
        scm1.close()
        xn2 = tile(scm, "x_mid_normed", [2, D])
        sg = tile(scm, "silu_gate", [S])
        ff = tile(scm, "ffn_hidden", [S])
        FH = tile(scm, "ffn_hidden_hi", [2, S], FR)
        FL = tile(scm, "ffn_hidden_lo", [2, S], FR)
        acc = tile(scm, "ffn_out", [SC, D])
        gc = tile(scm, "g_post_ffn", [D])
        scm.close()

        chunk_loaded = [sem(f"chunk_loaded{i}") for i in range(SC)]
        consts_loaded = sem("consts_loaded")
        ret_consts_loaded = sem("ret_consts_loaded")
        att_consts_loaded = sem("att_consts_loaded")
        block_loaded = [sem("block_loaded0"), sem("block_loaded1")]
        block_hi = sem("block_hi")
        block_split = sem("block_split")
        blocks_multiplied = sem("blocks_multiplied")
        zero_set = sem("zero_set")
        dve_passed = sem("dve_passed")

        block = ctx.enter_context(nc.Block())

        def matmul3(out, wh_, wl_, xh_, xl_, first, last):
            nc.tensor.matmul(out, wh_, xh_, start=first, stop=False)
            nc.tensor.matmul(out, wh_, xl_, start=False, stop=False)
            return nc.tensor.matmul(out, wl_, xh_, start=False, stop=last)

        def t_job(pe, slot, n, xh, xl, bank, k_ready=None):
            pe.wait_ge(block_split, n)
            for k in range(KC):
                if k_ready is not None:
                    pe.wait_ge(k_ready, k + 1)
                w_h, w_l = wh[:, slot, k * P:(k + 1) * P], wl[:, slot, k * P:(k + 1) * P]
                for w, x in ((w_h, xh), (w_h, xl), (w_l, xh)):
                    for half in range(2):
                        mm = nc.tensor.matmul(ps[:, bank + half, :], w, x[:, k, half * HALF:(half + 1) * HALF],
                                              start=(k == 0 and w is w_h and x is xh),
                                              stop=(k == KC - 1 and w is w_l))
            mm.then_inc(blocks_multiplied, 1)

        s1_sq, s1_ms, s1_rms, s1_rstd = sem("s1_sq"), sem("s1_ms"), sem("s1_rms"), sem("s1_rstd")
        s1_xn, s1_tr, s1_hi, s1_lo = sem("s1_xn"), sem("s1_tr"), sem("s1_hi"), sem("s1_lo")

        def turned_hi_act(act, t, hi, tr, hi_sem, bank0=0):
            s, g = divmod(t, 2)
            act.wait_ge(tr, t + 1)
            nc.scalar.activation(hi[:, 4 * g:4 * g + 4, s * P:(s + 1) * P],
                                 ps[:, bank0 + t % 4, :].rearrange("p (k n) -> p k n", k=4), ACT.Copy).then_inc(hi_sem, 1)

        def norm_lo(dve, s, hi, lo, hi_sem, lo_sem, bank0=0):
            for g in range(2):
                t = 2 * s + g
                dve.wait_ge(hi_sem, t + 1)
                at = (slice(None), slice(4 * g, 4 * g + 4), slice(s * P, (s + 1) * P))
                nc.vector.tensor_tensor(lo[at], ps[:, bank0 + t % 4, :].rearrange("p (k n) -> p k n", k=4),
                                        hi[at].bitcast(F32), ALU.subtract).then_inc(lo_sem, 1)

        def norm_T_pe(pe, rows, xn_sem, tr, lo_sem):
            for s in range(SC):
                pe.wait_ge(xn_sem, s + 1)
                for g in range(2):
                    turned_pe(pe, 2 * s + g, rows, tr, lo_sem)

        def turned_pe(pe, t, rows, tr, lo_sem, bank0=0):
            s, g = divmod(t, 2)
            if t >= 4:
                pe.wait_ge(lo_sem, t - 3)
            for k in range(4):
                mm = nc.tensor.transpose(ps[:, bank0 + t % 4, k * P:(k + 1) * P],
                                         rows[:, s % 2, (4 * g + k) * P:(4 * g + k + 1) * P], ident[:])
            mm.then_inc(tr, 1)

        def group_ms_dve(dve, g, size, sq_sem, ms_sem):
            at = slice(size * g, size * (g + 1))
            dve.wait_ge(sq_sem, size * (g + 1))
            nc.vector.tensor_scalar(ms[:, at], ss[:, at], 1.0 / D, EPS, ALU.mult, ALU.add).then_inc(ms_sem, 1)

        def group_rms_act(act, g, size, ms_sem, rms_sem):
            at = slice(size * g, size * (g + 1))
            act.wait_ge(ms_sem, g + 1)
            nc.scalar.activation(rms[:, at], ms[:, at], ACT.Sqrt).then_inc(rms_sem, 1)

        def group_rstd_dve(dve, g, size, rms_sem, rstd_sem):
            at = slice(size * g, size * (g + 1))
            dve.wait_ge(rms_sem, g + 1)
            nc.vector.reciprocal(rstd[:, at], rms[:, at]).then_inc(rstd_sem, 1)
            dve.wait_ge(rstd_sem, g + 1)

        def square_act(act, rows, s, junk, sq_sem):
            if s >= 1:
                act.wait_ge(sq_sem, s)
            nc.scalar.activation(junk, rows[:, s, :], ACT.Square, accum_out=ss[:, s:s + 1]).then_inc(sq_sem, 1)

        def s1_act(act):
            def turned(g):
                for t in range(4 * g, 4 * g + 4):
                    turned_hi_act(act, t, XH, s1_tr, s1_hi)

            for g in range(4):
                for s in (2 * g, 2 * g + 1):
                    act.wait_ge(chunk_loaded[s], 16)
                    square_act(act, xs, s, sq0[:], s1_sq)
                group_rms_act(act, g, 2, s1_ms, s1_rms)
                if g >= 1:
                    turned(g - 1)
            turned(3)

        def s1_dve(dve):
            group_ms_dve(dve, 0, 2, s1_sq, s1_ms)
            group_rstd_dve(dve, 0, 2, s1_rms, s1_rstd)
            dve.wait_ge(consts_loaded, 32)
            for s in range(SC):
                g = s // 2 + 1
                if s >= 2:
                    dve.wait_ge(s1_tr, 2 * (s - 1))
                nc.vector.scalar_tensor_tensor(out=xn[:, s % 2, :], in0=xs[:, s, :], scalar=rstd[:, s:s + 1],
                                               in1=g0[:], op0=ALU.mult, op1=ALU.mult).then_inc(s1_xn, 1)
                if s >= 2:
                    norm_lo(dve, s - 2, XH, XL, s1_hi, s1_lo)
                if g < 4 and s % 2 == 0:
                    group_ms_dve(dve, g, 2, s1_sq, s1_ms)
                if g < 4 and s % 2 == 1:
                    group_rstd_dve(dve, g, 2, s1_rms, s1_rstd)
            for s in (SC - 2, SC - 1):
                norm_lo(dve, s, XH, XL, s1_hi, s1_lo)

        def s1_pe(pe):
            pe.wait_ge(consts_loaded, 32)
            norm_T_pe(pe, xn, s1_xn, s1_tr, s1_lo)

        r_v_acc, r_v_hi, r_v_lo, r_g_half = sem("r_v_acc"), sem("r_v_hi"), sem("r_v_lo"), sem("r_gate_half")
        r_raw, r_swp, r_rope = sem("r_raw"), sem("r_swp"), sem("r_rope")
        r_rh, r_rl, r_silu = sem("r_rope_hi"), sem("r_rope_lo"), sem("r_silu")
        r_hc = sem("r_decays_loaded")
        r_kt, r_kn_hi, r_kn_lo = sem("r_kt"), sem("r_kn_hi"), sem("r_kn_lo")
        r_inner, r_u, r_o = sem("r_inner"), sem("r_u"), sem("r_o")
        r_im, r_im_hi, r_im_lo = sem("r_im"), sem("r_im_hi"), sem("r_im_lo")
        r_R, r_R_hi, r_R_lo = sem("r_R"), sem("r_R_hi"), sem("r_R_lo")
        r_t2, r_oacc = sem("r_t2"), sem("r_oacc")
        r_bn, r_mv, r_ve, r_std, r_rs = sem("r_bn"), sem("r_mv"), sem("r_ve"), sem("r_std"), sem("r_rs")
        r_xn, r_yt, r_y, r_y_stored = sem("r_xn"), sem("r_yt"), sem("r_y"), sem("r_y_stored")
        decT, dk, dq, dc = hc[:, 0:P], hc[:, P:P + 1], hc[:, P + 1:P + 2], hc[:, P + 2:P + 3]

        GATE_HEAD, GATE_STEP = 48, 6
        assert GATE_HEAD + SC * GATE_STEP == 4 * 24 and GATE_HEAD <= 2 * 24
        GATE_OUT = [max(0, -(-(24 * (j + 1) - GATE_HEAD) // GATE_STEP)) for j in range(4)]

        def values_pe(pe, h):
            for j in range(2):
                pe.wait_ge(block_split, h * B_RET + (j + 1))
                for k4 in range(4):
                    k = 4 * j + k4
                    for s in range(SC):
                        if k == 0 and s == 4 and not (isinstance(h, int) and h == 0):
                            pe.wait_ge(r_oacc, h * 8)
                        at = slice(s % 2 * DV, (s % 2 + 1) * DV)
                        mm = matmul3(ps[:, 4 + s // 2, at], XH[:, k, s * P:(s + 1) * P], XL[:, k, s * P:(s + 1) * P],
                                     wh[:, j, k4 * DV:(k4 + 1) * DV], wl[:, j, k4 * DV:(k4 + 1) * DV],
                                     k == 0 and s % 2 == 0, k == KC - 1 and s % 2 == 1)
                        if k == KC - 1 and s in (1, 3, 5):
                            mm.then_inc(r_v_acc, 1)
                mm.then_inc(blocks_multiplied, 1)

        def values_act(act, h):
            for b in range(4):
                if b < 3:
                    act.wait_ge(r_v_acc, h * 3 + (b + 1))
                else:
                    act.wait_ge(blocks_multiplied, h * B_RET + 2)
                nc.scalar.activation(vh[:, 2 * b:2 * b + 2, :].rearrange("p a n -> p (a n)"), ps[:, 4 + b, :],
                                     ACT.Copy).then_inc(r_v_hi, 1)

        def values_dve(dve, h):
            for b in range(4):
                dve.wait_ge(r_v_hi, h * 4 + (b + 1))
                nc.vector.tensor_tensor(vl[:, 2 * b:2 * b + 2, :].rearrange("p a n -> p (a n)"), ps[:, 4 + b, :],
                                        vh[:, 2 * b:2 * b + 2, :].rearrange("p a n -> p (a n)").bitcast(F32),
                                        ALU.subtract).then_inc(r_v_lo, 1)

        def head_pe(pe, h, last):
            for j in range(2):
                pe.wait_ge(r_v_lo, h * 4 + 2 * (j + 1))
                t_job(pe, j, h * B_RET + (3 + j), XH, XL, 4 + 2 * j)
            pe.wait_ge(r_rope, h * 6 + 3)
            pe.wait_ge(r_y, h * 4 + 4)
            for g in range(2):
                for c in range(4):
                    mm = nc.tensor.transpose(ps[:, 2 + g, c * P:(c + 1) * P],
                                             rraw[:, 1, (4 * g + c) * P:(4 * g + c + 1) * P], ident[:])
                mm.then_inc(r_kt, 1)

            def gates_to(m0, m1):
                for m in range(m0, m1):
                    j, r = divmod(m, 24)
                    (k, pas), half = divmod(r, 3), j % 2
                    if r == 0 and half == 0:
                        pe.wait_ge(block_split, h * B_RET + (5 + j // 2))
                    if r == 0 and j >= 2:
                        pe.wait_ge(r_silu, h * 4 + (j - 1))
                    w = (wl if pas == 2 else wh)[:, j // 2, k * P:(k + 1) * P]
                    x = (XL if pas == 1 else XH)[:, k, half * HALF:(half + 1) * HALF]
                    mm = nc.tensor.matmul(ps[:, half, :], w, x, start=(r == 0), stop=(r == 23))
                    if r == 23:
                        mm.then_inc(blocks_multiplied if half else r_g_half, 1)

            def inner_and_update(c):
                at = slice(c * P, (c + 1) * P)
                if c >= 2:
                    pe.wait_ge(r_im, h * 8 + (c - 1))
                matmul3(ps[:, 2 + c % 2, 0:P], rkh[:, at], rkl[:, at], rqh[:, at], rql[:, at],
                        True, True).then_inc(r_inner, 1)
                if c < SC - 1:
                    if c >= 2:
                        pe.wait_ge(r_R, h * 7 + (c - 1))
                    matmul3(ps[:, 4 + c % 2, 0:DV], knh[:, c, :], knl[:, c, :], vh[:, c, :], vl[:, c, :],
                            True, True).then_inc(r_u, 1)

            gates_to(0, GATE_HEAD)
            pe.wait_ge(r_kn_lo, h * 2 + 2)
            pe.wait_ge(r_rl, h * 2 + 2)
            inner_and_update(0)
            for c in range(SC):
                if c + 1 < SC:
                    inner_and_update(c + 1)
                gates_to(GATE_HEAD + c * GATE_STEP, GATE_HEAD + (c + 1) * GATE_STEP)
                at = slice(c * P, (c + 1) * P)
                if c >= 2:
                    pe.wait_ge(r_oacc, h * 8 + (c - 1))
                if c >= 1:
                    pe.wait_ge(r_R_lo, h * 7 + c)
                    matmul3(ps[:, 6 + c % 2, DV:2 * DV], rqh[:, at], rql[:, at], Rh[:, (c - 1) % 2, :],
                            Rl[:, (c - 1) % 2, :], True, True)
                pe.wait_ge(r_im_lo, h * 8 + (c + 1))
                matmul3(ps[:, 6 + c % 2, 0:DV], imh[:, c % 2, :], iml[:, c % 2, :], vh[:, c, :], vl[:, c, :],
                        True, True).then_inc(r_o, 1)
            pe.wait_ge(r_R, h * 7 + 7)
            if last:
                t_job(pe, 0, B_KV + 1, XH, XL, 4)
                pe.wait_ge(r_oacc, h * 8 + 8)
                t_job(pe, 1, B_KV + 2, XH, XL, 6)
            else:
                values_pe(pe, h + 1)
            pe.wait_ge(r_im, h * 8 + 8)
            pe.wait_ge(r_silu, h * 4 + 4)
            for e in range(2):
                for q in range(2):
                    pe.wait_ge(r_xn, h * 8 + 4 * (q + 1))
                    for c in range(4):
                        mm = nc.tensor.transpose(ps[:, 2 * e + q, c * P:(c + 1) * P],
                                                 ro[:, 4 * q + c, e * P:(e + 1) * P], ident[:])
                    mm.then_inc(r_yt, 1)

        def ret_pe(pe):
            pe.wait_ge(s1_lo, 2 * SC)
            values_pe(pe, 0)
            with pe.Fori(0, RH - 1) as h:
                head_pe(pe, h, False)
            head_pe(pe, RH - 1, True)

        def silu_act(act, h, j):
            if j % 2 == 0:
                act.wait_ge(r_g_half, h * 2 + (j // 2 + 1))
            else:
                act.wait_ge(blocks_multiplied, h * B_RET + (5 + j // 2))
            nc.scalar.activation(silu_g[:, j // 2, j % 2 * HALF:(j % 2 + 1) * HALF], ps[:, j % 2, :],
                                 ACT.Silu).then_inc(r_silu, 1)

        def head_act(act, h, last):
            act.dma_start(hc[:], ret_d[bass.ds(h, 1)].rearrange("a p n -> p (a n)")).then_inc(r_hc, 16)
            for j in range(2):
                act.wait_ge(blocks_multiplied, h * B_RET + (3 + j))
                nc.scalar.activation(rraw[:, 1 - j, :], ps[:, 4 + 2 * j:6 + 2 * j, :].rearrange("p a n -> p (a n)"),
                                     ACT.Copy, scale=1.0 if j == 0 else RET_SCALE).then_inc(r_raw, 1)
                act.wait_ge(r_raw, h * 2 + (j + 1))
                if j == 1:
                    act.wait_ge(r_rope, h * 6 + 3)
                for a in range(2):
                    act.dma_start(rswp[64 * a:64 * a + 64, :], rraw[64 - 64 * a:128 - 64 * a, 1 - j, :])\
                        .then_inc(r_swp, 16)
            nc.scalar.activation(rkh[:], rraw[:, 1, :], ACT.Copy).then_inc(r_rh, 1)
            act.wait_ge(r_hc, h * 16 + 16)
            for g in range(2):
                act.wait_ge(r_kt, h * 2 + (g + 1))
                nc.scalar.activation(knh[:, 4 * g:4 * g + 4, :], ps[:, 2 + g, :].rearrange("p (c n) -> p c n", c=4),
                                     ACT.Copy, scale=dk).then_inc(r_kn_hi, 1)
            act.wait_ge(r_rope, h * 6 + 6)
            nc.scalar.activation(rqh[:], rraw[:, 0, :], ACT.Copy).then_inc(r_rh, 1)
            for c in range(SC):
                act.wait_ge(r_im, h * 8 + (c + 1))
                if c >= 2:
                    act.wait_ge(r_o, h * 8 + (c - 1))
                nc.scalar.activation(imh[:, c % 2, :], im[:, c % 2, :], ACT.Copy).then_inc(r_im_hi, 1)
                if c < SC - 1:
                    act.wait_ge(r_R, h * 7 + (c + 1))
                    if c >= 2:
                        act.wait_ge(r_o, h * 8 + c)
                    nc.scalar.activation(Rh[:, c % 2, :], R[:], ACT.Copy).then_inc(r_R_hi, 1)
                for j in range(4):
                    if GATE_OUT[j] == c:
                        silu_act(act, h, j)
                if c >= 1:
                    act.wait_ge(r_o, h * 8 + (c + 1))
                    if c >= 3:
                        act.wait_ge(r_oacc, h * 8 + (c - 1))
                    nc.scalar.activation(t2[:, c % 2, :], ps[:, 6 + c % 2, DV:2 * DV], ACT.Copy, scale=dq)\
                        .then_inc(r_t2, 1)
            for j in range(4):
                if GATE_OUT[j] >= SC:
                    silu_act(act, h, j)
            act.wait_ge(r_ve, h + 1)
            nc.scalar.activation(rsd[:], ve[:], ACT.Sqrt).then_inc(r_std, 1)
            if not last:
                values_act(act, h + 1)
            act.wait_ge(r_y, h * 4 + 8)
            act.dma_start(yr_d[bass.ds(h * 2, 2)].rearrange("a p n -> p a n"), ry[:]).then_inc(r_y_stored, 16)

        def ret_act(act):
            act.wait_ge(s1_lo, 2 * SC)
            act.dma_start(rcos[:], rope_r_d[0]).then_inc(ret_consts_loaded, 16)
            act.dma_start(rsin[:], rope_r_d[1]).then_inc(ret_consts_loaded, 16)
            values_act(act, 0)
            with act.Fori(0, RH - 1) as h:
                head_act(act, h, False)
            head_act(act, RH - 1, True)

        def head_dve(dve, h, last):
            def rope(j, row):
                dve.wait_ge(r_swp, h * 64 + 32 * (j + 1))
                nc.vector.tensor_tensor(rraw[:, row, :], rraw[:, row, :], rcos[:], ALU.mult).then_inc(r_rope, 1)
                nc.vector.tensor_tensor(rswp[:], rswp[:], rsin[:], ALU.mult).then_inc(r_rope, 1)
                dve.wait_ge(r_rope, h * 6 + (3 * j + 2))
                nc.vector.tensor_tensor(rraw[:, row, :], rraw[:, row, :], rswp[:], ALU.add).then_inc(r_rope, 1)

            rope(0, 1)
            dve.wait_ge(r_rh, h * 2 + 1)
            nc.vector.tensor_tensor(rkl[:], rraw[:, 1, :], rkh[:].bitcast(F32), ALU.subtract).then_inc(r_rl, 1)
            dve.wait_ge(r_hc, h * 16 + 16)
            for g in range(2):
                dve.wait_ge(r_kn_hi, h * 2 + (g + 1))
                nc.vector.scalar_tensor_tensor(
                    out=knl[:, 4 * g:4 * g + 4, :].rearrange("p c n -> p (c n)"), in0=ps[:, 2 + g, :], scalar=dk,
                    in1=knh[:, 4 * g:4 * g + 4, :].rearrange("p c n -> p (c n)").bitcast(F32),
                    op0=ALU.mult, op1=ALU.subtract).then_inc(r_kn_lo, 1)
            rope(1, 0)
            dve.wait_ge(r_rh, h * 2 + 2)
            nc.vector.tensor_tensor(rql[:], rraw[:, 0, :], rqh[:].bitcast(F32), ALU.subtract).then_inc(r_rl, 1)
            for c in range(SC):
                dve.wait_ge(r_inner, h * 8 + (c + 1))
                nc.vector.tensor_tensor(im[:, c % 2, :], ps[:, 2 + c % 2, 0:P], decT, ALU.mult).then_inc(r_im, 1)
                if c < SC - 1:
                    dve.wait_ge(r_u, h * 7 + (c + 1))
                    if c == 0:
                        nc.vector.tensor_copy(R[:], ps[:, 4, 0:DV]).then_inc(r_R, 1)
                    else:
                        nc.vector.scalar_tensor_tensor(out=R[:], in0=R[:], scalar=dc, in1=ps[:, 4 + c % 2, 0:DV],
                                                       op0=ALU.mult, op1=ALU.add).then_inc(r_R, 1)
                dve.wait_ge(r_im_hi, h * 8 + (c + 1))
                nc.vector.tensor_tensor(iml[:, c % 2, :], im[:, c % 2, :], imh[:, c % 2, :].bitcast(F32),
                                        ALU.subtract).then_inc(r_im_lo, 1)
                if c < SC - 1:
                    dve.wait_ge(r_R_hi, h * 7 + (c + 1))
                    nc.vector.tensor_tensor(Rl[:, c % 2, :], R[:], Rh[:, c % 2, :].bitcast(F32),
                                            ALU.subtract).then_inc(r_R_lo, 1)
                if c == 0:
                    dve.wait_ge(r_o, h * 8 + 1)
                    nc.vector.tensor_copy(ro[:, 0, :], ps[:, 6, 0:DV]).then_inc(r_oacc, 1)
                else:
                    dve.wait_ge(r_t2, h * 7 + c)
                    nc.vector.tensor_tensor(ro[:, c, :], ps[:, 6 + c % 2, 0:DV], t2[:, c % 2, :], ALU.add)\
                        .then_inc(r_oacc, 1)
                if c >= 1:
                    dve.wait_ge(r_oacc, h * 8 + c)
                    nc.vector.bn_stats(bst[:, c - 1, :], ro[:, c - 1, :]).then_inc(r_bn, 1)
            dve.wait_ge(r_oacc, h * 8 + 8)
            nc.vector.bn_stats(bst[:, 7, :], ro[:, 7, :]).then_inc(r_bn, 1)
            dve.wait_ge(r_bn, h * 8 + 8)
            nc.vector.sem_inc(dve_passed, 1)
            for c in range(SC):
                nc.vector.bn_aggr(mv[:, c, :], bst[:, c, :]).then_inc(r_mv, 1)
            dve.wait_ge(r_mv, h * 8 + 8)
            nc.vector.tensor_scalar(ve[:], mv[:, :, 1], EPS, None, ALU.add).then_inc(r_ve, 1)
            dve.wait_ge(r_std, h + 1)
            nc.vector.reciprocal(rrs[:], rsd[:]).then_inc(r_rs, 1)
            dve.wait_ge(r_rs, h + 1)
            for c in range(SC):
                nc.vector.tensor_scalar(ro[:, c, :], ro[:, c, :], mv[:, c, 0:1], rrs[:, c:c + 1],
                                        ALU.subtract, ALU.mult).then_inc(r_xn, 1)
            if not last:
                values_dve(dve, h + 1)
            dve.wait_ge(r_y_stored, h * 16 + 16)
            for e in range(2):
                for q in range(2):
                    dve.wait_ge(r_yt, h * 4 + (2 * e + q + 1))
                    at = slice(q * HALF, (q + 1) * HALF)
                    nc.vector.tensor_tensor(ry[:, e, at], ps[:, 2 * e + q, :], silu_g[:, e, at], ALU.mult)\
                        .then_inc(r_y, 1)

        def ret_dve(dve):
            nc.vector.sem_inc(r_y, 4)
            nc.vector.sem_inc(r_y_stored, 16)
            dve.wait_ge(ret_consts_loaded, 32)
            values_dve(dve, 0)
            with dve.Fori(0, RH - 1) as h:
                head_dve(dve, h, False)
            head_dve(dve, RH - 1, True)

        a_raw, a_swp, a_rope = sem("a_raw"), sem("a_swapped"), sem("a_rope")
        a_vcs, a_kcs, a_kk = sem("a_cmp_v_in"), sem("a_cmp_k_in"), sem("a_keys_placed")
        a_pad, a_mask = sem("a_pad"), sem("a_mask")
        a_hi, a_lo, a_vh, a_vl = sem("a_key_hi"), sem("a_key_lo"), sem("a_value_hi"), sem("a_value_lo")
        a_gate, a_gv = sem("a_gate"), sem("a_gate_valid")
        a_mlp, a_hb, a_hid = sem("a_mlp"), sem("a_mlp_bias"), sem("a_hidden")
        a_cmp, a_chi, a_clo = sem("a_cmp"), sem("a_cmp_hi"), sem("a_cmp_lo")
        q_swp, q_steps, q_roped, q_asm = sem("q_swapped"), sem("q_rope_steps"), sem("q_roped"), sem("q_placed")
        fill_half, fill_out, m_stored = sem("fill_half"), sem("fill_out"), sem("merge_logits_stored")
        CMPM = 2 * P
        VALID = CMPM + SC * NCMP

        def bank_of(s):
            return (s + 4) % 8

        def fixed_pe(pe):
            pe.wait_ge(r_y, 4 * RH + 4)
            t_job(pe, 0, B_KV + 3, XH, XL, 0)
            t_job(pe, 1, B_KV + 4, XH, XL, 2)
            pe.wait_ge(a_raw, 1)
            t_job(pe, 0, B_Q0 + 1, XH, XL, 4)
            for j in range(4):
                pe.wait_ge(block_split, B_VG + 1 + j)
                for k2 in range(2):
                    k = 2 * j + k2
                    for s in (2, 3, 4, 5, 6, 7, 0, 1):
                        if k == 0 and s in (2, 4, 6):
                            pe.wait_ge(a_raw, s // 2 + 1)
                        if k == 0 and s == 0:
                            pe.wait_ge(fill_out, 1)
                        at = slice(k2 * HALF, k2 * HALF + 304)
                        mm = matmul3(ps[:, bank_of(s), 0:304], XH[:, k, s * P:(s + 1) * P], XL[:, k, s * P:(s + 1) * P],
                                     wh[:, (j + 1) % 2, at], wl[:, (j + 1) % 2, at], k == 0, k == KC - 1)
                mm.then_inc(blocks_multiplied, 1)
            pe.wait_ge(att_consts_loaded, 7 * 16)
            pe.wait_ge(a_pad, 10)
            pe.wait_ge(a_vl, 1)
            pe.wait_ge(a_gate, 1)
            for t, (src, ready) in enumerate(((kcs, a_kcs), (vcs, a_vcs))):
                pe.wait_ge(ready, 64)
                for jj in range(16):
                    mm = nc.tensor.matmul(ps[:, 4 + t, 0:KV * (NCMP + 2)].rearrange("p (v n) -> p v n", v=KV),
                                          w1[:, t, jj, :], src[:, :, 2 * jj:2 * jj + POS0 + 1:16],
                                          start=(jj == 0), stop=(jj == 15))
                mm.then_inc(a_mlp, 1)
            pe.wait_ge(a_hid, 1)
            nc.tensor.matmul(ps[:, 7, 0:P], w2k[:], hid[:, 0, :], start=True, stop=True).then_inc(a_cmp, 1)
            pe.wait_ge(a_hid, 2)
            pe.wait_ge(a_vl, 2)
            pe.wait_ge(a_gate, 2)
            for v in range(KV):
                mm = nc.tensor.matmul(ps[0:NCMP, 0, v * DH:(v + 1) * DH], hid[:, 1, v * NCMP:(v + 1) * NCMP], w2v[:],
                                      start=True, stop=True)
            mm.then_inc(a_cmp, 1)

        def swap32(act, dst, src, done):
            for a in range(4):
                b = a ^ 1
                act.dma_start(dst[32 * a:32 * a + 32], src[32 * b:32 * b + 32]).then_inc(done, 16)

        def place_cmp(act, dst, src, done):
            for v in range(KV):
                act.dma_start(dst[0:64, v, 0:S], src[64 * v:64 * v + 64, :]).then_inc(done, 16)
                act.dma_start(dst[64:128, v, 0:S - 1], src[64 * v:64 * v + 64, 1:S]).then_inc(done, 16)

        def place_keys(act, br):
            for v in range(KV):
                for a in range(2):
                    act.dma_start(kk[64 * a:64 * a + 64, br, v, :].bitcast(F32), qhi[64 * v:64 * v + 64, :].bitcast(F32)).then_inc(a_kk, 16)

        def two_banks(b):
            return ps[:, b:b + 2, :].rearrange("p a n -> p (a n)")

        def fixed_act(act):
            act.wait_ge(r_y_stored, 16 * (RH + 1))
            for dst, src in ((acos[:], rope_a_d[0]), (asin[:], rope_a_d[1]), (kcs[:, 0, 0:VALID + 1], mask_d),
                             (w1[:], w1_d), (pos[:], pos_d), (w2k[:], w2k_d), (w2v[:], w2v_d)):
                act.dma_start(dst, src).then_inc(att_consts_loaded, 16)
            act.wait_ge(blocks_multiplied, B_KV + 1)
            nc.scalar.activation(fraw[:, 0, :], two_banks(4), ACT.Copy).then_inc(a_raw, 1)
            act.wait_ge(a_raw, 1)
            swap32(act, fswp, fraw[:, 0, :], a_swp)
            act.wait_ge(blocks_multiplied, B_KV + 2)
            nc.scalar.activation(fraw[:, 1, :], two_banks(6), ACT.Copy).then_inc(a_raw, 1)
            act.wait_ge(a_raw, 2)
            place_cmp(act, vcs, fraw[:, 1, :], a_vcs)
            act.wait_ge(a_rope, 3)
            act.wait_ge(a_mask, 1)
            place_cmp(act, kcs, fraw[:, 0, :], a_kcs)
            act.wait_ge(blocks_multiplied, B_KV + 3)
            act.wait_ge(a_kcs, 64)
            nc.scalar.activation(fraw[:, 0, :], two_banks(0), ACT.Copy).then_inc(a_raw, 1)
            act.wait_ge(a_raw, 3)
            swap32(act, fswp, fraw[:, 0, :], a_swp)
            act.wait_ge(blocks_multiplied, B_KV + 4)
            act.wait_ge(a_vcs, 64)
            nc.scalar.activation(fraw[:, 1, :], two_banks(2), ACT.Copy).then_inc(a_raw, 1)
            act.wait_ge(a_rope, 6)
            nc.scalar.activation(qhi[:], fraw[:, 0, :], ACT.Copy).then_inc(a_hi, 1)
            act.wait_ge(a_raw, 4)
            swap32(act, fswp, fraw[:, 1, :], a_swp)
            act.wait_ge(a_hi, 1)
            act.wait_ge(a_lo, 1)
            act.wait_ge(blocks_multiplied, B_Q0 + 1)
            nc.scalar.activation(fraw[:, 0, :], two_banks(4), ACT.Copy).then_inc(fill_out, 1)
            place_keys(act, 0)
            act.wait_ge(fill_out, 1)
            swap32(act, swp, fraw[:, 0, :], q_swp)
            act.wait_ge(a_rope, 9)
            act.wait_ge(a_kk, 64)
            nc.scalar.activation(qhi[:], fraw[:, 1, :], ACT.Copy).then_inc(a_hi, 1)
            act.wait_ge(a_hi, 2)
            act.wait_ge(a_lo, 2)
            place_keys(act, 1)
            act.wait_ge(a_kk, 128)
            act.wait_ge(q_steps, 3)
            nc.scalar.activation(qhi[:], fraw[:, 0, :], ACT.Copy).then_inc(q_steps, 1)
            act.wait_ge(q_roped, 1)
            place_q(act, 0)
            act.wait_ge(blocks_multiplied, B_VG + 4)
            for g, b in ((0, 4), (1, 0)):
                nc.scalar.activation(V[:, 4 * g:4 * g + 4, :, 0, :], ps[:, b:b + 4, 0:256].rearrange("p s (m d) -> p s m d", m=4),
                                     ACT.Copy).then_inc(a_vh, 1)
            for g, b in ((0, 4), (1, 0)):
                act.wait_ge(a_vl, g + 1)
                nc.scalar.activation(gates[:, 4 * g:4 * g + 4, :], ps[:, b:b + 4, 256:304], ACT.Sigmoid)\
                    .then_inc(a_gate, 1)
            for t in range(2):
                act.wait_ge(a_mlp, t + 1)
                nc.scalar.activation(hb[:, t:t + 1], ps[:, 4 + t, NCMP + 1:NCMP + 2], ACT.Copy).then_inc(a_hb, 1)
                act.wait_ge(a_hb, t + 1)
                nc.scalar.activation(hid[:, t, :].rearrange("p (v n) -> p v n", v=KV),
                                     ps[:, 4 + t, 0:KV * (NCMP + 2)].rearrange("p (v n) -> p v n", v=KV)[:, :, 0:NCMP],
                                     ACT.Gelu_apprx_tanh, bias=hb[:, t:t + 1])\
                    .then_inc(a_hid, 1)
            act.wait_ge(a_cmp, 1)
            nc.scalar.activation(kch[:].rearrange("p v n -> p (v n)"), ps[:, 7, 0:P], ACT.Copy).then_inc(a_chi, 1)
            act.wait_ge(a_cmp, 2)
            nc.scalar.activation(vc[0:NCMP, :, 0, :], ps[0:NCMP, 0, 0:P].rearrange("p (v n) -> p v n", v=KV), ACT.Copy)\
                .then_inc(a_chi, 1)

        def rope_dve(x, y, count):
            nc.vector.tensor_tensor(x, x, acos[:], ALU.mult).then_inc(a_rope, 1)
            nc.vector.tensor_tensor(y, y, asin[:], ALU.mult).then_inc(a_rope, 1)
            nc.vector.wait_ge(a_rope, count + 2)
            nc.vector.tensor_tensor(x, x, y, ALU.add).then_inc(a_rope, 1)

        def fixed_dve(dve):
            dve.wait_ge(att_consts_loaded, 7 * 16)
            for t in (kcs, vcs):
                nc.vector.memset(t[0:64, :, S:S + 16], 0.0).then_inc(a_pad, 1)
                nc.vector.memset(t[64:128, :, S - 1:S + 16], 0.0).then_inc(a_pad, 1)
            for t, src in enumerate((kcs, vcs)):
                for v in range(KV):
                    nc.vector.tensor_copy(src[:, v, POS0:POS0 + 32:2], pos[:, t, :]).then_inc(a_pad, 1)
            for part in range(2):
                nc.vector.memset(vc[64:128, :, part, :].bitcast(F32), 0.0).then_inc(a_pad, 1)
            nc.vector.tensor_copy(maskr[:], kcs[:, 0, 0:VALID + 1]).then_inc(a_mask, 1)
            nc.vector.tensor_copy(identr[:], ident[:]).then_inc(a_mask, 1)
            dve.wait_ge(a_swp, 64)
            rope_dve(fraw[:, 0, :], fswp[:], 0)
            dve.wait_ge(a_swp, 128)
            rope_dve(fraw[:, 0, :], fswp[:], 3)
            dve.wait_ge(a_hi, 1)
            nc.vector.tensor_tensor(kl[:, 0, :], fraw[:, 0, :], qhi[:].bitcast(F32), ALU.subtract).then_inc(a_lo, 1)
            dve.wait_ge(a_swp, 192)
            rope_dve(fraw[:, 1, :], fswp[:], 6)
            dve.wait_ge(a_hi, 2)
            nc.vector.tensor_tensor(kl[:, 1, :], fraw[:, 1, :], qhi[:].bitcast(F32), ALU.subtract).then_inc(a_lo, 1)
            dve.wait_ge(q_swp, 64)
            nc.vector.tensor_tensor(fraw[:, 0, :], fraw[:, 0, :], acos[:], ALU.mult).then_inc(q_steps, 1)
            nc.vector.tensor_tensor(swp, swp, asin[:], ALU.mult).then_inc(q_steps, 1)
            dve.wait_ge(q_steps, 2)
            nc.vector.tensor_tensor(fraw[:, 0, :], fraw[:, 0, :], swp, ALU.add).then_inc(q_steps, 1)
            dve.wait_ge(q_steps, 4)
            nc.vector.tensor_tensor(qlo[:], fraw[:, 0, :], qhi[:].bitcast(F32), ALU.subtract).then_inc(q_roped, 1)
            for g, b in ((0, 4), (1, 0)):
                dve.wait_ge(a_vh, g + 1)
                for s in range(4 * g, 4 * g + 4):
                    done = nc.vector.tensor_tensor(V[:, s, :, 1, :], ps[:, b + s % 4, 0:256].rearrange("p (m d) -> p m d", m=4),
                                                   V[:, s, :, 0, :].bitcast(F32), ALU.subtract)
                done.then_inc(a_vl, 1)
            dve.wait_ge(a_gate, 2)
            first = gates[:, 0, :].rearrange("p (m b) -> p m b", b=3)[:, :, 0]
            nc.vector.tensor_scalar(first, first, maskr[:, VALID:VALID + 1].bitcast(F32), None, ALU.mult).then_inc(a_gv, 1)
            dve.wait_ge(a_chi, 1)
            nc.vector.tensor_tensor(kcl[:].rearrange("p v n -> p (v n)"), ps[:, 7, 0:P],
                                    kch[:].rearrange("p v n -> p (v n)").bitcast(F32), ALU.subtract).then_inc(a_clo, 1)
            dve.wait_ge(a_chi, 2)
            nc.vector.tensor_tensor(vc[0:NCMP, :, 1, :], ps[0:NCMP, 0, 0:P].rearrange("p (v n) -> p v n", v=KV),
                                    vc[0:NCMP, :, 0, :].bitcast(F32), ALU.subtract)\
                .then_inc(a_clo, 1)
            nc.vector.memset(Pw[:, :, 5 * P + NCMP:6 * P], 0.0).then_inc(a_pad, 1)

        UNITS = 2 * SC
        GROUPS = [groups_of(u // 2) for u in range(UNITS)]
        GOFF = [sum(len(g) for g in GROUPS[:u]) for u in range(UNITS + 1)]
        NG = GOFF[-1]
        FILL = 3 * 48
        BR = {"cmp": 0, "sel": 1, "win": 2}
        UNIT_OF = [u_ for u_ in range(UNITS) for _ in GROUPS[u_]]
        WIN0 = [len([g_ for g_ in GROUPS[u_] if g_[0][0] == "sel"]) for u_ in range(UNITS)]
        assert NG % 2 == 0
        SHARE = [9 - 1.7 * len(g_) for gs in GROUPS for g_ in gs]
        FILL_TO, FILL_AT = [], []
        for s_ in range(NG):
            last_ = FILL_TO[-1] if s_ else 0
            want_ = int((FILL - 24) * sum(SHARE[:s_ + 1]) / sum(SHARE) + 0.5)
            FILL_TO.append(min(want_, (last_ // 24 + 1) * 24))
            if FILL_TO[-1] % 24 == 0 and FILL_TO[-1] > last_:
                FILL_AT.append(s_)
        assert len(FILL_AT) == 5 and FILL_AT[-1] < NG and FILL_TO[-1] == FILL - 24
        GATED_AT = [GOFF[u_ + 1] + 1 for u_ in range(UNITS)]
        Y_AT = [GOFF[2 * q_ + 2] + 2 for q_ in range(SC)]
        TURNS = []
        for s_ in range(NG):
            TURNS += [("g", s_)] + ([("y", Y_AT.index(s_))] if s_ in Y_AT else [])
        TURNS.append(("y", SC - 1))
        assert len(TURNS) % 2 == 0
        O_BANK, F_BANK, T_BANK = 6, 7, 4

        att_s, att_mx, att_nm, att_exp = sem("att_scores"), sem("att_max"), sem("att_neg_max"), sem("att_exp")
        att_tr, att_hi, att_lo, att_pv = sem("att_turned"), sem("att_pt_hi"), sem("att_pt_lo"), sem("att_pv")
        att_c, att_og, att_y = sem("att_weights"), sem("att_gated_sem"), sem("att_y_rows")
        att_yt, att_yc, y_stored = sem("att_y_turned"), sem("att_y_copied"), sem("y_att_stored")

        def fill_pe(pe, base, done, slot0, m0, m1):
            for m in range(m0, m1):
                blk, half, r = m // 48, m // 24 % 2, m % 24
                k, pas = divmod(r, 3)
                slot = (slot0 + blk) % 2
                if r == 0:
                    if half == 0:
                        pe.wait_ge(block_split, base + (blk + 1))
                    pe.wait_ge(fill_out, done + (2 * blk + half))
                w = (wl if pas == 2 else wh)[:, slot, k * P:(k + 1) * P]
                x = (XL if pas == 1 else XH)[:, k, half * HALF:(half + 1) * HALF]
                mm = nc.tensor.matmul(ps[:, F_BANK, :], w, x, start=(r == 0), stop=(r == 23))
                if r == 23:
                    mm.then_inc(blocks_multiplied if half else fill_half, 1)

        def scores_pe(pe, n, kv0, u, part):
            kv, (qi, h) = (kv0 + u // UNITS) % KV, divmod(u % UNITS, 2)
            q2 = qst[kv][:, h, qi * P:(qi + 1) * P]
            own = slice(64 * kv, 64 * kv + 64)
            q1 = qst[kv][own, h, qi * P:(qi + 1) * P]

            def block(out, k_hi, k_lo, masks):
                nc.tensor.matmul(out, q2, k_hi, start=True, stop=False)
                for col, w, m in masks:
                    nc.tensor.matmul(out[:, col:col + w], identr[:], m, start=False, stop=False)
                return nc.tensor.matmul(out, q1, k_lo, start=False, stop=True)

            diag, edge = maskr[:, 0:P], maskr[:, P:2 * P]
            if u >= 1:
                pe.wait_ge(att_exp, n * 48 + (3 * u - 2 if part == 0 else 3 * u))
            if part == 0:
                for g in range(qi // 4 + 1):
                    a, b = g * HALF, min((g + 1) * HALF, (qi + 1) * P)
                    mm = block(ps[:, g, 0:b - a], kk[:, 0, kv, a:b], kl[own, 0, a:b],
                               [(qi % 4 * P, P, diag)] if g == qi // 4 else [])
                mm.then_inc(att_s, 1)
                return
            lo = max(0, qi - 4)
            nb = qi - lo + 1
            for g in range((nb + 3) // 4):
                a, b = (lo + 4 * g) * P, (lo + min(nb, 4 * g + 4)) * P
                masks = [(0, P, edge)] if qi >= 4 and g == 0 else []
                if g == (nb - 1) // 4:
                    masks.append(((nb - 1) % 4 * P, P, diag))
                block(ps[:, 2 + g, 0:b - a], kk[:, 1, kv, a:b], kl[own, 1, a:b], masks)
            block(ps[:, 3, P:P + NCMP], kch[:, kv, :], kcl[own, kv, :],
                  [(0, NCMP, maskr[:, CMPM + qi * NCMP:CMPM + (qi + 1) * NCMP])]).then_inc(att_s, 1)

        def bank_free(pe, n, turn):
            if turn >= 2:
                kind, i = TURNS[turn - 2]
                if kind == "g":
                    pe.wait_ge(att_lo, n * NG + (i + 1))
                else:
                    pe.wait_ge(att_yc, n * SC + (i + 2))
            if turn == 1:
                pe.wait_ge(att_yc, n * SC + 1)

        def turn_pe(pe, n, s):
            u = UNIT_OF[s]
            group = GROUPS[u][s - GOFF[u]]
            turn = TURNS.index(("g", s))
            pe.wait_ge(att_exp, n * 48 + (3 * u + (1 if group[0][0] == "sel" else 3)))
            bank_free(pe, n, turn)
            for j, (kind, _, col) in enumerate(group):
                probs = Ps if kind == "sel" else Pw
                mm = nc.tensor.transpose(ps[:, T_BANK + turn % 2, j * P:(j + 1) * P],
                                         probs[:, u % 2, col:col + P], ident[:])
            mm.then_inc(att_tr, 1)

        def pv_pe(pe, n, kv, s):
            u = UNIT_OF[s]
            qi, h = divmod(u, 2)
            if s == GOFF[u] and u >= 1:
                pe.wait_ge(att_og, n * UNITS + u)
            pe.wait_ge(att_lo, n * NG + (s + 1))
            last_kb = {"sel": qi, "win": qi, "cmp": None}
            for j, (kind, kb, _) in enumerate(GROUPS[u][s - GOFF[u]]):
                first = kind == "cmp" or kb == (0 if kind == "sel" else max(0, qi - 4))
                out = ps[:, O_BANK, BR[kind] * P:(BR[kind] + 1) * P]
                v = vc[:, kv] if kind == "cmp" else V[:, kb, (BR[kind] - 1) * KV + kv]
                nc.tensor.matmul(out, PTh[:, s % 3, j * P:(j + 1) * P], v.rearrange("p t d -> p (t d)"),
                                 start=first, stop=False)
                mm = nc.tensor.matmul(out[:, 0:DH], PTl[:, s % 3, j * P:(j + 1) * P], v[:, 0, :],
                                      start=False, stop=kb == last_kb[kind])
            mm.then_inc(att_pv, 1)

        def y_pe(pe, n, qi):
            turn = TURNS.index(("y", qi))
            pe.wait_ge(att_y, n * UNITS + (2 * qi + 2))
            bank_free(pe, n, turn)
            nc.tensor.transpose(ps[:, T_BANK + turn % 2, 0:P], yn[:, qi % 2, :], ident[:]).then_inc(att_yt, 1)

        def att_pe(pe):
            fixed_pe(pe)
            pe.wait_ge(a_clo, 2)
            pe.wait_ge(a_mask, 2)
            pe.wait_ge(a_kk, 128)
            pe.wait_ge(a_lo, 2)
            pe.wait_ge(a_pad, 11)
            pe.wait_ge(q_asm, 64)
            for part in range(2):
                scores_pe(pe, 0, 0, 0, part)
            with pe.Fori(0, PAIRS // 2) as i:
                for kv in range(KV):
                    n = i * 2 + kv

                    def fill(m0, m1):
                        fill_pe(pe, n * 3 + B_PAIR, n * 6 + 2, (B_PAIR + 3 * kv) % 2, m0, m1)

                    for s in range(NG):
                        u = UNIT_OF[s]
                        g = s - GOFF[u]
                        turn_pe(pe, n, s)
                        if g == 0:
                            if u == UNITS - 1:
                                pe.wait_ge(q_asm, n * 64 + 128)
                            scores_pe(pe, n, kv, u + 1, 0)
                        if g == WIN0[u]:
                            scores_pe(pe, n, kv, u + 1, 1)
                        if s >= 2:
                            pv_pe(pe, n, kv, s - 2)
                        fill(FILL_TO[s - 1] if s else 0, FILL_TO[s])
                        if s in Y_AT:
                            y_pe(pe, n, Y_AT.index(s))
                    pv_pe(pe, n, kv, NG - 2)
                    fill(FILL - 24, FILL - 12)
                    pv_pe(pe, n, kv, NG - 1)
                    fill(FILL - 12, FILL)
                    y_pe(pe, n, SC - 1)

        def fill_act(act, n, j):
            blk, half = divmod(j, 2)
            at = slice(half * HALF, (half + 1) * HALF)
            if half == 0:
                act.wait_ge(fill_half, n * 3 + (blk + 1))
            else:
                act.wait_ge(blocks_multiplied, n * 3 + (B_PAIR + blk + 1))
            if blk == 0:
                if half == 0:
                    act.wait_ge(q_roped, n + 1)
                nc.scalar.activation(raw[:, at], ps[:, F_BANK, :], ACT.Copy).then_inc(fill_out, 1)
            else:
                act.wait_ge(m_stored, n * 64 + 16 * (2 * (blk - 1) + half + 1))
                nc.scalar.activation(fm[:], ps[:, F_BANK, :], ACT.Copy).then_inc(fill_out, 1)

        def store_gate_sp(sp, n, blk, half):
            sp.wait_ge(fill_out, n * 6 + (2 * blk + half + 3))
            sp.dma_start(ml_d[bass.ds(n + (KC if blk == 2 else 0), 1), :, half * HALF:(half + 1) * HALF]
                         .rearrange("a p n -> p (a n)"), fm[:]).then_inc(m_stored, 16)

        def att_sp(sp):
            with sp.Fori(0, PAIRS // 2) as i:
                for kv in range(KV):
                    n = i * 2 + kv

                    def load(j):
                        b = B_PAIR + 3 + 3 * kv + j
                        sp.wait_ge(block_split, i * 6 + (b - 1))
                        sp.dma_start(wraw[:, b % 2, :], wst_d[bass.ds(i * 6 + b, 1)].rearrange("a p n -> p (a n)"))\
                            .then_inc(block_loaded[b % 2], 16)

                    load(0)
                    sp.wait_ge(fill_out, n * 6 + 4)
                    sp.wait_ge(q_asm, n * 64 + 64)
                    swap32(sp, swp, raw, q_swp)
                    load(1)
                    store_gate_sp(sp, n, 1, 0)
                    sp.wait_ge(q_roped, n + 2)
                    place_q(sp, 1 - kv)
                    store_gate_sp(sp, n, 1, 1)
                    load(2)
                    store_gate_sp(sp, n, 2, 0)
                    store_gate_sp(sp, n, 2, 1)
                    sp.wait_ge(att_yc, n * SC + (SC + 1))
                    sp.dma_start(ya_d[bass.ds(n, 1)].rearrange("a p n -> p (a n)"), yT[:]).then_inc(y_stored, 16)

        def exp_act(act, n, u, part):
            qi = u % UNITS // 2

            def exp(kind, out, src):
                b = BR[kind]
                nc.scalar.activation(out, src, ACT.Exp, bias=nm[:, u % 2, b:b + 1], scale=ATT_SCALE,
                                     accum_out=ls[:, u % 2, b:b + 1]).then_inc(att_exp, 1)

            if part == 0:
                act.wait_ge(att_nm, n * 32 + (2 * u + 1))
                exp("sel", Ps[:, u % 2, 0:(qi + 1) * P], two_banks(0)[:, 0:(qi + 1) * P])
            else:
                act.wait_ge(att_nm, n * 32 + (2 * u + 2))
                w = (min(qi, 4) + 1) * P
                exp("win", Pw[:, u % 2, 0:w], two_banks(2)[:, 0:w])
                exp("cmp", Pw[:, u % 2, 5 * P:5 * P + NCMP], ps[:, 3, P:P + NCMP])

        def hi_act(act, n, s):
            u = UNIT_OF[s]
            w = len(GROUPS[u][s - GOFF[u]]) * P
            act.wait_ge(att_tr, n * NG + (s + 1))
            if s >= 3:
                act.wait_ge(att_pv, n * NG + (s - 2))
            nc.scalar.activation(PTh[:, s % 3, 0:w], ps[:, T_BANK + TURNS.index(("g", s)) % 2, 0:w], ACT.Copy).then_inc(att_hi, 1)

        def y_act(act, n, qi):
            act.wait_ge(att_yt, n * SC + (qi + 1))
            if qi == 0:
                act.wait_ge(y_stored, n * 16 + 16)
            nc.scalar.activation(yT[:, qi * P:(qi + 1) * P], ps[:, T_BANK + TURNS.index(("y", qi)) % 2, 0:P], ACT.Copy)\
                .then_inc(att_yc, 1)

        def place_q(act, turn):
            for h in range(2):
                for a, part in ((64 * turn, qhi), (64 - 64 * turn, qlo)):
                    act.dma_start(qst[turn][a:a + 64, h, :].bitcast(F32),
                                  part[64 * h:64 * h + 64, :].bitcast(F32)).then_inc(q_asm, 16)

        def att_act(act):
            fixed_act(act)
            nc.scalar.sem_inc(m_stored, 16)
            nc.scalar.sem_inc(y_stored, 16)
            nc.scalar.sem_inc(fill_out, 1)
            nc.scalar.sem_inc(att_yc, 1)
            act.wait_ge(a_pad, 11)
            for part in range(2):
                exp_act(act, 0, 0, part)
            with act.Fori(0, PAIRS // 2) as i:
                for kv in range(KV):
                    n = i * 2 + kv
                    for s in range(NG):
                        u = UNIT_OF[s]
                        g = s - GOFF[u]
                        if s - 1 in FILL_AT:
                            fill_act(act, n, FILL_AT.index(s - 1))
                        if s - 1 in Y_AT:
                            y_act(act, n, Y_AT.index(s - 1))
                        hi_act(act, n, s)
                        if g == 0 and u >= 1 and len(GROUPS[u - 1]) - 1 == WIN0[u - 1]:
                            exp_act(act, n, u, 1)
                        if g == 1:
                            exp_act(act, n, u + 1, 0)
                        if g > WIN0[u] and g == len(GROUPS[u]) - 1:
                            exp_act(act, n, u + 1, 1)
                    if FILL_AT[-1] == NG - 1:
                        fill_act(act, n, 4)
                    fill_act(act, n, 5)
                    y_act(act, n, SC - 1)

        def max_dve(dve, n, u, part):
            qi = u % UNITS // 2
            p = u % 2
            if part == 0:
                dve.wait_ge(att_s, n * 32 + (2 * u + 1))
                nc.vector.reduce_max(mx[:, p, 1:2], two_banks(0)[:, 0:(qi + 1) * P], AX.X).then_inc(att_mx, 1)
                dve.wait_ge(att_mx, n * 48 + (3 * u + 1))
                nc.vector.tensor_scalar(nm[:, p, 1:2], mx[:, p, 1:2], -ATT_SCALE, None, ALU.mult).then_inc(att_nm, 1)
            else:
                w = (min(qi, 4) + 1) * P
                dve.wait_ge(att_s, n * 32 + (2 * u + 2))
                nc.vector.reduce_max(mx[:, p, 2:3], two_banks(2)[:, 0:w], AX.X).then_inc(att_mx, 1)
                nc.vector.reduce_max(mx[:, p, 0:1], ps[:, 3, P:P + NCMP], AX.X).then_inc(att_mx, 1)
                dve.wait_ge(att_mx, n * 48 + (3 * u + 3))
                nc.vector.tensor_scalar(nm[:, p, 0:3:2], mx[:, p, 0:3:2], -ATT_SCALE, None, ALU.mult)\
                    .then_inc(att_nm, 1)

        def lo_dve(dve, n, s):
            u = UNIT_OF[s]
            w = len(GROUPS[u][s - GOFF[u]]) * P
            dve.wait_ge(att_hi, n * NG + (s + 1))
            nc.vector.tensor_tensor(PTl[:, s % 3, 0:w], ps[:, T_BANK + TURNS.index(("g", s)) % 2, 0:w],
                                    PTh[:, s % 3, 0:w].bitcast(F32), ALU.subtract).then_inc(att_lo, 1)

        def weights_dve(dve, n, i, kv, u):
            qi, h = divmod(u, 2)
            dve.wait_ge(att_exp, n * 48 + (3 * u + 3))
            nc.vector.tensor_scalar(lm[:, u % 2, :], ls[:, u % 2, :], 1e-30, None, ALU.max).then_inc(att_c, 1)
            dve.wait_ge(att_c, n * 48 + (3 * u + 1))
            nc.vector.reciprocal(li[:, u % 2, :], lm[:, u % 2, :]).then_inc(att_c, 1)
            dve.wait_ge(att_c, n * 48 + (3 * u + 2))
            nc.vector.tensor_tensor(rg[:, u % 2, :], li[:, u % 2, :],
                                    gates[:, qi, bass.ds(i * 12 + (6 * kv + 3 * h), 3)], ALU.mult).then_inc(att_c, 1)

        def gated_dve(dve, n, u):
            qi, h = divmod(u, 2)
            dve.wait_ge(att_pv, n * NG + GOFF[u + 1])
            dve.wait_ge(att_c, n * 48 + (3 * u + 3))
            nc.vector.tensor_tensor(og[:], ps[:, O_BANK, 0:3 * P].rearrange("p (c d) -> p c d", c=3),
                                    rg[:, u % 2, :].unsqueeze(2).to_broadcast([P, 3, P]), ALU.mult).then_inc(att_og, 1)
            dve.wait_ge(att_og, n * UNITS + (u + 1))
            nc.vector.tensor_reduce(yn[:, qi % 2, h * DH:(h + 1) * DH], og[:].rearrange("p b (t d) -> p d (b t)", t=2), AX.X, ALU.add)\
                .then_inc(att_y, 1)

        def att_dve(dve):
            fixed_dve(dve)
            dve.wait_ge(a_gv, 1)
            for part in range(2):
                max_dve(dve, 0, 0, part)
            with dve.Fori(0, PAIRS // 2) as i:
                for kv in range(KV):
                    n = i * 2 + kv
                    for s in range(NG):
                        u = UNIT_OF[s]
                        g = s - GOFF[u]
                        lo_dve(dve, n, s)
                        if s in GATED_AT:
                            gated_dve(dve, n, GATED_AT.index(s))
                        if g == 0:
                            max_dve(dve, n, u + 1, 0)
                        if g == WIN0[u]:
                            max_dve(dve, n, u + 1, 1)
                            weights_dve(dve, n, i, kv, u)
                    gated_dve(dve, n, UNITS - 1)

        def rope_pool(pool, r):
            tt = nc.gpsimd.tensor_tensor
            pool.wait_ge(q_swp, r * 64 + 64)
            tt(raw[:], raw[:], acos[:], ALU.mult).then_inc(q_steps, 1)
            tt(swp, swp, asin[:], ALU.mult).then_inc(q_steps, 1)
            pool.wait_ge(q_steps, r * 4 + 2)
            tt(raw[:], raw[:], swp, ALU.add).then_inc(q_steps, 1)
            pool.wait_ge(q_steps, r * 4 + 3)

        def rope_pool_split(pool, r):
            tt = nc.gpsimd.tensor_tensor
            tt(qhi[:], raw[:], zero[:].to_broadcast([P, S]), ALU.add).then_inc(q_steps, 1)
            pool.wait_ge(q_steps, r * 4 + 4)
            tt(qlo[:], raw[:], qhi[:].bitcast(F32), ALU.subtract).then_inc(q_roped, 1)

        def att_pool(pool, split):
            pool.wait_ge(att_consts_loaded, 7 * 16)
            pool.wait_ge(a_kk, 128)
            with pool.Fori(0, PAIRS // 2) as i:
                for kv in range(KV):
                    n = i * 2 + kv
                    for j in range(3):
                        if j == 2:
                            rope_pool(pool, n + 1)
                            pool.wait_ge(q_asm, n * 64 + 64)
                            rope_pool_split(pool, n + 1)
                        b = B_PAIR + 1 + 3 * kv + j
                        split(b % 2, i * 6 + b, i * 3 + (b // 2 + 1))
        m_ld = [sem("y_att_loaded0"), sem("y_att_loaded1")]
        m_hi, m_lo = sem("m_y_hi"), sem("m_y_lo")
        mt_ld = [sem("gate_loaded0"), sem("gate_loaded1")]
        m_gate, m_out, m_sum = sem("m_gate"), sem("m_out"), sem("m_sum")
        x_hi, x_lo = sem("mix_hi_done"), sem("mix_lo_done")

        def merge_pe(pe):
            for xh, xl, b0, ready in ((YH, YL, B_WB, 0), (XH, XL, B_WA, KC)):
                pe.wait_ge(m_lo, ready + 1)
                with pe.Fori(0, 2) as i:
                    for j in range(4):
                        pe.wait_ge(m_out, i * 4 + (ready + j + 1))
                        if j == 0:
                            pe.wait_ge(block_split, i * 4 + (b0 + 1))
                        merge_job(pe, (b0 + j) % 2, i * 4 + (b0 + j + 1), xh, xl, 2 * j, ready)

        def merge_job(pe, slot, n, xh, xl, bank, ready):
            pe.wait_ge(block_split, n)
            for k in range(KC):
                pe.wait_ge(m_lo, ready + k + 1)
                w_h, w_l = wh[:, slot, k * P:(k + 1) * P], wl[:, slot, k * P:(k + 1) * P]
                for w, x in ((w_h, xh), (w_h, xl), (w_l, xh)):
                    for half in range(2):
                        mm = nc.tensor.matmul(ps[:, bank + half, :], w, x[:, k, half * HALF:(half + 1) * HALF],
                                              start=(k == 0 and w is w_h and x is xh),
                                              stop=(k == KC - 1 and w is w_l))
            mm.then_inc(blocks_multiplied, 1)

        def load_ret_sp(sp):
            sp.wait_ge(att_s, PAIRS * 32 + 2)
            sp.wait_ge(q_roped, PAIRS + 1)
            sp.wait_ge(r_y_stored, 16 * (RH + 1))
            for k in range(KC):
                sp.dma_start(x2[:, k, :], yr_d[k]).then_inc(chunk_loaded[k], 16)

        def merge_act(act):
            act.wait_ge(q_asm, (PAIRS + 1) * 64)

            def load_y(k):
                if k >= 2:
                    act.wait_ge(m_lo, KC + k - 1)
                act.dma_start(ring2[:, k % 2, :], ya_d[k]).then_inc(m_ld[k % 2], 16)

            def split_y(k):
                if k < KC:
                    act.wait_ge(chunk_loaded[k], 32)
                    nc.scalar.activation(YH[:, k, :], x2[:, k, :], ACT.Copy).then_inc(m_hi, 1)
                    return
                k -= KC
                act.wait_ge(m_ld[k % 2], 16 * (k // 2 + 1))
                nc.scalar.activation(XH[:, k, :], ring2[:, k % 2, :], ACT.Copy).then_inc(m_hi, 1)
                if k + 2 < KC:
                    load_y(k + 2)

            def load_gate(n):
                if n >= 2:
                    act.wait_ge(m_out, 4 + n - 1)
                act.dma_start(mt[:, n % 2, :], ml_d[n]).then_inc(mt_ld[n % 2], 16)

            for k in range(2):
                split_y(k)
            act.wait_ge(m_stored, (4 * PAIRS + 1) * 16)
            load_gate(0)
            load_gate(1)
            act.wait_ge(y_stored, (PAIRS + 1) * 16)
            load_y(0)
            load_y(1)
            for k in range(2, KC):
                split_y(k)
            for n in range(2 * KC):
                act.wait_ge(mt_ld[n % 2], 16 * (n // 2 + 1))
                nc.scalar.activation(mt[:, n % 2, :], mt[:, n % 2, :], ACT.Sigmoid).then_inc(m_gate, 1)
                if n < KC:
                    split_y(KC + n)
                else:
                    act.wait_ge(m_sum, n - KC + 1)
                    nc.scalar.activation(YH[:, n - KC, :], x2[:, n - KC, :], ACT.Copy).then_inc(x_hi, 1)
                if n + 2 < 2 * KC:
                    load_gate(n + 2)
            out_act(act)

        def merge_dve(dve):
            nc.vector.sem_inc(m_out, 4)

            def split_y(k):
                dve.wait_ge(m_hi, k + 1)
                hi, lo, src = (YH, YL, x2[:, k, :]) if k < KC else (XH, XL, ring2[:, k % 2, :])
                nc.vector.tensor_tensor(lo[:, k % KC, :], src, hi[:, k % KC, :].bitcast(F32),
                                        ALU.subtract).then_inc(m_lo, 1)

            for k in range(KC):
                split_y(k)
            for n in range(2 * KC):
                if n < KC:
                    split_y(KC + n)
                dve.wait_ge(m_gate, n + 1)
                dve.wait_ge(blocks_multiplied, B_WB + n + 1)
                if n < KC:
                    nc.vector.tensor_tensor(x2[:, n, :], two_banks(2 * (n % 4)), mt[:, n % 2, :], ALU.mult)\
                        .then_inc(m_out, 1)
                    continue
                k = n - KC
                if k >= 1:
                    dve.wait_ge(m_sum, k)
                nc.vector.tensor_tensor(tmp[:], two_banks(2 * (n % 4)), mt[:, n % 2, :], ALU.mult).then_inc(m_out, 1)
                dve.wait_ge(m_out, 4 + n + 1)
                nc.vector.tensor_tensor(x2[:, k, :], x2[:, k, :], tmp[:], ALU.add).then_inc(m_sum, 1)
                dve.wait_ge(x_hi, k + 1)
                nc.vector.tensor_tensor(YL[:, k, :], x2[:, k, :], YH[:, k, :].bitcast(F32), ALU.subtract)\
                    .then_inc(x_lo, 1)
            out_dve(dve)

        o_out, o_done, o_gain = sem("o_out"), sem("o_rows_done"), sem("o_gains_loaded")
        o_sq, o_sq2, o_scaled, o_ss = sem("o_sq_left"), sem("o_sq_right"), sem("o_scaled"), sem("o_sq_added")
        o_ms, o_rms, o_rstd, o_x2 = sem("o_ms"), sem("o_rms"), sem("o_rstd"), sem("o_x_mid")
        p_sq, p_ms, p_rms, p_rstd = sem("p_sq"), sem("p_ms"), sem("p_rms"), sem("p_rstd")
        p_xn, p_tr, p_hi, p_lo = sem("p_xn"), sem("p_tr"), sem("p_hi"), sem("p_lo")
        FREE_T = 4

        def x_rows(s):
            return ring2[:, s, :] if s < 2 else acc[:, s, :]

        def out_pe(pe):
            for nh in range(2):
                for j in range(4):
                    b = B_WO + 4 * nh + j
                    pe.wait_ge(block_split, b + 1)
                    for k2 in range(2):
                        k = 2 * j + k2
                        if nh == 0:
                            pe.wait_ge(x_lo, k + 1)
                        for s in range(SC):
                            if nh == 0 and k == 0 and s % 2 == 0:
                                pe.wait_ge(m_out, 4 + 2 * KC - 3 + s // 2)
                            if nh == 1 and k == 0:
                                pe.wait_ge(o_out, s + 1)
                            at = slice(k2 * HALF, (k2 + 1) * HALF)
                            mm = matmul3(ps[:, s, :], YH[:, k, s * P:(s + 1) * P], YL[:, k, s * P:(s + 1) * P],
                                         wh[:, b % 2, at], wl[:, b % 2, at], k == 0, k == KC - 1)
                            if nh == 1 and k == KC - 1 and s < SC - 1:
                                mm.then_inc(o_done, 1)
                    mm.then_inc(blocks_multiplied, 1)

        def out_act(act):
            act.wait_ge(m_out, 4 + 2 * KC)
            act.dma_start(mt[:, 0, :], norm_d[1]).then_inc(o_gain, 16)
            act.dma_start(mt[:, 1, :], norm_d[2]).then_inc(o_gain, 16)
            act.wait_ge(m_lo, 2 * KC)
            for s in range(2):
                act.dma_start(x_rows(s), x_d[s * P:(s + 1) * P, :]).then_inc(chunk_loaded[s], 16)
            act.wait_ge(x_lo, KC)
            act.wait_ge(blocks_multiplied, B_WO + 4)
            for s in range(SC):
                nc.scalar.activation(x2[:, s, 0:HALF], ps[:, s, :], ACT.Copy).then_inc(o_out, 1)
            for s in range(SC):
                act.wait_ge(o_out, s + 1)
                if s >= 1:
                    act.wait_ge(o_sq, s)
                nc.scalar.activation(tmp[:, 0:HALF], x2[:, s, 0:HALF], ACT.Square, accum_out=ss[:, s:s + 1])\
                    .then_inc(o_sq, 1)
            for s in range(SC):
                if s < SC - 1:
                    act.wait_ge(o_done, s + 1)
                else:
                    act.wait_ge(blocks_multiplied, B_WO + 8)
                if s >= 1:
                    act.wait_ge(o_sq2, s)
                nc.scalar.activation(tmp[:, HALF:2 * HALF], ps[:, s, :], ACT.Square, accum_out=ss2[:, s:s + 1])\
                    .then_inc(o_sq2, 1)
            for s in range(2, SC):
                act.dma_start(x_rows(s), x_d[s * P:(s + 1) * P, :]).then_inc(chunk_loaded[s], 16)
            act.wait_ge(o_ms, 1)
            nc.scalar.activation(rms[:], ms[:], ACT.Sqrt).then_inc(o_rms, 1)
            for g in range(2):
                for s in range(4 * g, 4 * g + 4):
                    act.wait_ge(o_x2, s + 1)
                    if s >= 1:
                        act.wait_ge(p_sq, s)
                    nc.scalar.activation(sg[:], x2[:, s, :], ACT.Square, accum_out=ss[:, s:s + 1]).then_inc(p_sq, 1)
                    if g == 1 and s < 6:
                        for t in range(4 * (s - 4), 4 * (s - 3)):
                            turned_hi_act(act, t, XH, p_tr, p_hi, FREE_T)
                act.wait_ge(p_ms, g + 1)
                at = slice(4 * g, 4 * g + 4)
                nc.scalar.activation(rms[:, at], ms[:, at], ACT.Sqrt).then_inc(p_rms, 1)
            for t in range(8, 2 * SC):
                turned_hi_act(act, t, XH, p_tr, p_hi, FREE_T)

        def out_dve(dve):
            dve.wait_ge(o_gain, 32)
            for s in range(SC):
                dve.wait_ge(o_sq, s + 1)
                nc.vector.tensor_tensor(x2[:, s, 0:HALF], x2[:, s, 0:HALF], mt[:, 0, 0:HALF], ALU.mult)\
                    .then_inc(o_scaled, 1)
            for s in range(SC):
                dve.wait_ge(o_sq2, s + 1)
                nc.vector.tensor_tensor(x2[:, s, HALF:2 * HALF], ps[:, s, :], mt[:, 0, HALF:2 * HALF], ALU.mult)\
                    .then_inc(o_scaled, 1)
            nc.vector.tensor_tensor(ms[:], ss[:], ss2[:], ALU.add).then_inc(o_ss, 1)
            dve.wait_ge(o_ss, 1)
            nc.vector.tensor_scalar(ms[:], ms[:], 1.0 / D, EPS, ALU.mult, ALU.add).then_inc(o_ms, 1)
            dve.wait_ge(o_rms, 1)
            nc.vector.reciprocal(rstd[:], rms[:]).then_inc(o_rstd, 1)
            dve.wait_ge(o_rstd, 1)
            dve.wait_ge(o_scaled, 2 * SC)

            def residual(s):
                dve.wait_ge(chunk_loaded[s], 48)
                nc.vector.scalar_tensor_tensor(out=x2[:, s, :], in0=x2[:, s, :], scalar=rstd[:, s:s + 1],
                                               in1=x_rows(s), op0=ALU.mult, op1=ALU.add).then_inc(o_x2, 1)

            def rows_rstd(g):
                at = slice(4 * g, 4 * g + 4)
                dve.wait_ge(p_sq, 4 * g + 4)
                nc.vector.tensor_scalar(ms[:, at], ss[:, at], 1.0 / D, EPS, ALU.mult, ALU.add).then_inc(p_ms, 1)
                dve.wait_ge(p_rms, g + 1)
                nc.vector.reciprocal(rstd[:, at], rms[:, at]).then_inc(p_rstd, 1)
                dve.wait_ge(p_rstd, g + 1)

            def normed(s):
                if s >= 2:
                    dve.wait_ge(p_tr, 2 * (s - 1))
                nc.vector.scalar_tensor_tensor(out=xn2[:, s % 2, :], in0=x2[:, s, :], scalar=rstd[:, s:s + 1],
                                               in1=mt[:, 1, :], op0=ALU.mult, op1=ALU.mult).then_inc(p_xn, 1)

            for s in range(6):
                residual(s)
            rows_rstd(0)
            for s in range(4):
                normed(s)
                if s >= 1:
                    norm_lo(dve, s - 1, XH, XL, p_hi, p_lo, FREE_T)
            for s in (6, 7):
                residual(s)
            norm_lo(dve, 3, XH, XL, p_hi, p_lo, FREE_T)
            rows_rstd(1)
            for s in range(4, SC):
                normed(s)
                if s >= 5:
                    norm_lo(dve, s - 1, XH, XL, p_hi, p_lo, FREE_T)
            norm_lo(dve, SC - 1, XH, XL, p_hi, p_lo, FREE_T)

        def turn_normed_pe(pe, s):
            pe.wait_ge(p_xn, s + 1)
            for g in range(2):
                turned_pe(pe, 2 * s + g, xn2, p_tr, p_lo, FREE_T)

        def ffn_start_pe(pe):
            def first_blocks(half, m0, m1):
                for m in range(m0, m1):
                    blk, (k, pas) = m // 24, divmod(m % 24, 3)
                    slot = (B_FFN + blk) % 2
                    w = (wl if pas == 2 else wh)[:, slot, k * P:(k + 1) * P]
                    x = (XL if pas == 1 else XH)[:, k, half * HALF:(half + 1) * HALF]
                    mm = nc.tensor.matmul(ps[:, 2 * blk + half, :], w, x, start=(m % 24 == 0), stop=(m % 24 == 23))
                    if half == 1 and m % 24 == 23:
                        mm.then_inc(blocks_multiplied, 1)

            pe.wait_ge(o_scaled, 2 * SC)
            for s in range(4):
                turn_normed_pe(pe, s)
            pe.wait_ge(block_split, B_FFN + 2)
            pe.wait_ge(p_lo, 8)
            for s in range(4, SC):
                first_blocks(0, 12 * (s - 4), 12 * (s - 3))
                turn_normed_pe(pe, s)
            pe.wait_ge(p_lo, 2 * SC)
            first_blocks(1, 0, 48)

        f_silu, f_mul, f_hi, f_lo = sem("f_silu"), sem("f_mul"), sem("f_hi"), sem("f_lo")
        f_down, f_add = sem("f_down"), sem("f_add")
        f_gain = sem("f_gain_loaded")
        e_sq, e_ms, e_rms, e_rstd = sem("e_sq"), sem("e_ms"), sem("e_rms"), sem("e_rstd")
        e_nrm, e_y, out_stored = sem("e_normed"), [sem("e_y_first"), sem("e_y_last")], sem("out_stored")
        DOWN = 2 * SC

        def ffn_gate_up_pe(pe, c, b, slot):
            pe.wait_ge(f_silu, c)
            t_job(pe, slot, b + 1, XH, XL, 0)
            pe.wait_ge(f_mul, c)
            t_job(pe, 1 - slot, b + 2, XH, XL, 2)

        def ffn_down_pe(pe, c, odd, b, slot, first=False):
            pe.wait_ge(block_split, b + 1)
            pe.wait_ge(f_lo, c + 1)
            for t in range(DOWN):
                s, nh = divmod(t, 2)
                if not (first and t < 4):
                    pe.wait_ge(f_add, c * DOWN + (t - 3))
                at = slice(nh * HALF, (nh + 1) * HALF)
                mm = matmul3(ps[:, 4 + t % 4, :], FH[:, odd, s * P:(s + 1) * P], FL[:, odd, s * P:(s + 1) * P],
                             wh[:, slot, at], wl[:, slot, at], True, True)
                mm.then_inc(f_down if t < DOWN - 1 else blocks_multiplied, 1)

        def ffn_pe(pe):
            out_pe(pe)
            ffn_start_pe(pe)
            b = B_FFN
            ffn_gate_up_pe(pe, 1, b + 2, b % 2)
            ffn_down_pe(pe, 0, 0, b + 4, b % 2, True)
            with pe.Fori(0, FF // 2 - 1) as i:
                for j in range(2):
                    c = i * 2 + (2 + j)
                    bj = i * 6 + (b + 5 + 3 * j)
                    slot = (b + 5 + 3 * j) % 2
                    ffn_gate_up_pe(pe, c, bj, slot)
                    ffn_down_pe(pe, i * 2 + (1 + j), 1 - j, bj + 2, slot)
            ffn_down_pe(pe, FF - 1, (FF - 1) % 2, N_BLOCKS - 1, (N_BLOCKS - 1) % 2)

        def ffn_chunk_act(act, c, odd, gate_block):
            act.wait_ge(blocks_multiplied, gate_block + 1)
            nc.scalar.activation(sg[:], two_banks(0), ACT.Silu).then_inc(f_silu, 1)
            act.wait_ge(f_mul, c + 1)
            nc.scalar.activation(FH[:, odd, :], ff[:], ACT.Copy).then_inc(f_hi, 1)

        def ffn_act(act):
            act.dma_start(gc[:], norm_d[3]).then_inc(f_gain, 16)
            ffn_chunk_act(act, 0, 0, B_FFN)
            ffn_chunk_act(act, 1, 1, B_FFN + 2)
            with act.Fori(0, FF // 2 - 1) as i:
                for j in range(2):
                    ffn_chunk_act(act, i * 2 + (2 + j), j, i * 6 + (B_FFN + 5 + 3 * j))
            for g in range(2):
                for s in range(4 * g, 4 * g + 4):
                    act.wait_ge(f_add, (FF - 1) * DOWN + 2 * s + 2)
                    square_act(act, acc, s, xn2[:, 0, :], e_sq)
                group_rms_act(act, g, 4, e_ms, e_rms)
            for s in range(SC):
                act.wait_ge(e_y[s // 4], 1 + s % 4)
                act.dma_start(out_d[s * P:(s + 1) * P, :], acc[:, s, :]).then_inc(out_stored, 16)
            act.wait_ge(out_stored, SC * 16)

        def ffn_mul_dve(dve, c, gate_block, later=True):
            dve.wait_ge(f_silu, c + 1)
            dve.wait_ge(blocks_multiplied, gate_block + 2)
            if later:
                dve.wait_ge(f_lo, c)
            nc.vector.tensor_tensor(ff[:], two_banks(2), sg[:], ALU.mult).then_inc(f_mul, 1)

        def ffn_lo_dve(dve, c, odd):
            dve.wait_ge(f_hi, c + 1)
            nc.vector.tensor_tensor(FL[:, odd, :], ff[:], FH[:, odd, :].bitcast(F32), ALU.subtract).then_inc(f_lo, 1)

        def ffn_add_dve(dve, c, down_block, t, first=False):
            s, nh = divmod(t, 2)
            if t < DOWN - 1:
                dve.wait_ge(f_down, c * (DOWN - 1) + (t + 1))
            else:
                dve.wait_ge(blocks_multiplied, down_block + 1)
            tile_ = acc[:, s, nh * HALF:(nh + 1) * HALF]
            if first:
                nc.vector.tensor_copy(tile_, ps[:, 4 + t % 4, :]).then_inc(f_add, 1)
            else:
                dve.wait_ge(f_add, c * DOWN + (t + 1 - DOWN))
                nc.vector.tensor_tensor(tile_, tile_, ps[:, 4 + t % 4, :], ALU.add).then_inc(f_add, 1)

        def ffn_dve(dve):
            ffn_mul_dve(dve, 0, B_FFN, False)
            ffn_lo_dve(dve, 0, 0)
            ffn_mul_dve(dve, 1, B_FFN + 2)
            ffn_lo_dve(dve, 1, 1)
            for t in range(DOWN):
                ffn_add_dve(dve, 0, B_FFN + 4, t, True)
            with dve.Fori(0, FF // 2 - 1) as i:
                for j in range(2):
                    gate_block = i * 6 + (B_FFN + 5 + 3 * j)
                    ffn_mul_dve(dve, i * 2 + (2 + j), gate_block)
                    for t in range(DOWN):
                        ffn_add_dve(dve, i * 2 + (1 + j), gate_block + 2, t)
                        if t == 2:
                            ffn_lo_dve(dve, i * 2 + (2 + j), j)
            def last_normed(s):
                nc.vector.scalar_tensor_tensor(out=acc[:, s, :], in0=acc[:, s, :], scalar=rstd[:, s:s + 1],
                                               in1=gc[:], op0=ALU.mult, op1=ALU.mult).then_inc(e_nrm, 1)

            dve.wait_ge(f_gain, 16)
            for t in range(DOWN):
                ffn_add_dve(dve, FF - 1, N_BLOCKS - 1, t)
                if t == 10:
                    group_ms_dve(dve, 0, 4, e_sq, e_ms)
                if t == 12:
                    group_rstd_dve(dve, 0, 4, e_rms, e_rstd)
                if t in (12, 14):
                    last_normed(t // 2 - 6)
            last_normed(2)
            last_normed(3)
            group_ms_dve(dve, 1, 4, e_sq, e_ms)
            group_rstd_dve(dve, 1, 4, e_rms, e_rstd)
            for s in range(4, SC):
                last_normed(s)
            dve.wait_ge(e_nrm, SC)
            for s in range(4, SC):
                nc.vector.tensor_tensor(acc[:, s, :], acc[:, s, :], x2[:, s, :], ALU.add).then_inc(e_y[1], 1)

        def ffn_pool(pool):
            for s in range(4):
                pool.wait_ge(e_nrm, s + 1)
                nc.gpsimd.tensor_tensor(acc[:, s, :], acc[:, s, :], x2[:, s, :], ALU.add).then_inc(e_y[0], 1)

        @block.sync
        def _(sp):
            for s in range(SC):
                sp.dma_start(xs[:, s, :], x_d[s * P:(s + 1) * P, :]).then_inc(chunk_loaded[s], 16)
                if s in (3, 4):
                    sp.dma_start(wraw[:, s - 3, :], wst_d[s - 3]).then_inc(block_loaded[s - 3], 16)
            def load_blocks(first, last):
                with sp.Fori(0, (last - first) // 2) as i:
                    for j in range(2):
                        sp.wait_ge(block_split, i * 2 + (first - 1 + j))
                        sp.dma_start(wraw[:, j, :], wst_d[bass.ds(i * 2 + (first + j), 1)].rearrange("a p n -> p (a n)"))\
                            .then_inc(block_loaded[j], 16)

            load_blocks(2, B_PAIR + 3)
            att_sp(sp)
            load_ret_sp(sp)
            load_blocks(B_WB + 3, N_BLOCKS - 1)
            sp.wait_ge(block_split, N_BLOCKS - 2)
            sp.dma_start(wraw[:, 0, :], wst_d[N_BLOCKS - 1]).then_inc(block_loaded[0], 16)

        @block.gpsimd
        def _(pool):
            nc.gpsimd.memset(zero[:], 0.0).then_inc(zero_set, 1)
            pool.wait_ge(zero_set, 1)

            def split(slot, b, loads, reused=True):
                pool.wait_ge(block_loaded[slot], loads * 16)
                if reused:
                    pool.wait_ge(blocks_multiplied, b - 1)
                nc.gpsimd.tensor_tensor(wh[:, slot, :], wraw[:, slot, :], zero[:].to_broadcast([P, 1024]),
                                        ALU.add).then_inc(block_hi, 1)
                pool.wait_ge(block_hi, b + 1)
                nc.gpsimd.tensor_tensor(wl[:, slot, :], wraw[:, slot, :], wh[:, slot, :].bitcast(F32),
                                        ALU.subtract).then_inc(block_split, 1)

            split(0, 0, 1, False)
            split(1, 1, 1, False)
            with pool.Fori(0, (B_PAIR - 1) // 2) as i:
                for j in range(2):
                    split(j, i * 2 + (2 + j), i + 2)
            att_pool(pool, split)
            first = B_WB + 1
            with pool.Fori(0, (N_BLOCKS - 1 - first) // 2) as i:
                for j in range(2):
                    split(j, i * 2 + (first + j), i + (first // 2 + 1))
            split(0, N_BLOCKS - 1, N_BLOCKS // 2 + 1)
            ffn_pool(pool)

        @block.tensor
        def _(pe):
            s1_pe(pe)
            ret_pe(pe)
            att_pe(pe)
            merge_pe(pe)
            ffn_pe(pe)

        @block.scalar
        def _(act):
            act.dma_start(ident[:], norm_d[4, :, 0:P]).then_inc(consts_loaded, 16)
            act.dma_start(g0[:], norm_d[0]).then_inc(consts_loaded, 16)
            s1_act(act)
            ret_act(act)
            att_act(act)
            merge_act(act)
            ffn_act(act)

        @block.vector
        def _(dve):
            s1_dve(dve)
            ret_dve(dve)
            att_dve(dve)
            merge_dve(dve)
            ffn_dve(dve)


def kernel(**inputs):
    import numpy as np
    import concourse.bacc as bacc
    from concourse.bass_utils import run_bass_kernel_spmd

    a = {k: np.asarray(v) for k, v in inputs.items()}
    w_in = a["w_in"][0]
    widths = (1024, 768, 48, 512, 512, 1024, 1024, 2048)
    ends = np.cumsum(widths)
    wq, wkv, wg, wqr, wkr, wvr, wgr, wm = (w_in[:, e - w:e] for e, w in zip(ends, widths))

    def t_blocks(w):
        return list(w.reshape(KC, P, -1, P).transpose(2, 1, 0, 3).reshape(-1, P, 1024))

    def row_blocks(w, n):
        per = 1024 // n
        return list(w.reshape(KC // per, per, P, n).transpose(0, 2, 1, 3).reshape(-1, P, 1024))

    q, kv = t_blocks(wq), t_blocks(wkv)
    qr, kr, gr, m = t_blocks(wqr), t_blocks(wkr), t_blocks(wgr), t_blocks(wm)
    order = [0, 4, 1, 5, 2, 6, 3, 7]
    gate_w = wg.reshape(D, PAIRS, 2, 3)[:, order].reshape(D, 48)
    vsg = np.zeros((D, HALF), np.float32)
    vsg[:, 0:P], vsg[:, P:2 * P], vsg[:, 2 * P:2 * P + 48] = wkv[:, 3 * P:4 * P], wkv[:, 5 * P:6 * P], gate_w
    blocks = []
    for h in range(RH):
        blocks += row_blocks(wvr[:, h * DV:(h + 1) * DV], DV) + [kr[h], qr[h], gr[2 * h], gr[2 * h + 1]]
    blocks += [kv[0], kv[1], kv[2], kv[4]] + [q[0]] + row_blocks(vsg, HALF)
    for n in range(PAIRS):
        blocks += [q[order[min(n + 1, PAIRS - 1)]], m[KC + n], m[n]]
    blocks += t_blocks(a["w_branch_b"][0])
    blocks += t_blocks(a["w_branch_a"][0].reshape(PAIRS, P, D)[order].reshape(D, D))
    wo = a["w_out"][0]
    blocks += row_blocks(wo[:, :HALF], HALF) + row_blocks(wo[:, HALF:], HALF)
    gate, up, down = t_blocks(a["w_ffn_gate"][0]), t_blocks(a["w_ffn_up"][0]), a["w_ffn_down"][0].reshape(FF, P, D)
    for c in range(FF):
        blocks += [gate[c], up[c]] + ([down[c - 1]] if c else [])
    blocks.append(down[FF - 1])
    assert len(blocks) == N_BLOCKS

    norm = np.zeros((5, P, D), np.float32)
    for i, name in enumerate(("g_pre_mix", "g_post_mix", "g_pre_ffn", "g_post_ffn")):
        norm[i] = np.broadcast_to(a[name][0], (P, D))
    norm[4, :, :P] = np.eye(P)

    def rope(d):
        half = d // 2
        inv = np.float32(10000.0) ** (-np.arange(half, dtype=np.float32) * np.float32(2.0) / np.float32(d))
        ang = (inv[:, None] * np.arange(S, dtype=np.float32)[None, :]).astype(np.float32).astype(np.float64)
        cos, sin = np.cos(ang), np.sin(ang)
        t = np.stack([np.concatenate([cos, cos]), np.concatenate([-sin, sin])])
        return np.ascontiguousarray(np.tile(t, (1, P // d, 1)).astype(np.float32))

    log_g = np.log1p(-np.exp2(-5.0 - np.arange(RH)))
    i = np.arange(P)
    ret = np.zeros((RH, P, P + 4), np.float32)
    diff = i[None, :] - i[:, None]
    for h in range(RH):
        ret[h, :, :P] = np.where(diff >= 0, np.exp(log_g[h] * np.maximum(diff, 0)), 0.0)
        ret[h, :, P] = np.exp(log_g[h] * (P - 1.0 - i))
        ret[h, :, P + 1] = np.exp(log_g[h] * (i + 1.0))
        ret[h, :, P + 2] = np.exp(log_g[h] * P)
    neg = np.float32(-2.0 ** 99)
    t = np.arange(S).reshape(SC, P).T
    cmp_end = np.arange(NCMP) * 16 + 31
    mask = np.zeros((P, 2 * P + SC * NCMP + 1), np.float32)
    mask[:, 0:P] = np.where(i[None, :] > i[:, None], neg, 0)
    mask[:, P:2 * P] = np.where(i[None, :] <= i[:, None], neg, 0)
    seen = (cmp_end[None, None, :] <= t[:, :, None]) & (np.arange(NCMP) < NCMP - 1)
    mask[:, 2 * P:-1] = np.where(seen, 0, neg).reshape(P, -1)
    mask[:, -1] = i >= 31

    arrays = {
        "x": a["x"][0],
        "weights": np.stack(blocks),
        "norm": norm,
        "rope_a": rope(DH),
        "rope_r": rope(128),
        "ret": ret,
        "mask": mask,
        "w1": np.stack([a[f"cmp_w1_{c}"][0].reshape(16, P, P).transpose(1, 0, 2) for c in "kv"], 1),
        "pos": np.stack([a[f"cmp_pos_{c}"][0].reshape(16, P).T for c in "kv"], 1),
        "w2k": np.concatenate([a["cmp_w2_k"][0]] * 2, 1),
        "w2v": a["cmp_w2_v"][0],
    }
    nc = bacc.Bacc("TRN2", target_bir_lowering=False, num_devices=1)
    args = []
    for name in arrays:
        arrays[name] = np.ascontiguousarray(arrays[name])
        args.append(nc.dram_tensor(name, arrays[name].shape, F32, kind="ExternalInput").ap())
    args.append(nc.dram_tensor("out", (S, D), F32, kind="ExternalOutput").ap())
    layer(nc, *args)
    r = run_bass_kernel_spmd(nc, [arrays], core_ids=[0])
    return r.results[0]["out"].reshape(1, S, D)
```
